# Optimizing a Trainium2 kernel written in Bass

```python
import math
import jax, jax.numpy as jnp
from jax import lax
import numpy as np

D_MODEL = 1024
BATCH = 1
SEQ = 512
DEPTH = 2

MEM_LEN = 256
RMS_EPS = 1e-6
POOL_GROUPS = 4
POOL_GROUP_W = D_MODEL // 16
POOL_W = POOL_GROUPS * POOL_GROUP_W
POOL_WINDOWS = (2, 4, 8, 16)
MOBA_HEADS = 4
MOBA_HD = D_MODEL // 16
MOBA_W = MOBA_HEADS * MOBA_HD
MOBA_BLOCK = 256
MOBA_TOPK = 3
MOBA_Q_CHUNK = 16
ROPE_THETA = 500000.0
ROPE_DIMS = MOBA_HD // 4
DN_HEADS = 8
DN_HD = D_MODEL // 16
DN_W = DN_HEADS * DN_HD
DN_CONV = 4
DN_CHUNK = 64
N_BRANCH = 3
OFF_POOL = 0
OFF_MOBA = OFF_POOL + POOL_W
OFF_DN_QKV = OFF_MOBA + 3 * MOBA_W
OFF_DN_BETA = OFF_DN_QKV + 3 * DN_W
OFF_DN_ALPHA = OFF_DN_BETA + DN_HEADS
OFF_DN_Z = OFF_DN_ALPHA + DN_HEADS
OFF_GATE = OFF_DN_Z + DN_W
IN_COLS = OFF_GATE + N_BRANCH * D_MODEL
XA_HEADS = 4
XA_HD = D_MODEL // 8
XA_W = XA_HEADS * XA_HD
DENSE_FF = 2816
N_EXPERTS = 8
MOE_TOPK = 2
EXPERT_FF = DENSE_FF // 2
N_DENSE = (DEPTH + 1) // 2
N_MOE = DEPTH // 2

kernel_name = "hybrid_pool_moba_gdn_moe_block"

def rmsnorm(x, g):
    x32 = x.astype(jnp.float32)
    y = x32 * lax.rsqrt(jnp.mean(x32 * x32, axis=-1, keepdims=True) + RMS_EPS)
    return (y * g.astype(jnp.float32)).astype(x.dtype)

def l2norm(x):
    x32 = x.astype(jnp.float32)
    return x32 * lax.rsqrt(jnp.sum(x32 * x32, axis=-1, keepdims=True) + RMS_EPS)

def partial_rope(x, positions):
    half = ROPE_DIMS // 2
    inv_freq = jnp.power(ROPE_THETA, -jnp.arange(half, dtype=jnp.float32) * 2.0 / ROPE_DIMS)
    ang = positions.astype(jnp.float32)[:, :, None] * inv_freq
    cos = jnp.cos(ang)[:, :, None, :].astype(x.dtype)
    sin = jnp.sin(ang)[:, :, None, :].astype(x.dtype)
    x1 = x[..., :half]
    x2 = x[..., half:ROPE_DIMS]
    return jnp.concatenate([x1 * cos - x2 * sin, x2 * cos + x1 * sin, x[..., ROPE_DIMS:]], axis=-1)

def pool_mixer(p, pool_w, pool_scale):
    B, S, _ = p.shape
    pg = p.reshape(B, S, POOL_GROUPS, POOL_GROUP_W).astype(jnp.float32)
    cs = jnp.cumsum(pg, axis=1)
    t1 = jnp.arange(1, S + 1, dtype=jnp.float32)
    outs = []
    for gi, w in enumerate(POOL_WINDOWS):
        c = cs[:, :, gi]
        lagged = jnp.pad(c, ((0, 0), (w, 0), (0, 0)))[:, :S]
        count = jnp.minimum(t1, float(w))[None, :, None]
        outs.append((c - lagged) / count - pg[:, :, gi])
    pooled = jnp.stack(outs, axis=2).astype(p.dtype)
    mixed = jnp.einsum('bsgc,gcd->bsgd', pooled, pool_w)
    return mixed.reshape(B, S, POOL_W) * pool_scale

def moba_attention(q, k, v):
    B, S, H, hd = q.shape
    nb = -(-S // MOBA_BLOCK)
    s_pad = nb * MOBA_BLOCK
    topk = min(MOBA_TOPK, nb)
    pad = ((0, 0), (0, 0), (0, s_pad - S), (0, 0))
    qh = jnp.pad(q.transpose(0, 2, 1, 3), pad)
    kb = jnp.pad(k.transpose(0, 2, 1, 3), pad).reshape(B, H, nb, MOBA_BLOCK, hd)
    vb = jnp.pad(v.transpose(0, 2, 1, 3), pad).reshape(B, H, nb, MOBA_BLOCK, hd)
    kbar = jnp.mean(kb.astype(jnp.float32), axis=3)
    scale = hd ** -0.5
    bi = jnp.arange(B)[:, None, None, None]
    hi = jnp.arange(H)[None, :, None, None]
    blk_ids = jnp.arange(nb)

    def chunk(ci):
        start = ci * MOBA_Q_CHUNK
        c = start // MOBA_BLOCK
        qc = lax.dynamic_slice_in_dim(qh, start, MOBA_Q_CHUNK, axis=2)
        gate = jnp.einsum('bhqd,bhnd->bhqn', qc.astype(jnp.float32), kbar)
        gate = jnp.where(blk_ids < c, gate, -jnp.inf)
        _, idx = lax.top_k(gate, topk)
        valid = idx < c
        kg = kb[bi, hi, idx]
        vg = vb[bi, hi, idx]
        s_sel = jnp.einsum('bhqd,bhqknd->bhqkn', qc, kg).astype(jnp.float32) * scale
        s_sel = jnp.where(valid[..., None], s_sel, -jnp.inf)
        s_sel = s_sel.reshape(B, H, MOBA_Q_CHUNK, topk * MOBA_BLOCK)
        k_own = lax.dynamic_index_in_dim(kb, c, axis=2, keepdims=False)
        v_own = lax.dynamic_index_in_dim(vb, c, axis=2, keepdims=False)
        s_own = jnp.einsum('bhqd,bhnd->bhqn', qc, k_own).astype(jnp.float32) * scale
        qpos = start + jnp.arange(MOBA_Q_CHUNK)
        kpos = c * MOBA_BLOCK + jnp.arange(MOBA_BLOCK)
        s_own = jnp.where(kpos[None, :] <= qpos[:, None], s_own, -jnp.inf)
        p = jax.nn.softmax(jnp.concatenate([s_sel, s_own], axis=-1), axis=-1).astype(q.dtype)
        p_sel = p[..., :topk * MOBA_BLOCK].reshape(B, H, MOBA_Q_CHUNK, topk, MOBA_BLOCK)
        p_own = p[..., topk * MOBA_BLOCK:]
        return (jnp.einsum('bhqkn,bhqknd->bhqd', p_sel, vg)
                + jnp.einsum('bhqn,bhnd->bhqd', p_own, v_own))

    out = lax.map(chunk, jnp.arange(s_pad // MOBA_Q_CHUNK))
    out = out.transpose(1, 0, 3, 2, 4).reshape(B, s_pad, H, hd)[:, :S]
    return out.reshape(B, S, H * hd)

def short_conv(x, w):
    S = x.shape[1]
    K = w.shape[0]
    xp = jnp.pad(x, ((0, 0), (K - 1, 0), (0, 0)))
    y = w[0] * xp[:, :S]
    for j in range(1, K):
        y = y + w[j] * xp[:, j:j + S]
    return y

def gated_delta_rule(q, k, v, g, beta):
    B, H, S, dk = q.shape
    dv = v.shape[-1]
    C = DN_CHUNK
    nc = S // C

    def chunks(t):
        return t.reshape(t.shape[:2] + (nc, C) + t.shape[3:])

    q, k, v, g, beta = chunks(q), chunks(k), chunks(v), chunks(g), chunks(beta)
    G = jnp.cumsum(g, axis=-1)
    tril = jnp.tril(jnp.ones((C, C), dtype=bool))
    strict = jnp.tril(jnp.ones((C, C), dtype=bool), -1)
    decay = jnp.exp(jnp.where(tril, G[..., :, None] - G[..., None, :], -jnp.inf))
    kbeta = k * beta[..., None]
    a = jnp.where(strict, jnp.einsum('bhnid,bhnjd->bhnij', kbeta, k) * decay, 0.0)
    lhs = a + jnp.eye(C, dtype=jnp.float32)
    rhs = jnp.concatenate([v * beta[..., None], kbeta * jnp.exp(G)[..., None]], axis=-1)
    sol = lax.linalg.triangular_solve(lhs, rhs, left_side=True, lower=True, unit_diagonal=True)
    u = sol[..., :dv]
    w = sol[..., dv:]
    aqk = jnp.einsum('bhnid,bhnjd->bhnij', q, k) * decay
    q_dec = q * jnp.exp(G)[..., None]
    g_last = G[..., -1]
    k_dec = k * jnp.exp(g_last[..., None] - G)[..., None]

    def step(state, xs):
        u_c, w_c, qd_c, aqk_c, kd_c, gl_c = xs
        v_new = u_c - jnp.einsum('bhcd,bhde->bhce', w_c, state)
        o_c = (jnp.einsum('bhcd,bhde->bhce', qd_c, state)
               + jnp.einsum('bhij,bhje->bhie', aqk_c, v_new))
        state = state * jnp.exp(gl_c)[..., None, None] + jnp.einsum('bhcd,bhce->bhde', kd_c, v_new)
        return state, o_c

    xs = (jnp.moveaxis(u, 2, 0), jnp.moveaxis(w, 2, 0), jnp.moveaxis(q_dec, 2, 0),
          jnp.moveaxis(aqk, 2, 0), jnp.moveaxis(k_dec, 2, 0), jnp.moveaxis(g_last, 2, 0))
    _, o = lax.scan(step, jnp.zeros((B, H, dk, dv), jnp.float32), xs)
    return jnp.moveaxis(o, 0, 2).reshape(B, H, S, dv)

def deltanet_mixer(qkv, b_raw, a_raw, z, conv_w, a_log, dt_bias, norm_g):
    B, S, _ = qkv.shape
    qkv = jax.nn.silu(short_conv(qkv, conv_w))
    qkv = qkv.reshape(B, S, 3, DN_HEADS, DN_HD).transpose(2, 0, 3, 1, 4)
    q = l2norm(qkv[0]) * (DN_HD ** -0.5)
    k = l2norm(qkv[1])
    v = qkv[2].astype(jnp.float32)
    beta = jax.nn.sigmoid(b_raw.astype(jnp.float32)).transpose(0, 2, 1)
    g = -jnp.exp(a_log.astype(jnp.float32)) * jax.nn.softplus(
        a_raw.astype(jnp.float32) + dt_bias.astype(jnp.float32))
    g = g.transpose(0, 2, 1)
    o = gated_delta_rule(q, k, v, g, beta).transpose(0, 2, 1, 3)
    o = o * lax.rsqrt(jnp.mean(o * o, axis=-1, keepdims=True) + RMS_EPS) * norm_g.astype(jnp.float32)
    o = o * jax.nn.silu(z.astype(jnp.float32).reshape(B, S, DN_HEADS, DN_HD))
    return o.reshape(B, S, DN_W).astype(z.dtype)

def memory_cross_attention(h, mem_n, wq, wkv, wo):
    B, S, _ = h.shape
    M = mem_n.shape[1]
    q = (h @ wq).reshape(B, S, XA_HEADS, XA_HD)
    kv = (mem_n @ wkv).reshape(B, M, 2, XA_HEADS, XA_HD)
    s = jnp.einsum('bshd,bmhd->bhsm', q, kv[:, :, 0]).astype(jnp.float32) * (XA_HD ** -0.5)
    p = jax.nn.softmax(s, axis=-1).astype(h.dtype)
    o = jnp.einsum('bhsm,bmhd->bshd', p, kv[:, :, 1]).reshape(B, S, XA_W)
    return o @ wo

def swiglu(h, w_gate_up, w_down):
    gate, up = jnp.split(h @ w_gate_up, 2, axis=-1)
    return (jax.nn.silu(gate) * up) @ w_down

def moe_ffn(h, router, w_gate_up, w_down):
    B, S, D = h.shape
    hf = h.reshape(B * S, D)
    logits = (hf @ router).astype(jnp.float32)
    top_logit, top_idx = lax.top_k(logits, MOE_TOPK)
    top_w = jax.nn.softmax(top_logit, axis=-1)
    combine = jnp.sum(jax.nn.one_hot(top_idx, N_EXPERTS, dtype=jnp.float32) * top_w[..., None], axis=1)
    combine = combine.astype(h.dtype)
    y = jnp.zeros_like(hf)
    for e in range(N_EXPERTS):
        y = y + combine[:, e:e + 1] * swiglu(hf, w_gate_up[e], w_down[e])
    return y.reshape(B, S, D)

def setup_inputs(seed: int = 0) -> dict:
    f32 = jnp.float32
    ks = iter(jax.random.split(jax.random.key(seed), 40))

    def nrm(shape, scale):
        return jax.random.normal(next(ks), shape, f32) * scale

    def gain(shape):
        return 1.0 + nrm(shape, 0.02)

    x = nrm((BATCH, SEQ, D_MODEL), 1.0)
    mem = nrm((BATCH, MEM_LEN, D_MODEL), 1.0)
    positions = jnp.broadcast_to(jnp.arange(SEQ, dtype=jnp.int32)[None, :], (BATCH, SEQ))
    mix_norm_g = gain((DEPTH, D_MODEL))
    w_in = nrm((DEPTH, D_MODEL, IN_COLS), D_MODEL ** -0.5)
    pool_w = nrm((DEPTH, POOL_GROUPS, POOL_GROUP_W, POOL_GROUP_W), POOL_GROUP_W ** -0.5)
    pool_scale = 1.0 + nrm((DEPTH, POOL_W), 0.1)
    dn_conv_w = nrm((DEPTH, DN_CONV, 3 * DN_W), DN_CONV ** -0.5)
    dn_a_log = jnp.log(jax.random.uniform(next(ks), (DEPTH, DN_HEADS), f32, 1.0, 16.0))
    dt = jnp.exp(jax.random.uniform(next(ks), (DEPTH, DN_HEADS), f32, math.log(1e-3), math.log(1e-1)))
    dn_dt_bias = dt + jnp.log(-jnp.expm1(-dt))
    dn_norm_g = gain((DEPTH, DN_HD))
    w_up_pool = nrm((DEPTH, POOL_W, D_MODEL), POOL_W ** -0.5)
    w_up_moba = nrm((DEPTH, MOBA_W, D_MODEL), MOBA_W ** -0.5)
    w_up_dn = nrm((DEPTH, DN_W, D_MODEL), DN_W ** -0.5)
    w_out = nrm((DEPTH, D_MODEL, D_MODEL), D_MODEL ** -0.5)
    xa_norm_g = gain((DEPTH, D_MODEL))
    mem_norm_g = gain((DEPTH, D_MODEL))
    xa_wq = nrm((DEPTH, D_MODEL, XA_W), D_MODEL ** -0.5)
    xa_wkv = nrm((DEPTH, D_MODEL, 2 * XA_W), D_MODEL ** -0.5)
    xa_wo = nrm((DEPTH, XA_W, D_MODEL), XA_W ** -0.5)
    ffn_norm_g = gain((DEPTH, D_MODEL))
    dense_w_gate_up = nrm((N_DENSE, D_MODEL, 2 * DENSE_FF), D_MODEL ** -0.5)
    dense_w_down = nrm((N_DENSE, DENSE_FF, D_MODEL), DENSE_FF ** -0.5)
    moe_router = nrm((N_MOE, D_MODEL, N_EXPERTS), D_MODEL ** -0.5)
    moe_w_gate_up = nrm((N_MOE, N_EXPERTS, D_MODEL, 2 * EXPERT_FF), D_MODEL ** -0.5)
    moe_w_down = nrm((N_MOE, N_EXPERTS, EXPERT_FF, D_MODEL), EXPERT_FF ** -0.5)
    final_norm_g = gain((D_MODEL,))
    return {"x": x, "mem": mem, "positions": positions, "mix_norm_g": mix_norm_g, "w_in": w_in,
            "pool_w": pool_w, "pool_scale": pool_scale, "dn_conv_w": dn_conv_w, "dn_a_log": dn_a_log,
            "dn_dt_bias": dn_dt_bias, "dn_norm_g": dn_norm_g, "w_up_pool": w_up_pool,
            "w_up_moba": w_up_moba, "w_up_dn": w_up_dn, "w_out": w_out, "xa_norm_g": xa_norm_g,
            "mem_norm_g": mem_norm_g, "xa_wq": xa_wq, "xa_wkv": xa_wkv, "xa_wo": xa_wo,
            "ffn_norm_g": ffn_norm_g, "dense_w_gate_up": dense_w_gate_up, "dense_w_down": dense_w_down,
            "moe_router": moe_router, "moe_w_gate_up": moe_w_gate_up, "moe_w_down": moe_w_down,
            "final_norm_g": final_norm_g}

def reference(x, mem, positions, mix_norm_g, w_in, pool_w, pool_scale, dn_conv_w, dn_a_log,
              dn_dt_bias, dn_norm_g, w_up_pool, w_up_moba, w_up_dn, w_out, xa_norm_g, mem_norm_g,
              xa_wq, xa_wkv, xa_wo, ffn_norm_g, dense_w_gate_up, dense_w_down, moe_router,
              moe_w_gate_up, moe_w_down, final_norm_g):
    B, S, D = x.shape
    for layer in range(DEPTH):
        h = rmsnorm(x, mix_norm_g[layer])
        proj = h @ w_in[layer]
        p_in = proj[..., OFF_POOL:OFF_MOBA]
        mqkv = proj[..., OFF_MOBA:OFF_DN_QKV].reshape(B, S, 3, MOBA_HEADS, MOBA_HD)
        mq = partial_rope(mqkv[:, :, 0], positions)
        mk = partial_rope(mqkv[:, :, 1], positions)
        mv = mqkv[:, :, 2]
        dn_qkv = proj[..., OFF_DN_QKV:OFF_DN_BETA]
        dn_b = proj[..., OFF_DN_BETA:OFF_DN_ALPHA]
        dn_a = proj[..., OFF_DN_ALPHA:OFF_DN_Z]
        dn_z = proj[..., OFF_DN_Z:OFF_GATE]
        gates = jax.nn.sigmoid(proj[..., OFF_GATE:].astype(jnp.float32)).astype(x.dtype)
        gates = gates.reshape(B, S, N_BRANCH, D)

        y_pool = pool_mixer(p_in, pool_w[layer], pool_scale[layer]) @ w_up_pool[layer]
        y_moba = moba_attention(mq, mk, mv) @ w_up_moba[layer]
        y_dn = deltanet_mixer(dn_qkv, dn_b, dn_a, dn_z, dn_conv_w[layer], dn_a_log[layer],
                              dn_dt_bias[layer], dn_norm_g[layer]) @ w_up_dn[layer]
        merged = gates[:, :, 0] * y_pool + gates[:, :, 1] * y_moba + gates[:, :, 2] * y_dn
        x = x + merged @ w_out[layer]

        x = x + memory_cross_attention(rmsnorm(x, xa_norm_g[layer]), rmsnorm(mem, mem_norm_g[layer]),
                                       xa_wq[layer], xa_wkv[layer], xa_wo[layer])

        h = rmsnorm(x, ffn_norm_g[layer])
        if layer % 2 == 0:
            x = x + swiglu(h, dense_w_gate_up[layer // 2], dense_w_down[layer // 2])
        else:
            x = x + moe_ffn(h, moe_router[layer // 2], moe_w_gate_up[layer // 2], moe_w_down[layer // 2])
    return rmsnorm(x, final_norm_g)


_drawn_inputs = setup_inputs


def setup_inputs(seed=0):
    import zlib

    import numpy as np

    out = dict(_drawn_inputs(seed))
    spreads = {}
    factors = {'xa_norm_g': 7.218, 'mem_norm_g': 8.0, 'final_norm_g': 7.874, 'ffn_norm_g': 4.437}
    for name, (base, spread) in spreads.items():
        noise = np.random.default_rng([zlib.crc32(name.encode()), seed]).standard_normal(out[name].shape)
        drawn = base * np.exp(spread * noise) if base else spread * noise
        out[name] = __import__('jax').numpy.asarray(drawn.astype(out[name].dtype))
    for name, factor in factors.items():
        out[name] = (out[name] * factor).astype(out[name].dtype)
    return out
```

```python
from contextlib import ExitStack

import numpy as np

import concourse.bass as bass
from concourse import mybir

F32 = mybir.dt.float32
F32R = mybir.dt.float32r
I32 = mybir.dt.int32
ALU = mybir.AluOpType
ACT = mybir.ActivationFunctionType
AX = mybir.AxisListType

P = 128
SEQ = 512
D = 1024
DEPTH = 2
MEM = 256
KT = D // P
TT = SEQ // P
RMS_EPS = 1e-6
POOL_WINDOWS = (2, 4, 8, 16)
HD = 64
PAIRS = 4
CH = 64
NC = SEQ // CH
MOBA_PAIRS = 2
XH = 4
FF = 1408
FT = FF // P
NE = 8
DENSE_PARTS = 2
UNIT = KT * P
BIG = FT * P
MIX_UNITS = 2 + 2 + MOBA_PAIRS * 2 + PAIRS * 4 + KT * 4 + KT + 4 + XH * 2 + KT // 2
LEVELS = 6
ROPE_HALF = 8
ROPE_THETA = 500000.0
NEG = -1e30
MAGIC = 12582912.0

V_MIXG, V_XAG, V_MEMG, V_FFNG, V_FING = 0, 8, 16, 24, 32
V_CONV = 40
V_POOLS = 88
V_DNG = 90
V_ALOG = 91
V_DTB = 95
V_DENSE = 99
NV = 100

C_ID, C_ONE, C_BONE, C_ROT, C_UB, C_VB = 0, 128, 256, 384, 512, 640
C_V64, C_U64, C_LOW, C_UPI, C_ID64, C_LV1 = 768, 832, 896, 960, 1024, 1088
C_LVT = 1152
C_CAUS = C_LVT + LEVELS * 64
C_CNT = C_CAUS + SEQ
C_FREQ = C_CNT + 2 * SEQ
C_RANK = C_FREQ + 1
C_EPS = C_RANK + NE
NCST = C_EPS + 1


def constants():
    c = np.zeros((P, NCST), np.float32)
    p = np.arange(P)[:, None]
    j = np.arange(P)[None, :]
    same = (p // HD) == (j // HD)
    c[:, C_ID:C_ID + P] = p == j
    c[:, C_ONE:C_ONE + P] = 1
    c[:, C_BONE:C_BONE + P] = same
    jd = j % HD
    c[:, C_ROT:C_ROT + P] = (1.0 * ((p == j - ROPE_HALF) & (jd >= ROPE_HALF) & (jd < 2 * ROPE_HALF))
                             - 1.0 * ((p == j + ROPE_HALF) & (jd < ROPE_HALF)))
    c[:, C_UB:C_UB + P] = same & (p <= j)
    c[:, C_VB:C_VB + P] = same & (p > j)
    r = p % CH
    k = np.arange(CH)[None, :]
    c[:, C_V64:C_V64 + CH] = r > k
    c[:, C_U64:C_U64 + CH] = r <= k
    c[:, C_LOW:C_LOW + CH] = r > k
    c[:, C_UPI:C_UPI + CH] = k >= r
    c[:, C_ID64:C_ID64 + CH] = r == k
    for l in range(LEVELS):
        s = 1 << l
        low = (r // (2 * s) == k // (2 * s)) & (r % (2 * s) >= s) & (k % (2 * s) < s)
        up = (r // (2 * s) == k // (2 * s)) & (k % (2 * s) >= s) & (r % (2 * s) < s)
        if l == 0:
            c[:, C_LV1:C_LV1 + CH] = low
        c[:, C_LVT + l * CH:C_LVT + (l + 1) * CH] = up
    t = np.arange(SEQ)[None, :]
    c[:, C_CAUS:C_CAUS + SEQ] = np.where(t - (SEQ - P) <= p, 0.0, NEG)
    for b in range(2):
        w = np.where(p < HD, POOL_WINDOWS[2 * b], POOL_WINDOWS[2 * b + 1])
        c[:, C_CNT + b * SEQ:C_CNT + (b + 1) * SEQ] = 1.0 / np.minimum(t + 1, w)
    freq = np.power(np.float32(ROPE_THETA), -np.arange(ROPE_HALF, dtype=np.float32) * np.float32(2.0) / np.float32(16))
    d = np.arange(P) % HD
    c[:, C_FREQ] = np.where(d < 2 * ROPE_HALF, freq[d % ROPE_HALF], 0.0)
    c[:, C_RANK:C_RANK + NE] = NE - np.arange(NE)[None, :]
    c[:, C_EPS] = RMS_EPS
    return c


def program(nc, x_t, mem_t, pos, cst, vec, wsm, wst, wdn, out_t):
    ctx = ExitStack()
    with ctx:
        def sb(name, shape, dt=F32):
            return ctx.enter_context(nc.sbuf_tensor(name, shape, dt))

        def sem(name):
            return ctx.enter_context(nc.semaphore(name))

        X = sb("X", [P, KT, SEQ])
        h_hi = sb("h_hi", [P, KT, SEQ], F32R)
        h_lo = sb("h_lo", [P, KT, SEQ], F32R)
        C = sb("C", [P, NCST])
        vecs = sb("vecs", [P, NV])
        NSM = 2 * P + KT * 16 + KT * NE
        wsmall = sb("wsmall", [P, NSM])
        raw = sb("raw", [P, 2, BIG])
        w_hi = sb("w_hi", [P, 2, BIG], F32R)
        w_lo = sb("w_lo", [P, 2, BIG], F32R)
        ropeC = sb("ropeC", [P, SEQ])
        ropeS = sb("ropeS", [P, SEQ])
        rinv = sb("rinv", [P, SEQ])
        tA = sb("tA", [P, SEQ])
        tB = sb("tB", [P, SEQ])
        tC = sb("tC", [P, SEQ])
        tD = sb("tD", [P, SEQ])
        tE = sb("tE", [P, SEQ])
        B_hi = sb("B_hi", [P, FT, SEQ], F32R)
        B_lo = sb("B_lo", [P, FT, SEQ], F32R)
        AR_COLS = 11500
        with ExitStack() as same:
            def first(name, shape, dt):
                return same.enter_context(nc.sbuf_tensor(name, shape, dt))
            M_hi = first("M_hi", [P, KT, SEQ], F32R)
            M_lo = first("M_lo", [P, KT, SEQ], F32R)
        with ExitStack() as same:
            N_hi = first("N_hi", [P, KT, MEM], F32R)
            N_lo = first("N_lo", [P, KT, MEM], F32R)
        AR = sb("AR", [P, AR_COLS])
        at = [0]

        def arena(*shape):
            n = int(np.prod(shape))
            a = AR[:, at[0]:at[0] + n]
            at[0] += n
            assert at[0] <= AR_COLS, at[0]
            if len(shape) == 2:
                return a.rearrange("p (a b) -> p a b", a=shape[0])
            if len(shape) == 3:
                return a.rearrange("p (a b c) -> p a b c", a=shape[0], b=shape[1])
            return a

        ps = ctx.enter_context(nc.psum_tensor("ps", [P, 8, SEQ], F32))

        ident = C[:, C_ID:C_ID + P]
        id64 = C[:, C_ID64:C_ID64 + CH]

        at[0] = 0
        Vt = arena(TT, 256)
        vh = arena(TT, P)
        qT = arena(SEQ)
        kT = arena(SEQ)
        sc = arena(SEQ)
        pr = arena(SEQ)
        pT = arena(TT, P)
        stat = arena(4)
        at[0] = 0
        px = [arena(16 + SEQ) for _ in range(2)]
        pw = [arena(16 + SEQ) for _ in range(2)]
        at[0] = 0
        baT = arena(SEQ)
        ba = arena(2, PAIRS, NC)
        spl = arena(3, PAIRS, NC)
        ealog = arena(PAIRS)
        tok = arena(6, PAIRS * NC)
        tk = arena(6, NC)
        cw = arena(12)
        at_cv = at[0]
        cv = arena(3, 4 + SEQ)
        end_cv, at[0] = at[0], at_cv
        XX, MT, P1 = (arena(NC, CH) for _ in range(3))
        at[0] = end_cv
        qkv = arena(3, SEQ)
        zz = arena(SEQ)
        E1, E2, A_, AT, XT = (arena(NC, CH) for _ in range(5))
        kd, kg, vb, Uu, wT, aq, oo = (arena(NC, CH) for _ in range(7))
        St = arena(CH)
        vn = arena(CH)
        ost = arena(NC)
        at[0] = 0
        cg = arena(NE, SEQ)
        lg, oh1, oh2, tt1, comb = (arena(TT, NE) for _ in range(5))
        m1, m2, m3 = (arena(TT) for _ in range(3))
        cb = arena(TT, P)
        gu = arena(SEQ)
        at[0] = 2 * KT * MEM
        xv = arena(2, XH * P)
        xvh = arena(2, P)
        xq = arena(SEQ)
        xk = arena(MEM)
        xp = arena(MEM)
        xpT = arena(2, SEQ)
        xst = arena(4)
        memx = arena(KT, MEM)
        at[0] = 0
        final = arena(KT, SEQ)
        gts = [tB, tC, tD]

        load_x = sem("load_x")
        load_mem = sem("load_mem")
        load_pos = sem("load_pos")
        load_cst = sem("load_cst")
        load_vec = sem("load_vec")
        load_sm = sem("load_sm")
        raw_full = [sem(f"raw_full{s}") for s in range(2)]
        raw_free = [sem(f"raw_free{s}") for s in range(2)]
        split_full = [sem(f"split_full{s}") for s in range(2)]
        split_free = [sem(f"split_free{s}") for s in range(2)]
        pool_own = sem("pool_own")
        act_own = sem("act_own")
        dve_own = sem("dve_own")
        acc_free = [sem(f"acc_free{s}") for s in range(2)]
        to_act = sem("to_act")
        to_dve = sem("to_dve")
        act_pe = sem("act_pe")
        dve_pe = sem("dve_pe")
        act_dve = sem("act_dve")
        dve_act = sem("dve_act")
        dve_sp = sem("dve_sp")
        store_out = sem("store_out")

        block = ctx.enter_context(nc.Block())

        @block.sync
        def _(sp):
            sp.dma_start(C[:, :], cst).then_inc(load_cst, 16)
            sp.dma_start(tA[:, :].bitcast(I32), pos.to_broadcast([P, SEQ])).then_inc(load_pos, 16)
            sp.dma_start(X[:, :, :], x_t).then_inc(load_x, 16)
            for s in range(2):
                sp.sem_inc(raw_free[s], 1)
            with sp.Fori(0, DEPTH) as lay:
                sp.wait_ge(dve_sp, 1).then_inc(dve_sp, -1)
                sp.dma_start(vecs[:, :], vec[bass.ds(lay, 1)].rearrange("a p n -> (a p) n")).then_inc(load_vec, 16)
                sp.dma_start(wsmall[:, :], wsm[bass.ds(lay, 1)].rearrange("a p n -> (a p) n")).then_inc(load_sm, 16)
                with sp.Fori(0, MIX_UNITS // 2) as i:
                    for s in range(2):
                        sp.wait_ge(raw_free[s], 1).then_inc(raw_free[s], -1)
                        sp.dma_start(raw[:, s, 0:UNIT],
                                     wst[bass.ds(lay * (MIX_UNITS + DENSE_PARTS * 2 * FT) + i * 2 + s, 1)]
                                     .rearrange("a p n -> (a p) n")).then_inc(raw_full[s], 16)
                with sp.Fori(0, lay * (NE - DENSE_PARTS) + DENSE_PARTS) as e:
                    with sp.Fori(0, FT) as i:
                        for s in range(2):
                            sp.wait_ge(raw_free[s], 1).then_inc(raw_free[s], -1)
                            sp.dma_start(raw[:, s, 0:UNIT],
                                         wst[bass.ds(lay * (MIX_UNITS + DENSE_PARTS * 2 * FT) + MIX_UNITS
                                                     + e * (2 * FT) + i * 2 + s, 1)]
                                         .rearrange("a p n -> (a p) n")).then_inc(raw_full[s], 16)
                    with sp.Fori(0, KT // 2) as i:
                        for s in range(2):
                            sp.wait_ge(raw_free[s], 1).then_inc(raw_free[s], -1)
                            sp.dma_start(raw[:, s, :],
                                         wdn[bass.ds(lay * (DENSE_PARTS * KT) + e * KT + i * 2 + s, 1)]
                                         .rearrange("a p n -> (a p) n")).then_inc(raw_full[s], 16)
            sp.wait_ge(dve_sp, 1).then_inc(dve_sp, -1)
            sp.wait_ge(dve_sp, 1).then_inc(dve_sp, -1)
            sp.dma_start(out_t, final).then_inc(store_out, 16)
            sp.wait_ge(store_out, 16)

        @block.gpsimd
        def _(pool):
            for s in range(2):
                pool.sem_inc(split_free[s], 1)

            def split(s, n):
                pool.wait_ge(raw_full[s], 16).then_inc(raw_full[s], -16)
                pool.wait_ge(split_free[s], 1).then_inc(split_free[s], -1)
                nc.gpsimd.tensor_copy(w_hi[:, s, 0:n], raw[:, s, 0:n]).then_inc(pool_own, 1)
                pool.wait_ge(pool_own, 1).then_inc(pool_own, -1)
                nc.gpsimd.tensor_tensor(w_lo[:, s, 0:n], raw[:, s, 0:n], w_hi[:, s, 0:n].bitcast(F32),
                                        ALU.subtract).then_inc(pool_own, 1)
                pool.wait_ge(pool_own, 1).then_inc(pool_own, -1)
                pool.sem_inc(raw_free[s], 1)
                pool.sem_inc(split_full[s], 1)

            with pool.Fori(0, DEPTH) as lay:
                with pool.Fori(0, MIX_UNITS // 2):
                    for s in range(2):
                        split(s, UNIT)
                with pool.Fori(0, lay * (NE - DENSE_PARTS) + DENSE_PARTS):
                    with pool.Fori(0, FT):
                        for s in range(2):
                            split(s, UNIT)
                    with pool.Fori(0, KT // 2):
                        for s in range(2):
                            split(s, BIG)

        @block.tensor
        def _(pe):
            mm = nc.tensor.matmul

            def prod3(acc, whi, wlo, xhi, xlo, start, stop):
                mm(acc, wlo, xhi, start=start, stop=False)
                mm(acc, whi, xlo, start=False, stop=False)
                return mm(acc, whi, xhi, start=False, stop=stop)

            def unit(s, hi, lo, n=SEQ, nk=KT):
                pe.wait_ge(split_full[s], 1).then_inc(split_full[s], -1)
                pe.wait_ge(acc_free[s], 1).then_inc(acc_free[s], -1)
                for k in range(nk):
                    last = prod3(ps[:, s, 0:n], w_hi[:, s, k * P:(k + 1) * P], w_lo[:, s, k * P:(k + 1) * P],
                                 hi[:, k, 0:n], lo[:, k, 0:n], k == 0, k == nk - 1)
                return last

            def sumsq(n=SEQ):
                for k in range(KT):
                    pe.wait_ge(act_pe, 1).then_inc(act_pe, -1)
                    mm(ps[:, 2, 0:n], C[:, C_ONE:C_ONE + P], (tA, tE)[k % 2][:, 0:n],
                       start=(k == 0), stop=(k == KT - 1)).then_inc(to_act, 1)

            def both(o, a, b, n):
                for h in range(2):
                    q = slice(h * HD, (h + 1) * HD)
                    last = mm(o(q), a(q), b(q), start=True, stop=True)
                return last

            def cs(n):
                return slice(n * CH, (n + 1) * CH)

            pe.wait_ge(load_cst, 16)
            for s in range(2):
                pe.sem_inc(acc_free[s], 1)
            with pe.Fori(0, DEPTH) as lay:
                pe.wait_ge(load_sm, 16).then_inc(load_sm, -16)
                sumsq()
                pe.wait_ge(dve_pe, 1).then_inc(dve_pe, -1)
                for s in range(2):
                    unit(s, h_hi, h_lo).then_inc(to_dve, 1)
                for b in range(2):
                    pe.wait_ge(dve_pe, 1).then_inc(dve_pe, -1)
                    mm(ps[:, 2 + b, :], wsmall[:, b * P:(b + 1) * P], (tB, tC)[b][:, :],
                       start=True, stop=True).then_inc(to_dve, 1)
                for s in range(2):
                    pe.wait_ge(split_full[s], 1).then_inc(split_full[s], -1)
                    if s == 0:
                        pe.wait_ge(dve_pe, 1).then_inc(dve_pe, -1)
                    for t in range(TT):
                        for k in range(4):
                            last = prod3(ps[:, 2 + t, 0:256], h_hi[:, 4 * s + k, t * P:(t + 1) * P],
                                         h_lo[:, 4 * s + k, t * P:(t + 1) * P],
                                         w_hi[:, s, k * 256:(k + 1) * 256], w_lo[:, s, k * 256:(k + 1) * 256],
                                         s == 0 and k == 0, s == 1 and k == 3)
                    last.then_inc(to_act, 1)
                pe.wait_ge(act_pe, 1).then_inc(act_pe, -1)
                with pe.Fori(0, MOBA_PAIRS):
                    for s in range(2):
                        unit(s, h_hi, h_lo).then_inc(to_dve, 1)
                    for s in range(2):
                        pe.wait_ge(dve_pe, 1).then_inc(dve_pe, -1)
                        mm(ps[:, 2 + s, :], C[:, C_ROT:C_ROT + P], (qT, kT)[s], start=True, stop=True).then_inc(to_dve, 1)
                    pe.wait_ge(dve_pe, 1).then_inc(dve_pe, -1)
                    for h in range(2):
                        q = slice(h * HD, (h + 1) * HD)
                        for t in range(TT):
                            nk = t + 1
                            mm(ps[:, 3, 0:nk * P], qT[q, t * P:(t + 1) * P], kT[q, 0:nk * P],
                               start=True, stop=True).then_inc(to_dve, 1)
                            pe.wait_ge(dve_pe, 1).then_inc(dve_pe, -1)
                            for k in range(nk):
                                last = nc.tensor.transpose(ps[:, 4, k * P:(k + 1) * P], pr[:, k * P:(k + 1) * P], ident)
                            last.then_inc(to_act, 1)
                            pe.wait_ge(act_pe, 1).then_inc(act_pe, -1)
                            for k in range(nk):
                                last = mm(ps[q, 5, t * P:(t + 1) * P], vh[:, k, q], pT[:, k, :],
                                          start=(k == 0), stop=(k == nk - 1))
                    last.then_inc(to_dve, 1)
                    pe.wait_ge(dve_pe, 1).then_inc(dve_pe, -1)
                for k in range(KT):
                    w = wsmall[:, 2 * P + k * 16:2 * P + (k + 1) * 16]
                    for part in (h_lo, h_hi):
                        last = mm(ps[0:16, 2, :], w, part[:, k, :].bitcast(F32),
                                  start=(k == 0 and part is h_lo), stop=(k == KT - 1 and part is h_hi))
                last.then_inc(to_act, 1)
                pe.wait_ge(act_pe, 1).then_inc(act_pe, -1)
                for n in range(NC):
                    for h in range(2):
                        last = mm(ps[h * CH:(h + 1) * CH, 3, n * 16:(n + 1) * 16], baT[0:16, cs(n)], ident[0:16, 0:16],
                                  start=True, stop=True)
                last.then_inc(to_dve, 1)
                pe.wait_ge(dve_pe, 1).then_inc(dve_pe, -1)
                mm(ps[:, 2, 0:32], C[:, C_UB:C_UB + P], tok[:, 0, :], start=True, stop=True)
                mm(ps[:, 2, 64:96], C[:, C_VB:C_VB + P], tok[:, 0, :], start=True, stop=True)
                mm(ps[:, 2, 128:160], C[:, C_BONE:C_BONE + P], tok[:, 0, :], start=True, stop=True).then_inc(to_act, 1)
                pe.wait_ge(act_pe, 1).then_inc(act_pe, -1)
                with pe.Fori(0, PAIRS):
                    for u in range(4):
                        unit(u % 2, h_hi, h_lo).then_inc(to_dve if u < 3 else to_act, 1)
                    for u in range(2):
                        pe.wait_ge(act_pe, 1).then_inc(act_pe, -1)
                        mm(ps[:, 2 + u, :], C[:, C_BONE:C_BONE + P], (tA, tE)[u][:, :], start=True, stop=True).then_inc(to_act, 1)
                    pe.wait_ge(dve_pe, 1).then_inc(dve_pe, -1)
                    mm(ps[:, 4, :], C[:, C_UB:C_UB + P], E1.rearrange("p a b -> p (a b)"), start=True, stop=True)
                    mm(ps[:, 5, :], C[:, C_VB:C_VB + P], E2.rearrange("p a b -> p (a b)"),
                       start=True, stop=True).then_inc(to_act, 1)
                    pe.wait_ge(dve_pe, 1).then_inc(dve_pe, -1)
                    Q, K, V = (qkv[:, i, :] for i in range(3))
                    for n in range(NC):
                        both(lambda q: ps[q, 2, cs(n)], lambda q: K[q, cs(n)], lambda q: K[q, cs(n)], CH)
                        both(lambda q: ps[q, 3, cs(n)], lambda q: K[q, cs(n)], lambda q: Q[q, cs(n)], CH)
                        both(lambda q: ps[q, 4, cs(n)], lambda q: K[q, cs(n)], lambda q: id64[q, :], CH)
                        last = both(lambda q: ps[q, 5, cs(n)], lambda q: V[q, cs(n)], lambda q: id64[q, :], CH)
                    last.then_inc(to_dve, 1)
                    pe.wait_ge(dve_pe, 1).then_inc(dve_pe, -1)
                    for n in range(NC):
                        last = both(lambda q: ps[q, 2, cs(n)], lambda q: A_[q, n, :], lambda q: id64[q, :], CH)
                    last.then_inc(to_dve, 1)
                    for l in range(1, LEVELS):
                        pe.wait_ge(dve_pe, 1).then_inc(dve_pe, -1)
                        for n in range(NC):
                            last = both(lambda q: ps[q, 2, cs(n)], lambda q: MT[q, n, :], lambda q: XX[q, n, :], CH)
                        last.then_inc(to_act, 1)
                        pe.wait_ge(act_pe, 1).then_inc(act_pe, -1)
                        for n in range(NC):
                            both(lambda q: ps[q, 3, cs(n)], lambda q: XT[q, n, :], lambda q: P1[q, n, :], CH)
                            last = both(lambda q: ps[q, 4, cs(n)], lambda q: P1[q, n, :], lambda q: XT[q, n, :], CH)
                        last.then_inc(to_dve, 1)
                    pe.wait_ge(dve_pe, 1).then_inc(dve_pe, -1)
                    for n in range(NC):
                        both(lambda q: ps[q, 2, cs(n)], lambda q: XT[q, n, :], lambda q: vb[q, n, :], CH)
                        last = both(lambda q: ps[q, 3, cs(n)], lambda q: kg[q, n, :], lambda q: XT[q, n, :], CH)
                    last.then_inc(to_act, 1)
                    pe.wait_ge(act_pe, 1).then_inc(act_pe, -1)
                    for n in range(NC):
                        both(lambda q: ps[q, 4, 0:CH], lambda q: wT[q, n, :], lambda q: St[q, :], CH).then_inc(to_dve, 1)
                        both(lambda q: ps[q, 5, 0:CH], lambda q: Q[q, cs(n)], lambda q: St[q, :], CH).then_inc(to_dve, 1)
                        pe.wait_ge(dve_pe, 1).then_inc(dve_pe, -1)
                        both(lambda q: ps[q, 6, 0:CH], lambda q: kd[q, n, :], lambda q: vn[q, :], CH).then_inc(to_dve, 1)
                        both(lambda q: ps[q, 7, 0:CH], lambda q: aq[q, n, :], lambda q: vn[q, :], CH).then_inc(to_dve, 1)
                        pe.wait_ge(dve_pe, 1).then_inc(dve_pe, -1)
                    pe.wait_ge(dve_pe, 1).then_inc(dve_pe, -1)
                    for n in range(NC):
                        last = both(lambda q: ps[q, 2, cs(n)], lambda q: oo[q, n, :], lambda q: id64[q, :], CH)
                    last.then_inc(to_dve, 1)
                    pe.wait_ge(dve_pe, 1).then_inc(dve_pe, -1)
                with pe.Fori(0, KT):
                    for s in (0, 1, 0):
                        unit(s, h_hi, h_lo).then_inc(to_act, 1)
                    pe.wait_ge(split_full[1], 1).then_inc(split_full[1], -1)
                    pe.wait_ge(dve_pe, 1).then_inc(dve_pe, -1)
                    for br, (k0, k1) in enumerate(((0, 2), (2, 4), (4, 8))):
                        for k in range(k0, k1):
                            last = prod3(ps[:, 2 + br, :], w_hi[:, 1, k * P:(k + 1) * P], w_lo[:, 1, k * P:(k + 1) * P],
                                         B_hi[:, k, :], B_lo[:, k, :], k == k0, k == k1 - 1)
                    last.then_inc(to_dve, 1)
                pe.wait_ge(dve_pe, 1).then_inc(dve_pe, -1)
                with pe.Fori(0, KT // 2):
                    for s in range(2):
                        unit(s, M_hi, M_lo).then_inc(to_dve, 1)
                sumsq()
                pe.wait_ge(dve_pe, 1).then_inc(dve_pe, -1)
                sumsq(MEM)
                pe.wait_ge(dve_pe, 1).then_inc(dve_pe, -1)
                for u in range(4):
                    s = u % 2
                    pe.wait_ge(split_full[s], 1).then_inc(split_full[s], -1)
                    for t in range(2):
                        for k in range(2):
                            last = prod3(ps[:, 4 + t, :], N_hi[:, 2 * u + k, t * P:(t + 1) * P],
                                         N_lo[:, 2 * u + k, t * P:(t + 1) * P],
                                         w_hi[:, s, k * SEQ:(k + 1) * SEQ], w_lo[:, s, k * SEQ:(k + 1) * SEQ],
                                         u == 0 and k == 0, u == 3 and k == 1)
                    last.then_inc(to_act, 1)
                pe.wait_ge(act_pe, 1).then_inc(act_pe, -1)
                with pe.Fori(0, XH):
                    unit(0, h_hi, h_lo).then_inc(to_dve, 1)
                    unit(1, N_hi, N_lo, MEM).then_inc(to_dve, 1)
                    pe.wait_ge(dve_pe, 1).then_inc(dve_pe, -1)
                    for t in range(TT):
                        mm(ps[:, 3, 0:MEM], xq[:, t * P:(t + 1) * P], xk, start=True, stop=True).then_inc(to_dve, 1)
                        pe.wait_ge(dve_pe, 1).then_inc(dve_pe, -1)
                        for k in range(2):
                            last = nc.tensor.transpose(ps[:, 4, k * P:(k + 1) * P], xp[:, k * P:(k + 1) * P], ident)
                        last.then_inc(to_act, 1)
                        pe.wait_ge(act_pe, 1).then_inc(act_pe, -1)
                    for k in range(2):
                        last = mm(ps[:, 5, :], xvh[:, k, :], xpT[:, k, :], start=(k == 0), stop=(k == 1))
                    last.then_inc(to_dve, 1)
                    pe.wait_ge(dve_pe, 1).then_inc(dve_pe, -1)
                with pe.Fori(0, KT // 4):
                    for s in range(2):
                        pe.wait_ge(split_full[s], 1).then_inc(split_full[s], -1)
                        pe.wait_ge(acc_free[s], 1).then_inc(acc_free[s], -1)
                        for j in range(2):
                            for k in range(4):
                                c = (j * 4 + k) * P
                                last = prod3(ps[:, (s, 2 + s)[j], :], w_hi[:, s, c:c + P], w_lo[:, s, c:c + P],
                                             B_hi[:, k, :], B_lo[:, k, :], k == 0, k == 3)
                        last.then_inc(to_dve, 1)
                sumsq()
                pe.wait_ge(dve_pe, 1).then_inc(dve_pe, -1)
                for t in range(TT):
                    for k in range(KT):
                        c = 2 * P + KT * 16 + k * NE
                        for part in (h_lo, h_hi):
                            last = mm(ps[:, 4 + t, 0:NE], part[:, k, t * P:(t + 1) * P].bitcast(F32), wsmall[:, c:c + NE],
                                      start=(k == 0 and part is h_lo), stop=(k == KT - 1 and part is h_hi))
                last.then_inc(to_dve, 1)
                with pe.Fori(0, NE):
                    pe.wait_ge(dve_pe, 1).then_inc(dve_pe, -1)
                    for t in range(TT):
                        last = mm(ps[:, 3, t * P:(t + 1) * P], cb[:, t, :], ident, start=True, stop=True)
                    last.then_inc(to_dve, 1)
                pe.wait_ge(dve_pe, 1).then_inc(dve_pe, -1)
                with pe.Fori(0, lay * (NE - DENSE_PARTS) + DENSE_PARTS):
                    with pe.Fori(0, FT):
                        unit(0, h_hi, h_lo).then_inc(to_act, 1)
                        unit(1, h_hi, h_lo).then_inc(to_dve, 1)
                    pe.wait_ge(dve_pe, 1).then_inc(dve_pe, -1)
                    with pe.Fori(0, KT // 2):
                        for s in range(2):
                            unit(s, B_hi, B_lo, nk=FT).then_inc(to_dve, 1)
            sumsq()

        @block.scalar
        def _(act):
            def fn(out, in_, f, *posts, **kw):
                nc.scalar.activation(out, in_, f, **kw).then_inc(act_own, 1)
                act.wait_ge(act_own, 1).then_inc(act_own, -1)
                for p in posts:
                    act.sem_inc(p, 1)

            def rsqrt(out, in_, scale, *posts):
                fn(out, in_, ACT.Ln, scale=scale, bias=C[0:out.shape[0], C_EPS:C_EPS + 1])
                fn(out, out, ACT.Exp, *posts, scale=-0.5)

            def norm(src, n=SEQ):
                for k in range(KT):
                    if k >= 2:
                        act.wait_ge(to_act, 1).then_inc(to_act, -1)
                    fn((tA, tE)[k % 2][:, 0:n], src[:, k, 0:n], ACT.Square, act_pe)
                for _ in range(2):
                    act.wait_ge(to_act, 1).then_inc(to_act, -1)
                rsqrt(rinv[:, 0:n], ps[:, 2, 0:n], 1.0 / D, act_dve)

            act.wait_ge(load_cst, 16)
            act.wait_ge(load_x, 16)
            for t in (ropeC, ropeS):
                act.wait_ge(dve_act, 1).then_inc(dve_act, -1)
                fn(t[:, :], t[:, :], ACT.Sin, act_dve)
            with act.Fori(0, DEPTH) as lay:
                act.wait_ge(dve_act, 1).then_inc(dve_act, -1)
                norm(X)
                for s in range(2):
                    act.wait_ge(to_act, 1).then_inc(to_act, -1)
                    act.sem_inc(split_free[s], 1)
                fn(Vt, ps[:, 2:6, 0:256], ACT.Copy, act_pe)
                with act.Fori(0, MOBA_PAIRS):
                    for h in range(2):
                        for t in range(TT):
                            nk = t + 1
                            act.wait_ge(dve_act, 1).then_inc(dve_act, -1)
                            fn(pr[:, 0:nk * P], sc[:, 0:nk * P], ACT.Exp, act_dve, bias=stat[:, 0:1], accum_out=stat[:, 1:2])
                            act.wait_ge(to_act, 1).then_inc(to_act, -1)
                            fn(pT[:, 0:nk, :].rearrange("p a b -> p (a b)"), ps[:, 4, 0:nk * P], ACT.Copy, act_pe)
                act.wait_ge(to_act, 1).then_inc(to_act, -1)
                fn(baT[0:16, :], ps[0:16, 2, :], ACT.Copy, act_pe)
                act.wait_ge(dve_act, 1).then_inc(dve_act, -1)
                fn(spl[:, 0], spl[:, 0], ACT.Exp)
                fn(spl[:, 0], spl[:, 0], ACT.Ln, bias=C[:, C_ONE:C_ONE + 1])
                fn(ealog, vecs[:, V_ALOG:V_ALOG + PAIRS], ACT.Exp)
                fn(spl[:, 1], ba[:, 0], ACT.Exp, act_dve, scale=-1.0)
                act.wait_ge(to_act, 1).then_inc(to_act, -1)
                fn(tok[:, 3, :], ps[:, 2, 0:32], ACT.Exp)
                fn(tok[:, 4, :], ps[:, 2, 64:96], ACT.Exp)
                fn(tok[:, 5, :], ps[:, 2, 128:160], ACT.Exp, act_pe, act_dve)
                with act.Fori(0, PAIRS):
                    for u in range(3):
                        act.wait_ge(dve_act, 1).then_inc(dve_act, -1)
                        fn(qkv[:, u, :], (tB, tC, tD)[u][:, :], ACT.Silu)
                        if u < 2:
                            fn((tA, tE)[u][:, :], qkv[:, u, :], ACT.Square, act_pe)
                    act.wait_ge(to_act, 1).then_inc(to_act, -1)
                    act.sem_inc(split_free[1], 1)
                    fn(zz, ps[:, 1, :], ACT.Silu, acc_free[1])
                    for u in range(2):
                        act.wait_ge(to_act, 1).then_inc(to_act, -1)
                        rsqrt((tA, tE)[u][:, :], ps[:, 2 + u, :], 1.0, act_dve)
                    act.wait_ge(to_act, 1).then_inc(to_act, -1)
                    fn(E1.rearrange("p a b -> p (a b)"), ps[:, 4, :], ACT.Exp)
                    fn(E2.rearrange("p a b -> p (a b)"), ps[:, 5, :], ACT.Exp, act_dve)
                    for l in range(1, LEVELS):
                        act.wait_ge(to_act, 1).then_inc(to_act, -1)
                        fn(P1.rearrange("p a b -> p (a b)"), ps[:, 2, :], ACT.Copy, act_pe)
                    act.wait_ge(to_act, 1).then_inc(to_act, -1)
                    fn(Uu.rearrange("p a b -> p (a b)"), ps[:, 2, :], ACT.Copy)
                    fn(wT.rearrange("p a b -> p (a b)"), ps[:, 3, :], ACT.Copy, act_pe)
                    act.wait_ge(dve_act, 1).then_inc(dve_act, -1)
                    rsqrt(ost, ost, 1.0 / HD, act_dve)
                with act.Fori(0, KT):
                    act.wait_ge(dve_act, 1).then_inc(dve_act, -1)
                    for b, s in enumerate((0, 1, 0)):
                        act.wait_ge(to_act, 1).then_inc(to_act, -1)
                        act.sem_inc(split_free[s], 1)
                        fn(gts[b][:, :], ps[:, s, :], ACT.Sigmoid, acc_free[s], act_dve)
                act.wait_ge(dve_act, 1).then_inc(dve_act, -1)
                act.wait_ge(dve_act, 1).then_inc(dve_act, -1)
                act.dma_start(memx, mem_t).then_inc(load_mem, 16)
                norm(X)
                act.wait_ge(load_mem, 16).then_inc(load_mem, -16)
                norm(memx, MEM)
                for u in range(4):
                    act.wait_ge(to_act, 1).then_inc(to_act, -1)
                    act.sem_inc(split_free[u % 2], 1)
                fn(xv, ps[:, 4:6, :], ACT.Copy, act_pe)
                with act.Fori(0, XH):
                    for t in range(TT):
                        act.wait_ge(dve_act, 1).then_inc(dve_act, -1)
                        fn(xp, ps[:, 3, 0:MEM], ACT.Exp, act_dve, bias=xst[:, 0:1], scale=float(P) ** -0.5,
                           accum_out=xst[:, 1:2])
                        act.wait_ge(to_act, 1).then_inc(to_act, -1)
                        fn(xpT[:, :, t * P:(t + 1) * P], ps[:, 4, 0:MEM].rearrange("p (a b) -> p a b", a=2), ACT.Copy, act_pe)
                act.wait_ge(dve_act, 1).then_inc(dve_act, -1)
                norm(X)
                act.wait_ge(dve_act, 1).then_inc(dve_act, -1)
                fn(m3, m3, ACT.Exp, act_dve)
                with act.Fori(0, lay * (NE - DENSE_PARTS) + DENSE_PARTS):
                    with act.Fori(0, FT):
                        act.wait_ge(to_act, 1).then_inc(to_act, -1)
                        act.sem_inc(split_free[0], 1)
                        act.wait_ge(dve_act, 1).then_inc(dve_act, -1)
                        fn(gu, ps[:, 0, :], ACT.Silu, acc_free[0], act_dve)
                act.wait_ge(dve_act, 1).then_inc(dve_act, -1)
            act.wait_ge(dve_act, 1).then_inc(dve_act, -1)
            norm(X)

        @block.vector
        def _(dve):
            V = nc.vector

            def v(ins, *posts):
                ins.then_inc(dve_own, 1)
                dve.wait_ge(dve_own, 1).then_inc(dve_own, -1)
                for p in posts:
                    dve.sem_inc(p, 1)

            def parts(src, hi, lo, *posts):
                v(V.tensor_copy(hi, src))
                v(V.tensor_tensor(lo, src, hi.bitcast(F32), ALU.subtract), *posts)

            def tile_of(t, i):
                return t[:, bass.ds(i, 1), :].rearrange("p a n -> p (a n)")

            def norm(src, g, hi, lo, n=SEQ):
                dve.wait_ge(act_dve, 1).then_inc(act_dve, -1)
                for k in range(KT):
                    tmp = (tB, tC)[k % 2][:, 0:n]
                    v(V.scalar_tensor_tensor(out=tmp, in0=src[:, k, 0:n], scalar=vecs[:, g + k:g + k + 1],
                                             in1=rinv[:, 0:n], op0=ALU.mult, op1=ALU.mult))
                    parts(tmp, hi[:, k, 0:n], lo[:, k, 0:n])
                dve.sem_inc(dve_pe, 1)

            def rows(col, w):
                return C[:, None, col:col + w].to_broadcast([P, NC, w])

            def chan(i):
                return tk[:, i, :, None].to_broadcast([P, NC, CH])

            dve.wait_ge(load_cst, 16)
            dve.wait_ge(load_pos, 16)
            v(V.tensor_copy(tB[:, :], tA[:, :].bitcast(I32)))
            v(V.tensor_scalar(tB[:, :], tB[:, :], C[:, C_FREQ:C_FREQ + 1], None, ALU.mult))
            v(V.tensor_scalar(tC[:, :], tB[:, :], float(1 / (2 * np.pi)), MAGIC, ALU.mult, ALU.add))
            v(V.tensor_scalar(tC[:, :], tC[:, :], MAGIC, None, ALU.subtract))
            c1 = 6.28125
            c2 = float(np.float32(np.round((2 * np.pi - c1) * 2 ** 22) / 2 ** 22))
            c3 = float(2 * np.pi - c1 - c2)
            for c in (c1, c2, c3):
                v(V.scalar_tensor_tensor(out=tB[:, :], in0=tC[:, :], scalar=-c, in1=tB[:, :], op0=ALU.mult, op1=ALU.add))
            v(V.tensor_scalar(tC[:, :], tB[:, :], float(np.pi / 2), None, ALU.add))
            v(V.tensor_scalar(tD[:, :], tC[:, :], float(np.pi), -2 * float(np.pi), ALU.is_gt, ALU.mult))
            v(V.tensor_tensor(tC[:, :], tC[:, :], tD[:, :], ALU.add))
            for t, src in ((ropeC, tC), (ropeS, tB)):
                v(V.tensor_scalar(t[:, :], src[:, :], 3.14159, -3.14159, ALU.min, ALU.max), dve_act)
            for _ in range(2):
                dve.wait_ge(act_dve, 1).then_inc(act_dve, -1)
            dve.sem_inc(dve_act, 1)
            dve.sem_inc(dve_sp, 1)
            with dve.Fori(0, DEPTH) as lay:
                dve.wait_ge(load_vec, 16).then_inc(load_vec, -16)
                norm(X, V_MIXG, h_hi, h_lo)
                for b in range(2):
                    v(V.memset(px[b][:, 0:16], 0.0))
                    v(V.memset(pw[b][:, 0:16], 0.0))
                    dve.wait_ge(to_dve, 1).then_inc(to_dve, -1)
                    dve.sem_inc(split_free[b], 1)
                    v(V.tensor_copy(px[b][:, 16:], ps[:, b, :]), acc_free[b])

                def shifted(o, i, sh, rows=slice(0, P)):
                    v(V.tensor_tensor(o[rows, :], i[rows, 16:], i[rows, 16 - sh:16 + SEQ - sh], ALU.add))
                lo_half, hi_half = slice(0, HD), slice(HD, P)
                for b, out in ((0, tB), (1, tC)):
                    shifted(pw[0][:, 16:], px[b], 1)
                    if b == 1:
                        shifted(pw[1][:, 16:], pw[0], 2)
                        shifted(pw[0][:, 16:], pw[1], 4)
                    v(V.tensor_copy(out[lo_half, :], pw[0][lo_half, 16:]))
                    shifted(out[:, :], pw[0], (2, 8)[b], hi_half)
                    v(V.tensor_tensor(out[:, :], out[:, :], C[:, C_CNT + b * SEQ:C_CNT + (b + 1) * SEQ], ALU.mult))
                    v(V.tensor_tensor(out[:, :], out[:, :], px[b][:, 16:], ALU.subtract), dve_pe)
                for b in range(2):
                    dve.wait_ge(to_dve, 1).then_inc(to_dve, -1)
                    v(V.tensor_scalar(tD[:, :], ps[:, 2 + b, :], vecs[:, V_POOLS + b:V_POOLS + b + 1], None, ALU.mult))
                    parts(tD[:, :], B_hi[:, b, :], B_lo[:, b, :])
                dve.sem_inc(dve_pe, 1)
                with dve.Fori(0, MOBA_PAIRS) as j:
                    for s in range(2):
                        dve.wait_ge(to_dve, 1).then_inc(to_dve, -1)
                        dve.sem_inc(split_free[s], 1)
                        v(V.tensor_copy((qT, kT)[s], ps[:, s, :]), acc_free[s], dve_pe)
                    for s in range(2):
                        dve.wait_ge(to_dve, 1).then_inc(to_dve, -1)
                        x = (qT, kT)[s]
                        v(V.tensor_tensor(tB[:, :], ps[:, 2 + s, :], ropeS[:, :], ALU.mult))
                        v(V.tensor_tensor(x, x, ropeC[:, :], ALU.mult))
                        v(V.tensor_tensor(x, x, tB[:, :], ALU.add))
                    v(V.tensor_copy(vh, Vt[:, :, bass.ds(j * P, P)]), dve_pe)
                    for h in range(2):
                        for t in range(TT):
                            n = (t + 1) * P
                            dve.wait_ge(to_dve, 1).then_inc(to_dve, -1)
                            v(V.scalar_tensor_tensor(out=sc[:, 0:n], in0=ps[:, 3, 0:n], scalar=float(HD) ** -0.5,
                                                     in1=C[:, C_CAUS + SEQ - n:C_CAUS + SEQ], op0=ALU.mult, op1=ALU.add))
                            v(V.tensor_reduce(stat[:, 0:1], sc[:, 0:n], AX.X, ALU.max, negate=True), dve_act)
                            dve.wait_ge(act_dve, 1).then_inc(act_dve, -1)
                            v(V.reciprocal(stat[:, 2:3], stat[:, 1:2]))
                            v(V.tensor_scalar(pr[:, 0:n], pr[:, 0:n], stat[:, 2:3], None, ALU.mult), dve_pe)
                    dve.wait_ge(to_dve, 1).then_inc(to_dve, -1)
                    parts(ps[:, 5, :], tile_of(B_hi, j + 2), tile_of(B_lo, j + 2), dve_pe)
                dve.wait_ge(to_dve, 1).then_inc(to_dve, -1)
                for h in range(2):
                    q = slice(h * CH, (h + 1) * CH)
                    v(V.tensor_copy(ba[q].rearrange("p a b c -> p (a b) c"),
                                    ps[q, 3, 0:NC * 16].rearrange("p (n m h) -> p h m n", n=NC, h=2)[:, h]))
                dtb = vecs[:, V_DTB:V_DTB + PAIRS, None].to_broadcast([P, PAIRS, NC])
                v(V.tensor_tensor(spl[:, 2], ba[:, 1], dtb, ALU.add))
                v(V.scalar_tensor_tensor(out=spl[:, 0], in0=spl[:, 2], scalar=-1.0, in1=spl[:, 2], op0=ALU.mult, op1=ALU.min), dve_act)
                dve.wait_ge(act_dve, 1).then_inc(act_dve, -1)
                v(V.scalar_tensor_tensor(out=spl[:, 2], in0=spl[:, 2], scalar=0.0, in1=spl[:, 0], op0=ALU.max, op1=ALU.add))
                tg = tok[:, 0].rearrange("p (a b) -> p a b", a=PAIRS)
                v(V.scalar_tensor_tensor(out=tg, in0=spl[:, 2], scalar=-1.0, in1=ealog[:, :, None].to_broadcast([P, PAIRS, NC]),
                                         op0=ALU.mult, op1=ALU.mult), dve_pe)
                v(V.tensor_scalar(spl[:, 1], spl[:, 1], 1.0, None, ALU.add))
                v(V.reciprocal(tok[:, 1].rearrange("p (a b) -> p a b", a=PAIRS), spl[:, 1]))
                dve.wait_ge(act_dve, 1).then_inc(act_dve, -1)
                v(V.tensor_tensor(tok[:, 2], tok[:, 1], tok[:, 3], ALU.mult))
                with dve.Fori(0, PAIRS) as j:
                    v(V.tensor_copy(tk, tok[:, :, bass.ds(j * NC, NC)]))
                    v(V.tensor_copy(cw, vecs[:, bass.ds(j * 12 + V_CONV, 12)]))
                    v(V.memset(St, 0.0))
                    v(V.memset(cv[:, :, 0:4], 0.0))
                    v(V.tensor_tensor(E1, rows(C_V64, CH), chan(0), ALU.mult))
                    v(V.tensor_tensor(E2, rows(C_U64, CH), chan(0), ALU.mult), dve_pe)
                    for u in range(3):
                        dve.wait_ge(to_dve, 1).then_inc(to_dve, -1)
                        dve.sem_inc(split_free[u % 2], 1)
                        v(V.tensor_copy(cv[:, u, 4:], ps[:, u % 2, :]), acc_free[u % 2])
                        y = (tB, tC, tD)[u][:, :]
                        v(V.tensor_scalar(y, cv[:, u, 1:1 + SEQ], cw[:, u * 4:u * 4 + 1], None, ALU.mult))
                        for tap in range(1, 4):
                            v(V.scalar_tensor_tensor(out=y, in0=cv[:, u, 1 + tap:1 + tap + SEQ],
                                                     scalar=cw[:, u * 4 + tap:u * 4 + tap + 1], in1=y,
                                                     op0=ALU.mult, op1=ALU.add), *((dve_act,) if tap == 3 else ()))
                    dve.wait_ge(act_dve, 1).then_inc(act_dve, -1)
                    v(V.scalar_tensor_tensor(out=qkv[:, 0, :], in0=qkv[:, 0, :], scalar=float(HD) ** -0.5, in1=tA[:, :],
                                             op0=ALU.mult, op1=ALU.mult))
                    dve.wait_ge(act_dve, 1).then_inc(act_dve, -1)
                    v(V.tensor_tensor(qkv[:, 1, :], qkv[:, 1, :], tE[:, :], ALU.mult))
                    dve.wait_ge(act_dve, 1).then_inc(act_dve, -1)
                    dve.sem_inc(dve_pe, 1)
                    v(V.tensor_tensor(E1, E1, rows(C_LOW, CH), ALU.mult))
                    v(V.tensor_tensor(E1, E1, chan(1), ALU.mult))
                    v(V.tensor_tensor(E2, E2, rows(C_UPI, CH), ALU.mult))
                    dve.wait_ge(to_dve, 1).then_inc(to_dve, -1)

                    def bank(b):
                        return ps[:, b, :].rearrange("p (a b) -> p a b", a=NC)
                    v(V.tensor_tensor(A_, bank(2), E1, ALU.mult), dve_pe)
                    v(V.tensor_tensor(aq, bank(3), E2, ALU.mult))
                    v(V.tensor_tensor(kd, bank(4), chan(4), ALU.mult))
                    v(V.tensor_tensor(kg, bank(4), chan(2), ALU.mult))
                    v(V.tensor_tensor(vb, bank(5), chan(1), ALU.mult))
                    dve.wait_ge(to_dve, 1).then_inc(to_dve, -1)
                    v(V.tensor_copy(AT, bank(2)))
                    v(V.tensor_tensor(XX, A_, rows(C_LV1, CH), ALU.mult))
                    v(V.tensor_tensor(XX, rows(C_ID64, CH), XX, ALU.subtract))
                    v(V.tensor_tensor(XT, AT, rows(C_LVT, CH), ALU.mult))
                    v(V.tensor_tensor(XT, rows(C_ID64, CH), XT, ALU.subtract))
                    for l in range(1, LEVELS):
                        v(V.tensor_tensor(MT, AT, rows(C_LVT + l * CH, CH), ALU.mult), dve_pe)
                        dve.wait_ge(to_dve, 1).then_inc(to_dve, -1)
                        v(V.tensor_tensor(XX, XX, bank(3), ALU.subtract))
                        v(V.tensor_tensor(XT, XT, bank(4), ALU.subtract))
                    dve.sem_inc(dve_pe, 1)
                    for n in range(NC):
                        dve.wait_ge(to_dve, 1).then_inc(to_dve, -1)
                        v(V.tensor_tensor(vn, Uu[:, n, :], ps[:, 4, 0:CH], ALU.subtract), dve_pe)
                        dve.wait_ge(to_dve, 1).then_inc(to_dve, -1)
                        v(V.tensor_scalar(oo[:, n, :], ps[:, 5, 0:CH], tk[:, 3, n:n + 1], None, ALU.mult))
                        dve.wait_ge(to_dve, 1).then_inc(to_dve, -1)
                        v(V.scalar_tensor_tensor(out=St, in0=St, scalar=tk[:, 5, n:n + 1], in1=ps[:, 6, 0:CH],
                                                 op0=ALU.mult, op1=ALU.add))
                        dve.wait_ge(to_dve, 1).then_inc(to_dve, -1)
                        v(V.tensor_tensor(oo[:, n, :], oo[:, n, :], ps[:, 7, 0:CH], ALU.add), dve_pe)
                    v(V.tensor_tensor(MT, oo, oo, ALU.mult))
                    v(V.tensor_reduce(ost, MT, AX.X, ALU.add), dve_act)
                    dve.wait_ge(act_dve, 1).then_inc(act_dve, -1)
                    v(V.tensor_tensor(oo, oo, ost[:, :, None].to_broadcast([P, NC, CH]), ALU.mult), dve_pe)
                    dve.wait_ge(to_dve, 1).then_inc(to_dve, -1)
                    v(V.scalar_tensor_tensor(out=tB[:, :], in0=ps[:, 2, :], scalar=vecs[:, V_DNG:V_DNG + 1], in1=zz,
                                             op0=ALU.mult, op1=ALU.mult))
                    parts(tB[:, :], tile_of(B_hi, j + 4), tile_of(B_lo, j + 4), dve_pe)
                dve.sem_inc(dve_pe, 1)
                dve.sem_inc(dve_act, 1)
                with dve.Fori(0, KT) as n:
                    dve.wait_ge(to_dve, 1).then_inc(to_dve, -1)
                    dve.sem_inc(split_free[1], 1)
                    for b in range(3):
                        dve.wait_ge(act_dve, 1).then_inc(act_dve, -1)
                        v(V.tensor_tensor(gts[b][:, :], gts[b][:, :], ps[:, 2 + b, :], ALU.mult))
                    for b in (1, 2):
                        v(V.tensor_tensor(tB[:, :], tB[:, :], gts[b][:, :], ALU.add))
                    parts(tB[:, :], tile_of(M_hi, n), tile_of(M_lo, n), dve_pe, dve_act)
                with dve.Fori(0, KT // 2) as i:
                    for s in range(2):
                        dve.wait_ge(to_dve, 1).then_inc(to_dve, -1)
                        dve.sem_inc(split_free[s], 1)
                        x = tile_of(X, i * 2 + s)
                        v(V.tensor_tensor(x, x, ps[:, s, :], ALU.add), acc_free[s])
                dve.sem_inc(dve_act, 1)
                norm(X, V_XAG, h_hi, h_lo)
                norm(memx, V_MEMG, N_hi, N_lo, MEM)
                with dve.Fori(0, XH) as h:
                    dve.wait_ge(to_dve, 1).then_inc(to_dve, -1)
                    dve.sem_inc(split_free[0], 1)
                    v(V.tensor_copy(xq, ps[:, 0, :]), acc_free[0])
                    dve.wait_ge(to_dve, 1).then_inc(to_dve, -1)
                    dve.sem_inc(split_free[1], 1)
                    v(V.tensor_copy(xk, ps[:, 1, 0:MEM]), acc_free[1])
                    v(V.tensor_copy(xvh, xv[:, :, bass.ds(h * P, P)]), dve_pe)
                    for t in range(TT):
                        dve.wait_ge(to_dve, 1).then_inc(to_dve, -1)
                        v(V.tensor_reduce(xst[:, 0:1], ps[:, 3, 0:MEM], AX.X, ALU.max))
                        v(V.tensor_scalar(xst[:, 0:1], xst[:, 0:1], -float(P) ** -0.5, None, ALU.mult), dve_act)
                        dve.wait_ge(act_dve, 1).then_inc(act_dve, -1)
                        v(V.reciprocal(xst[:, 2:3], xst[:, 1:2]))
                        v(V.tensor_scalar(xp, xp, xst[:, 2:3], None, ALU.mult), dve_pe)
                    dve.wait_ge(to_dve, 1).then_inc(to_dve, -1)
                    parts(ps[:, 5, :], tile_of(B_hi, h), tile_of(B_lo, h), dve_pe)
                with dve.Fori(0, KT // 4) as i:
                    for s in range(2):
                        dve.wait_ge(to_dve, 1).then_inc(to_dve, -1)
                        dve.sem_inc(split_free[s], 1)
                        for jj in range(2):
                            x = tile_of(X, i * 4 + 2 * s + jj)
                            v(V.tensor_tensor(x, x, ps[:, (s, 2 + s)[jj], :], ALU.add), *((acc_free[s],) if jj else ()))
                dve.sem_inc(dve_act, 1)
                norm(X, V_FFNG, h_hi, h_lo)
                dve.wait_ge(to_dve, 1).then_inc(to_dve, -1)
                v(V.tensor_copy(lg, ps[:, 4:8, 0:NE]))
                rank = C[:, None, C_RANK:C_RANK + NE].to_broadcast([P, TT, NE])

                def spread(m):
                    return m[:, :, None].to_broadcast([P, TT, NE])

                def best(m, oh):
                    v(V.tensor_reduce(m, lg, AX.X, ALU.max))
                    v(V.tensor_tensor(tt1, lg, spread(m), ALU.is_ge))
                    v(V.tensor_tensor(tt1, tt1, rank, ALU.mult))
                    v(V.tensor_reduce(m3, tt1, AX.X, ALU.max))
                    v(V.tensor_tensor(oh, tt1, spread(m3), ALU.is_ge))
                best(m1, oh1)
                v(V.scalar_tensor_tensor(out=lg, in0=oh1, scalar=NEG, in1=lg, op0=ALU.mult, op1=ALU.add))
                best(m2, oh2)
                v(V.tensor_tensor(m3, m2, m1, ALU.subtract), dve_act)
                dve.wait_ge(act_dve, 1).then_inc(act_dve, -1)
                v(V.tensor_scalar(m1, m3, 1.0, None, ALU.add))
                v(V.reciprocal(m1, m1))
                v(V.tensor_tensor(m2, m3, m1, ALU.mult))
                v(V.tensor_tensor(oh1, oh1, spread(m1), ALU.mult))
                v(V.tensor_tensor(oh2, oh2, spread(m2), ALU.mult))
                v(V.tensor_tensor(comb, oh1, oh2, ALU.add))
                v(V.tensor_scalar(comb.rearrange("p a b -> p (a b)"), comb.rearrange("p a b -> p (a b)"),
                                  vecs[:, V_DENSE:V_DENSE + 1], None, ALU.max))
                with dve.Fori(0, NE) as e:
                    v(V.tensor_copy(cb, comb[:, :, bass.ds(e, 1)].to_broadcast([P, TT, P])), dve_pe)
                    dve.wait_ge(to_dve, 1).then_inc(to_dve, -1)
                    v(V.tensor_copy(tile_of(cg, e), ps[:, 3, :]))
                dve.sem_inc(dve_pe, 1)
                dve.sem_inc(dve_act, 1)
                with dve.Fori(0, lay * (NE - DENSE_PARTS) + DENSE_PARTS) as e:
                    with dve.Fori(0, FT) as i:
                        dve.wait_ge(act_dve, 1).then_inc(act_dve, -1)
                        dve.wait_ge(to_dve, 1).then_inc(to_dve, -1)
                        dve.sem_inc(split_free[1], 1)
                        v(V.tensor_tensor(tB[:, :], gu, ps[:, 1, :], ALU.mult), acc_free[1], dve_act)
                        v(V.tensor_tensor(tB[:, :], tB[:, :], tile_of(cg, e), ALU.mult))
                        parts(tB[:, :], tile_of(B_hi, i), tile_of(B_lo, i))
                    dve.sem_inc(dve_pe, 1)
                    with dve.Fori(0, KT // 2) as i:
                        for s in range(2):
                            dve.wait_ge(to_dve, 1).then_inc(to_dve, -1)
                            dve.sem_inc(split_free[s], 1)
                            x = tile_of(X, i * 2 + s)
                            v(V.tensor_tensor(x, x, ps[:, s, :], ALU.add), acc_free[s])
                dve.sem_inc(dve_act, 1)
                dve.sem_inc(dve_sp, 1)
            dve.wait_ge(act_dve, 1).then_inc(act_dve, -1)
            for k in range(KT):
                v(V.scalar_tensor_tensor(out=final[:, k, :], in0=X[:, k, :],
                                         scalar=vecs[:, V_FING + k:V_FING + k + 1],
                                         in1=rinv[:, :], op0=ALU.mult, op1=ALU.mult))
            dve.sem_inc(dve_sp, 1)



def by_partition(w):
    return w.reshape(w.shape[0] // P, P, w.shape[1]).transpose(1, 0, 2)


def tiles(w, n_out):
    a = by_partition(w)
    k, n = a.shape[1], w.shape[1]
    a = a.reshape(P, k, n // (P * n_out), n_out, P).transpose(2, 0, 3, 1, 4)
    return a.reshape(n // (P * n_out), P, n_out * k * P)


def rows_first(w, k):
    a = by_partition(w)
    n = w.shape[1]
    return a.reshape(P, a.shape[1] // k, k, n).transpose(1, 0, 2, 3).reshape(-1, P, k * n)


def mix_stream(w_in, w_up, w_out, wq, wkv, wo):
    o_moba, o_dn = 256, 256 + 768
    o_ba = o_dn + 1536
    o_z = o_ba + 16
    o_gate = o_z + 512
    t = tiles(w_in[:, 0:256], 1)
    out = [t, rows_first(w_in[:, o_moba + 512:o_moba + 768], 4)]
    q, k = tiles(w_in[:, o_moba:o_moba + 256], 1), tiles(w_in[:, o_moba + 256:o_moba + 512], 1)
    out += [x[j:j + 1] for j in range(MOBA_PAIRS) for x in (q, k)]
    qkvz = [tiles(w_in[:, o:o + 512], 1) for o in (o_dn, o_dn + 512, o_dn + 1024, o_z)]
    out += [x[j:j + 1] for j in range(PAIRS) for x in qkvz]
    gates = [tiles(w_in[:, o_gate + b * D:o_gate + (b + 1) * D], 1) for b in range(3)]
    up = tiles(w_up, 1)
    out += [x[j:j + 1] for j in range(KT) for x in (*gates, up)]
    out += [tiles(w_out, 1), rows_first(wkv[:, 512:1024], 2)]
    q, k = tiles(wq, 1), tiles(wkv[:, 0:512], 1)
    out += [x[j:j + 1] for j in range(XH) for x in (q, k)]
    out += [tiles(wo, 2)]
    return out


def ffn_streams(w_gate_up, w_down, e):
    ff = w_gate_up.shape[1] // 2
    c = slice(e * FF, (e + 1) * FF)
    gate, up = tiles(w_gate_up[:, 0:ff][:, c], 1), tiles(w_gate_up[:, ff:][:, c], 1)
    return [x[j:j + 1] for j in range(FT) for x in (gate, up)], tiles(w_down[c], 1)


def kernel(**inputs):
    import concourse.bacc as bacc
    from concourse.bass_utils import run_bass_kernel_spmd

    a = {k: np.asarray(v) for k, v in inputs.items()}
    stream, down = [], []
    vec = np.zeros((DEPTH, P, NV), np.float32)
    small = np.zeros((DEPTH, P, 2 * P + KT * 16 + KT * NE), np.float32)
    for l in range(DEPTH):
        w_up = np.concatenate([a["w_up_pool"][l], a["w_up_moba"][l], a["w_up_dn"][l]], axis=0)
        stream += mix_stream(a["w_in"][l], w_up, a["w_out"][l], a["xa_wq"][l], a["xa_wkv"][l], a["xa_wo"][l])
        for e in range(NE if l % 2 else DENSE_PARTS):
            s, d = (ffn_streams(a["moe_w_gate_up"][l // 2, e], a["moe_w_down"][l // 2, e], 0) if l % 2
                    else ffn_streams(a["dense_w_gate_up"][l // 2], a["dense_w_down"][l // 2], e))
            stream += s
            down.append(d)
        for c, name in ((V_MIXG, "mix_norm_g"), (V_XAG, "xa_norm_g"), (V_MEMG, "mem_norm_g"), (V_FFNG, "ffn_norm_g")):
            vec[l, :, c:c + KT] = a[name][l].reshape(KT, P).T
        vec[l, :, V_FING:V_FING + KT] = a["final_norm_g"].reshape(KT, P).T
        vec[l, :, V_CONV:V_CONV + 48] = a["dn_conv_w"][l].reshape(4, 3, PAIRS, P).transpose(3, 2, 1, 0).reshape(P, 48)
        vec[l, :, V_POOLS:V_POOLS + 2] = a["pool_scale"][l].reshape(2, P).T
        vec[l, :, V_DNG] = np.concatenate([a["dn_norm_g"][l]] * 2)
        for c, name in ((V_ALOG, "dn_a_log"), (V_DTB, "dn_dt_bias")):
            vec[l, :, c:c + PAIRS] = np.repeat(a[name][l].reshape(PAIRS, 2).T, HD, axis=0)
        vec[l, :, V_DENSE] = 1 - l % 2
        for b in range(4):
            r = slice((b % 2) * HD, (b % 2 + 1) * HD)
            c = (b // 2) * P + (b % 2) * HD
            small[l, r, c:c + HD] = a["pool_w"][l, b]
        small[l, :, 2 * P:2 * P + KT * 16] = by_partition(a["w_in"][l][:, 2560:2576]).reshape(P, KT * 16)
        small[l, :, 2 * P + KT * 16:] = by_partition(a["moe_router"][0]).reshape(P, KT * NE)

    nc = bacc.Bacc("TRN2", target_bir_lowering=False, num_devices=1)
    arrays = {
        "x_t": by_partition(a["x"][0].T),
        "mem_t": by_partition(a["mem"][0].T),
        "pos": a["positions"].astype(np.int32),
        "cst": constants(),
        "vec": vec,
        "wsm": small,
        "wst": np.concatenate(stream, axis=0),
        "wdn": np.concatenate(down, axis=0),
    }
    arrays = {k: np.ascontiguousarray(v) for k, v in arrays.items()}
    args = [nc.dram_tensor(k, v.shape, mybir.dt.from_np(v.dtype), kind="ExternalInput").ap() for k, v in arrays.items()]
    out = nc.dram_tensor("out_t", (P, KT, SEQ), F32, kind="ExternalOutput").ap()
    program(nc, *args, out)
    r = run_bass_kernel_spmd(nc, [arrays], core_ids=[0])
    got = np.asarray(r.results[0]["out_t"])
    return np.ascontiguousarray(got.transpose(1, 0, 2).reshape(D, SEQ).T).reshape(1, SEQ, D)
```

```python
from contextlib import ExitStack

import numpy as np

import concourse.bass as bass
from concourse import mybir

F32 = mybir.dt.float32
F32R = mybir.dt.float32r
I32 = mybir.dt.int32
ALU = mybir.AluOpType
ACT = mybir.ActivationFunctionType
AX = mybir.AxisListType

P = 128
SEQ = 512
D = 1024
DEPTH = 2
MEM = 256
KT = D // P
TT = SEQ // P
RMS_EPS = 1e-6
POOL_WINDOWS = (2, 4, 8, 16)
HD = 64
PAIRS = 4
CH = 64
NC = SEQ // CH
MOBA_PAIRS = 2
XH = 4
FF = 1408
FT = FF // P
NE = 8
DENSE_PARTS = 2
CAP = 256
PASSES = SEQ // CAP
NQ = NE * PASSES
ST = CAP // P
UNIT = KT * P
PART_UNITS = 3 * FT + 1
HALF = UNIT // 2
MIX_UNITS = 2 + 2 + MOBA_PAIRS * 2 + PAIRS * 4 + KT * 4 + KT + 4 + XH * 2 + KT // 2
LEVELS = 6
ROPE_HALF = 8
ROPE_THETA = 500000.0
NEG = -1e30
MAGIC = 12582912.0

V_MIXG, V_XAG, V_MEMG, V_FFNG, V_FING = 0, 8, 16, 24, 32
V_CONV = 40
V_POOLS = 88
V_DNG = 90
V_ALOG = 91
V_DTB = 95
V_ROUTED = 99
V_PART = 100
V_NPART = V_PART + NE
NV = V_NPART + 1

C_ID, C_ONE, C_BONE, C_ROT, C_UB, C_VB = 0, 128, 256, 384, 512, 640
C_V64, C_U64, C_LOW, C_UPI, C_ID64, C_LV1 = 768, 832, 896, 960, 1024, 1088
C_LVT = 1152
C_CAUS = C_LVT + LEVELS * 64
C_CNT = C_CAUS + SEQ
C_FREQ = C_CNT + 2 * SEQ
C_RANK = C_FREQ + 1
C_EPS = C_RANK + NE
C_SU = C_EPS + 1
C_SLOT = C_SU + P
C_JPASS = C_SLOT + CAP
C_JPART = C_JPASS + NQ
C_JNUM = C_JPART + NQ
C_JLT = C_JNUM + NQ + 1
NCST = C_JLT + NQ * NQ


def constants():
    c = np.zeros((P, NCST), np.float32)
    p = np.arange(P)[:, None]
    j = np.arange(P)[None, :]
    same = (p // HD) == (j // HD)
    c[:, C_ID:C_ID + P] = p == j
    c[:, C_ONE:C_ONE + P] = 1
    c[:, C_BONE:C_BONE + P] = same
    jd = j % HD
    c[:, C_ROT:C_ROT + P] = (1.0 * ((p == j - ROPE_HALF) & (jd >= ROPE_HALF) & (jd < 2 * ROPE_HALF))
                             - 1.0 * ((p == j + ROPE_HALF) & (jd < ROPE_HALF)))
    c[:, C_UB:C_UB + P] = same & (p <= j)
    c[:, C_VB:C_VB + P] = same & (p > j)
    r = p % CH
    k = np.arange(CH)[None, :]
    c[:, C_V64:C_V64 + CH] = r > k
    c[:, C_U64:C_U64 + CH] = r <= k
    c[:, C_LOW:C_LOW + CH] = r > k
    c[:, C_UPI:C_UPI + CH] = k >= r
    c[:, C_ID64:C_ID64 + CH] = r == k
    for l in range(LEVELS):
        s = 1 << l
        low = (r // (2 * s) == k // (2 * s)) & (r % (2 * s) >= s) & (k % (2 * s) < s)
        up = (r // (2 * s) == k // (2 * s)) & (k % (2 * s) >= s) & (r % (2 * s) < s)
        if l == 0:
            c[:, C_LV1:C_LV1 + CH] = low
        c[:, C_LVT + l * CH:C_LVT + (l + 1) * CH] = up
    t = np.arange(SEQ)[None, :]
    c[:, C_CAUS:C_CAUS + SEQ] = np.where(t - (SEQ - P) <= p, 0.0, NEG)
    for b in range(2):
        w = np.where(p < HD, POOL_WINDOWS[2 * b], POOL_WINDOWS[2 * b + 1])
        c[:, C_CNT + b * SEQ:C_CNT + (b + 1) * SEQ] = 1.0 / np.minimum(t + 1, w)
    freq = np.power(np.float32(ROPE_THETA), -np.arange(ROPE_HALF, dtype=np.float32) * np.float32(2.0) / np.float32(16))
    d = np.arange(P) % HD
    c[:, C_FREQ] = np.where(d < 2 * ROPE_HALF, freq[d % ROPE_HALF], 0.0)
    c[:, C_RANK:C_RANK + NE] = NE - np.arange(NE)[None, :]
    c[:, C_EPS] = RMS_EPS
    c[:, C_SU:C_SU + P] = p < j
    c[:, C_SLOT:C_SLOT + CAP] = np.arange(CAP)
    q = np.arange(NQ)
    c[:, C_JPASS:C_JPASS + NQ] = (q % PASSES) * CAP
    c[:, C_JPART:C_JPART + NQ] = q // PASSES
    c[:, C_JNUM:C_JNUM + NQ + 1] = np.arange(NQ + 1)
    c[:, C_JLT:C_JLT + NQ * NQ] = (q[None, :] < q[:, None]).reshape(-1)
    return c


def program(nc, x_t, mem_t, pos, cst, vec, wsm, wst, out_t):
    ctx = ExitStack()
    with ctx:
        def sb(name, shape, dt=F32):
            return ctx.enter_context(nc.sbuf_tensor(name, shape, dt))

        def sem(name):
            return ctx.enter_context(nc.semaphore(name))

        X = sb("X", [P, KT, SEQ])
        h_hi = sb("h_hi", [P, KT, SEQ], F32R)
        h_lo = sb("h_lo", [P, KT, SEQ], F32R)
        C = sb("C", [P, NCST])
        vecs = sb("vecs", [P, NV])
        NSM = 2 * P + KT * 16 + KT * NE
        wsmall = sb("wsmall", [P, NSM])
        raw = sb("raw", [P, 2, UNIT])
        w_hi = sb("w_hi", [P, 2, UNIT], F32R)
        w_lo = sb("w_lo", [P, 2, UNIT], F32R)
        ropeC = sb("ropeC", [P, SEQ])
        ropeS = sb("ropeS", [P, SEQ])
        rinv = sb("rinv", [P, SEQ])
        jobs = sb("jobs", [P, NQ + 2], I32)
        tA = sb("tA", [P, SEQ])
        tB = sb("tB", [P, SEQ])
        tC = sb("tC", [P, SEQ])
        tD = sb("tD", [P, SEQ])
        tE = sb("tE", [P, SEQ])
        B_hi = sb("B_hi", [P, FT, SEQ], F32R)
        B_lo = sb("B_lo", [P, KT, SEQ], F32R)
        AR_COLS = 12900
        with ExitStack() as same:
            def first(name, shape, dt):
                return same.enter_context(nc.sbuf_tensor(name, shape, dt))
            M_hi = first("M_hi", [P, KT, SEQ], F32R)
            M_lo = first("M_lo", [P, KT, SEQ], F32R)
        with ExitStack() as same:
            N_hi = first("N_hi", [P, KT, MEM], F32R)
            N_lo = first("N_lo", [P, KT, MEM], F32R)
        with ExitStack() as same:
            Y_hi = first("Y_hi", [P, ST, D], F32R)
            Y_lo = first("Y_lo", [P, ST, D], F32R)
            Pm = first("Pm", [P, TT, CAP], F32R)
            PT = first("PT", [P, ST, SEQ], F32R)
        AR = sb("AR", [P, AR_COLS])
        at = [0]

        def arena(*shape):
            n = int(np.prod(shape))
            a = AR[:, at[0]:at[0] + n]
            at[0] += n
            assert at[0] <= AR_COLS, at[0]
            if len(shape) == 2:
                return a.rearrange("p (a b) -> p a b", a=shape[0])
            if len(shape) == 3:
                return a.rearrange("p (a b c) -> p a b c", a=shape[0], b=shape[1])
            return a

        ps = ctx.enter_context(nc.psum_tensor("ps", [P, 8, SEQ], F32))

        ident = C[:, C_ID:C_ID + P]
        id64 = C[:, C_ID64:C_ID64 + CH]

        at[0] = 0
        Vt = arena(TT, 256)
        vh = arena(TT, P)
        qT = arena(SEQ)
        kT = arena(SEQ)
        sc = arena(SEQ)
        pr = arena(SEQ)
        pT = arena(TT, P)
        stat = arena(4)
        at[0] = 0
        px = [arena(16 + SEQ) for _ in range(2)]
        pw = [arena(16 + SEQ) for _ in range(2)]
        at[0] = 0
        ba = arena(2, PAIRS, NC)
        spl = arena(3, PAIRS, NC)
        ealog = arena(PAIRS)
        tok = arena(6, PAIRS * NC)
        tk = [arena(6, NC) for _ in range(2)]
        cw = [arena(12) for _ in range(2)]
        St = [arena(CH) for _ in range(2)]
        vn = [arena(CH) for _ in range(2)]
        ost = [arena(NC) for _ in range(2)]
        baT = AR[:, at[0]:at[0] + SEQ]
        AT, MT, XX, XT, P1, EE, cv, sq1 = [], [], [], [], [], [], [], []
        for g in range(2):
            cv.append(AR[:, at[0]:at[0] + 3 * (4 + SEQ)].rearrange("p (a b) -> p a b", a=3))
            sq1.append(AR[:, at[0] + SEQ:at[0] + 2 * SEQ].rearrange("p (a b) -> p a b", a=NC))
            AT.append(arena(NC, CH))
            MT.append(arena(NC, CH))
            arena(CH)
            XX.append(arena(NC, CH))
            XT.append(arena(NC, CH))
            P1.append(arena(NC, CH))
            EE.append(arena(2, SEQ))

        def flat(t):
            return t.rearrange("p a b -> p (a b)")

        def chunked(t):
            return t.rearrange("p (a b) -> p a b", a=NC)

        E1 = [chunked(t[:, 0, :]) for t in EE]
        E2 = [chunked(t[:, 1, :]) for t in EE]
        A_, Uu, wT, oo = XX, AT, XX, P1
        Kt, Vv = [flat(t) for t in XT], [flat(t) for t in P1]
        Qt = [arena(SEQ) for _ in range(2)]
        aq = [arena(NC, CH) for _ in range(2)]
        kd = [arena(NC, CH), chunked(tE[:, :])]
        zz = [rinv[:, :], arena(SEQ)]
        vb = [chunked(tB[:, :]), chunked(tD[:, :])]
        kg = [chunked(tC[:, :]), chunked(tA[:, :])]
        sqs = [(tA[:, :], tE[:, :]), (flat(aq[0]), flat(kd[0]))]
        at[0] = 2 * ST * D + TT * CAP + ST * SEQ
        hF = arena(KT, SEQ)
        lg, oh1, oh2, tt1, mask = (arena(TT, NE) for _ in range(5))
        comb, rk = (arena(TT, NE + 1) for _ in range(2))
        m1, m2, m3 = (arena(TT) for _ in range(3))
        cnt = arena(NE)
        flag = arena(NQ)
        jpos = arena(NQ)
        jw = arena(NQ, NQ)
        jw2 = arena(NQ + 1, NQ)
        jpart = arena(NQ + 1)
        jbase = arena(NQ + 1)
        jn = arena(1)
        rj = arena(TT)
        cj = arena(TT)
        ws = arena(ST)
        gu, hid = tB[:, 0:CAP], tC[:, 0:CAP]
        at[0] = 2 * KT * MEM
        xv = arena(2, XH * P)
        xvh = arena(2, P)
        xq = arena(SEQ)
        xk = arena(MEM)
        xp = arena(MEM)
        xpT = arena(2, SEQ)
        xst = arena(4)
        memx = arena(KT, MEM)
        at[0] = 0
        final = arena(KT, SEQ)
        gts = [tB, tC, tD]

        load_x = sem("load_x")
        load_mem = sem("load_mem")
        load_pos = sem("load_pos")
        load_cst = sem("load_cst")
        load_vec = sem("load_vec")
        load_sm = sem("load_sm")
        raw_full = [sem(f"raw_full{s}") for s in range(2)]
        raw_full2 = [sem(f"raw_full2{s}") for s in range(2)]
        raw_free = [sem(f"raw_free{s}") for s in range(2)]
        raw_free2 = [sem(f"raw_free2{s}") for s in range(2)]
        hi_full = [sem(f"hi_full{s}") for s in range(2)]
        split_full = [sem(f"split_full{s}") for s in range(2)]
        split_free = [sem(f"split_free{s}") for s in range(2)]
        first_full = [sem(f"first_full{s}") for s in range(2)]
        half_free = [sem(f"half_free{s}") for s in range(2)]
        high_full = [sem(f"high_full{s}") for s in range(2)]
        pool_own = sem("pool_own")
        act_own = sem("act_own")
        dve_own = sem("dve_own")
        acc_free = [sem(f"acc_free{s}") for s in range(2)]
        to_act = sem("to_act")
        to_dve = sem("to_dve")
        act_pe = sem("act_pe")
        dve_pe = sem("dve_pe")
        act_dve = sem("act_dve")
        dve_act = sem("dve_act")
        dve_sp = sem("dve_sp")
        store_out = sem("store_out")
        dve_pool = sem("dve_pool")
        pool_dve = sem("pool_dve")
        act_pool = sem("act_pool")
        hidden_ready = sem("hidden_ready")

        H_hi = h_hi[:, :, :].rearrange("p (t a) s -> p t (a s)", a=2)
        H_lo = h_lo[:, :, :].rearrange("p (t a) s -> p t (a s)", a=2)
        hg, hh = B_lo, B_hi
        GB = (6, 7, 2, 3, 4, 5, 6, 7)
        SB = (6, 7, 0, 1, 2, 3, 4, 5)

        block = ctx.enter_context(nc.Block())

        @block.sync
        def _(sp):
            sp.dma_start(C[:, :], cst).then_inc(load_cst, 16)
            sp.dma_start(tA[:, :].bitcast(I32), pos.to_broadcast([P, SEQ])).then_inc(load_pos, 16)
            sp.dma_start(X[:, :, :], x_t).then_inc(load_x, 16)
            for s in range(2):
                u = wst[s:s + 1].rearrange("a p n -> (a p) n")
                sp.dma_start(raw[:, s, 0:HALF], u[:, 0:HALF]).then_inc(raw_full[s], 16)
                sp.dma_start(raw[:, s, HALF:UNIT], u[:, HALF:UNIT]).then_inc(raw_full2[s], 16)
            with sp.Fori(0, DEPTH) as lay:
                sp.wait_ge(dve_sp, 1).then_inc(dve_sp, -1)
                sp.dma_start(vecs[:, :], vec[bass.ds(lay, 1)].rearrange("a p n -> (a p) n")).then_inc(load_vec, 16)
                sp.dma_start(wsmall[:, :], wsm[bass.ds(lay, 1)].rearrange("a p n -> (a p) n")).then_inc(load_sm, 16)
                wbase = lay * (MIX_UNITS + DENSE_PARTS * PART_UNITS)

                def load_pair(at):
                    for s in range(2):
                        u = wst[bass.ds(at + s, 1)].rearrange("a p n -> (a p) n")
                        sp.wait_ge(raw_free[s], 1).then_inc(raw_free[s], -1)
                        sp.dma_start(raw[:, s, 0:HALF], u[:, 0:HALF]).then_inc(raw_full[s], 16)
                        sp.wait_ge(raw_free2[s], 1).then_inc(raw_free2[s], -1)
                        sp.dma_start(raw[:, s, HALF:UNIT], u[:, HALF:UNIT]).then_inc(raw_full2[s], 16)

                with sp.Fori(0, MIX_UNITS // 2 - 1) as i:
                    load_pair(wbase + 2 + i * 2)
                load_pair(wbase + MIX_UNITS)
                sp.wait_ge(dve_sp, 1).then_inc(dve_sp, -1)
                n_jobs = sp.value_load(jobs[0:1, NQ + 1:NQ + 2], min_val=1, max_val=NQ)
                with sp.Fori(0, n_jobs) as j:
                    e = sp.value_load(jobs[0:1, bass.ds(j, 1)], min_val=0, max_val=NE - 1)
                    with sp.Fori(0, PART_UNITS // 2 - 1) as i:
                        load_pair(wbase + MIX_UNITS + e * PART_UNITS + 2 + i * 2)
                    e1 = sp.value_load(jobs[0:1, bass.ds(j + 1, 1)], min_val=0, max_val=NE)
                    load_pair(wbase + MIX_UNITS + e1 * PART_UNITS)
            sp.wait_ge(dve_sp, 1).then_inc(dve_sp, -1)
            sp.wait_ge(dve_sp, 1).then_inc(dve_sp, -1)
            sp.dma_start(out_t, final).then_inc(store_out, 16)
            sp.wait_ge(store_out, 16)

        @block.gpsimd
        def _(pool):
            def rest(s, n):
                pool.wait_ge(hi_full[s], 1).then_inc(hi_full[s], -1)
                nc.gpsimd.tensor_tensor(w_lo[:, s, 0:n], raw[:, s, 0:n], w_hi[:, s, 0:n].bitcast(F32),
                                        ALU.subtract).then_inc(pool_own, 1)
                pool.wait_ge(pool_own, 1).then_inc(pool_own, -1)
                pool.sem_inc(raw_free[s], 1)
                pool.sem_inc(raw_free2[s], 1)
                pool.sem_inc(split_full[s], 1)

            for s in range(2):
                rest(s, UNIT)
            with pool.Fori(0, DEPTH):
                with pool.Fori(0, MIX_UNITS // 2):
                    for s in range(2):
                        rest(s, UNIT)
                pool.wait_ge(dve_pool, 1).then_inc(dve_pool, -1)
                n_jobs = pool.value_load(jobs[0:1, NQ + 1:NQ + 2], min_val=1, max_val=NQ)
                with pool.Fori(0, n_jobs):
                    pool.sem_inc(pool_dve, 1)
                    with pool.Fori(0, FT) as i:
                        pool.wait_ge(act_pool, 1).then_inc(act_pool, -1)
                        t = hh[:, bass.ds(i, 1), :].rearrange("p a n -> p (a n)")
                        nc.gpsimd.tensor_tensor(t[:, CAP:2 * CAP], hid, t[:, 0:CAP].bitcast(F32),
                                                ALU.subtract).then_inc(pool_own, 1)
                        pool.wait_ge(pool_own, 1).then_inc(pool_own, -1)
                        pool.sem_inc(pool_dve, 1)

        @block.tensor
        def _(pe):
            mm = nc.tensor.matmul

            def prod3(acc, whi, wlo, xhi, xlo, start, stop):
                mm(acc, wlo, xhi, start=start, stop=False)
                mm(acc, whi, xlo, start=False, stop=False)
                return mm(acc, whi, xhi, start=False, stop=stop)

            def unit(s, hi, lo, n=SEQ, nk=KT):
                pe.wait_ge(split_full[s], 1).then_inc(split_full[s], -1)
                pe.wait_ge(acc_free[s], 1).then_inc(acc_free[s], -1)
                for k in range(nk):
                    last = prod3(ps[:, s, 0:n], w_hi[:, s, k * P:(k + 1) * P], w_lo[:, s, k * P:(k + 1) * P],
                                 hi[:, k, 0:n], lo[:, k, 0:n], k == 0, k == nk - 1)
                return last

            def narrow(s):
                pe.wait_ge(first_full[s], 1).then_inc(first_full[s], -1)
                pe.wait_ge(acc_free[s], 1).then_inc(acc_free[s], -1)
                for k in range(KT):
                    if k == KT // 2:
                        pe.wait_ge(split_full[s], 1).then_inc(split_full[s], -1)
                    last = prod3(ps[:, s, 0:CAP], w_hi[:, s, k * P:(k + 1) * P], w_lo[:, s, k * P:(k + 1) * P],
                                 hg[:, k, 0:CAP], hg[:, k, CAP:2 * CAP], k == 0, k == KT - 1)
                    if k == KT // 2 - 1:
                        last.then_inc(half_free[s], 1)
                return last

            def gather():
                for f in range(KT):
                    if f == 6:
                        pe.wait_ge(act_pe, 1).then_inc(act_pe, -1)
                    if f == 7:
                        pe.wait_ge(dve_pe, 1).then_inc(dve_pe, -1)
                    for h, part in enumerate((H_hi, H_lo)):
                        for t in range(TT):
                            last = mm(ps[:, GB[f], h * CAP:(h + 1) * CAP], part[:, t, f * P:(f + 1) * P], Pm[:, t, :],
                                      start=(t == 0), stop=(t == TT - 1))
                    last.then_inc(to_dve if f % 2 else to_act, 1)
                for _ in range(2):
                    pe.wait_ge(act_pe, 1).then_inc(act_pe, -1)
                    pe.wait_ge(dve_pe, 1).then_inc(dve_pe, -1)

            def slots():
                for st in range(ST):
                    for t in range(TT):
                        last = nc.tensor.transpose(ps[:, 6 + st, t * P:(t + 1) * P],
                                                   Pm[:, t, st * P:(st + 1) * P].bitcast(F32), ident)
                    last.then_inc(to_act, 1)
                for st in range(ST):
                    pe.wait_ge(act_pe, 1).then_inc(act_pe, -1)
                for st in range(ST):
                    for t in range(TT):
                        last = mm(ps[:, 6, st:st + 1], Pm[:, t, st * P:(st + 1) * P].bitcast(F32), cj[:, t:t + 1],
                                  start=(t == 0), stop=(t == TT - 1))
                last.then_inc(to_dve, 1)

            def sumsq(n=SEQ):
                for k in range(KT):
                    pe.wait_ge(act_pe, 1).then_inc(act_pe, -1)
                    mm(ps[:, 2, 0:n], C[:, C_ONE:C_ONE + P], (tA, tE)[k % 2][:, 0:n],
                       start=(k == 0), stop=(k == KT - 1)).then_inc(to_act, 1)

            def both(o, a, b, n):
                for h in range(2):
                    q = slice(h * HD, (h + 1) * HD)
                    last = mm(o(q), a(q), b(q), start=True, stop=True)
                return last

            def cs(n):
                return slice(n * CH, (n + 1) * CH)

            pe.wait_ge(load_cst, 16)
            for s in range(2):
                pe.sem_inc(acc_free[s], 1)
            with pe.Fori(0, DEPTH) as lay:
                pe.wait_ge(load_sm, 16).then_inc(load_sm, -16)
                sumsq()
                pe.wait_ge(dve_pe, 1).then_inc(dve_pe, -1)
                for s in range(2):
                    unit(s, h_hi, h_lo).then_inc(to_dve, 1)
                for b in range(2):
                    pe.wait_ge(dve_pe, 1).then_inc(dve_pe, -1)
                    mm(ps[:, 2 + b, :], wsmall[:, b * P:(b + 1) * P], (tB, tC)[b][:, :],
                       start=True, stop=True).then_inc(to_dve, 1)
                for s in range(2):
                    pe.wait_ge(split_full[s], 1).then_inc(split_full[s], -1)
                    if s == 0:
                        pe.wait_ge(dve_pe, 1).then_inc(dve_pe, -1)
                    for t in range(TT):
                        for k in range(4):
                            last = prod3(ps[:, 2 + t, 0:256], h_hi[:, 4 * s + k, t * P:(t + 1) * P],
                                         h_lo[:, 4 * s + k, t * P:(t + 1) * P],
                                         w_hi[:, s, k * 256:(k + 1) * 256], w_lo[:, s, k * 256:(k + 1) * 256],
                                         s == 0 and k == 0, s == 1 and k == 3)
                    last.then_inc(to_act, 1)
                pe.wait_ge(act_pe, 1).then_inc(act_pe, -1)
                with pe.Fori(0, MOBA_PAIRS):
                    for s in range(2):
                        unit(s, h_hi, h_lo).then_inc(to_dve, 1)
                    for s in range(2):
                        pe.wait_ge(dve_pe, 1).then_inc(dve_pe, -1)
                        mm(ps[:, 2 + s, :], C[:, C_ROT:C_ROT + P], (qT, kT)[s], start=True, stop=True).then_inc(to_dve, 1)
                    pe.wait_ge(dve_pe, 1).then_inc(dve_pe, -1)
                    for h in range(2):
                        q = slice(h * HD, (h + 1) * HD)
                        for t in range(TT):
                            nk = t + 1
                            mm(ps[:, 3, 0:nk * P], qT[q, t * P:(t + 1) * P], kT[q, 0:nk * P],
                               start=True, stop=True).then_inc(to_dve, 1)
                            pe.wait_ge(dve_pe, 1).then_inc(dve_pe, -1)
                            for k in range(nk):
                                last = nc.tensor.transpose(ps[:, 4, k * P:(k + 1) * P], pr[:, k * P:(k + 1) * P], ident)
                            last.then_inc(to_act, 1)
                            pe.wait_ge(act_pe, 1).then_inc(act_pe, -1)
                            for k in range(nk):
                                last = mm(ps[q, 5, t * P:(t + 1) * P], vh[:, k, q], pT[:, k, :],
                                          start=(k == 0), stop=(k == nk - 1))
                    last.then_inc(to_dve, 1)
                    pe.wait_ge(dve_pe, 1).then_inc(dve_pe, -1)
                for k in range(KT):
                    w = wsmall[:, 2 * P + k * 16:2 * P + (k + 1) * 16]
                    for part in (h_lo, h_hi):
                        last = mm(ps[0:16, 2, :], w, part[:, k, :].bitcast(F32),
                                  start=(k == 0 and part is h_lo), stop=(k == KT - 1 and part is h_hi))
                last.then_inc(to_act, 1)
                pe.wait_ge(act_pe, 1).then_inc(act_pe, -1)
                for n in range(NC):
                    for h in range(2):
                        last = mm(ps[h * CH:(h + 1) * CH, 3, n * 16:(n + 1) * 16], baT[0:16, cs(n)], ident[0:16, 0:16],
                                  start=True, stop=True)
                last.then_inc(to_dve, 1)
                pe.wait_ge(dve_pe, 1).then_inc(dve_pe, -1)
                mm(ps[:, 2, 0:32], C[:, C_UB:C_UB + P], tok[:, 0, :], start=True, stop=True)
                mm(ps[:, 2, 64:96], C[:, C_VB:C_VB + P], tok[:, 0, :], start=True, stop=True)
                mm(ps[:, 2, 128:160], C[:, C_BONE:C_BONE + P], tok[:, 0, :], start=True, stop=True).then_inc(to_act, 1)
                pe.wait_ge(act_pe, 1).then_inc(act_pe, -1)
                with pe.Fori(0, PAIRS // 2):
                    for g in range(2):
                        b = 2 + 3 * g
                        pe.wait_ge(dve_pe, 1).then_inc(dve_pe, -1)
                        mm(ps[:, b, :], C[:, C_UB:C_UB + P], flat(E1[g]), start=True, stop=True)
                        mm(ps[:, b + 1, :], C[:, C_VB:C_VB + P], flat(E2[g]), start=True, stop=True).then_inc(to_act, 1)
                    for g in range(2):
                        for u in range(4):
                            unit(u % 2, h_hi, h_lo).then_inc(to_dve if u < 3 else to_act, 1)
                    for g in range(2):
                        for u in range(2):
                            pe.wait_ge(act_pe, 1).then_inc(act_pe, -1)
                            mm(ps[:, 2 + 3 * g + u, :], C[:, C_BONE:C_BONE + P], sqs[g][u], start=True, stop=True).then_inc(to_act, 1)
                        pe.wait_ge(act_pe, 1).then_inc(act_pe, -1)
                    for g in range(2):
                        pe.wait_ge(acc_free[g], 1).then_inc(acc_free[g], -1)
                        for n in range(NC):
                            last = both(lambda q: ps[q, g, cs(n)], lambda q: Vv[g][q, cs(n)], lambda q: id64[q, :], CH)
                        last.then_inc(to_dve, 1)
                    for g in range(2):
                        b = 2 + 3 * g
                        pe.wait_ge(dve_pe, 1).then_inc(dve_pe, -1)
                        for n in range(NC):
                            both(lambda q: ps[q, b, cs(n)], lambda q: Kt[g][q, cs(n)], lambda q: Kt[g][q, cs(n)], CH)
                            both(lambda q: ps[q, b + 1, cs(n)], lambda q: Kt[g][q, cs(n)], lambda q: Qt[g][q, cs(n)], CH)
                            last = both(lambda q: ps[q, b + 2, cs(n)], lambda q: Kt[g][q, cs(n)], lambda q: id64[q, :], CH)
                        last.then_inc(to_dve, 1)
                    for g in range(2):
                        pe.wait_ge(dve_pe, 1).then_inc(dve_pe, -1)
                        for n in range(NC):
                            last = both(lambda q: ps[q, 2 + 3 * g, cs(n)], lambda q: A_[g][q, n, :], lambda q: id64[q, :], CH)
                        last.then_inc(to_dve, 1)
                    for l in range(1, LEVELS):
                        for g in range(2):
                            pe.wait_ge(dve_pe, 1).then_inc(dve_pe, -1)
                            for n in range(NC):
                                last = both(lambda q: ps[q, 2 + 3 * g, cs(n)], lambda q: MT[g][q, n, :],
                                            lambda q: XX[g][q, n, :], CH)
                            last.then_inc(to_act, 1)
                        for g in range(2):
                            pe.wait_ge(act_pe, 1).then_inc(act_pe, -1)
                            if l < LEVELS - 1:
                                for n in range(NC):
                                    last = both(lambda q: ps[q, 3 + 3 * g, cs(n)], lambda q: XT[g][q, n, :],
                                                lambda q: P1[g][q, n, :], CH)
                                last.then_inc(to_dve, 1)
                            for n in range(NC):
                                last = both(lambda q: ps[q, 4 + 3 * g, cs(n)], lambda q: P1[g][q, n, :],
                                            lambda q: XT[g][q, n, :], CH)
                            last.then_inc(to_dve, 1)
                    for g in range(2):
                        pe.wait_ge(dve_pe, 1).then_inc(dve_pe, -1)
                        for n in range(NC):
                            both(lambda q: ps[q, 2 + 3 * g, cs(n)], lambda q: XT[g][q, n, :], lambda q: vb[g][q, n, :], CH)
                            last = both(lambda q: ps[q, 3 + 3 * g, cs(n)], lambda q: kg[g][q, n, :], lambda q: XT[g][q, n, :], CH)
                        last.then_inc(to_act, 1)
                    for n in range(NC):
                        for g in range(2):
                            b = 2 + 3 * g
                            if n == 0:
                                pe.wait_ge(act_pe, 1).then_inc(act_pe, -1)
                            else:
                                pe.wait_ge(dve_pe, 1).then_inc(dve_pe, -1)
                            both(lambda q: ps[q, b, 0:CH], lambda q: wT[g][q, n, :], lambda q: St[g][q, :], CH).then_inc(to_dve, 1)
                            both(lambda q: ps[q, b + 1, 0:CH], lambda q: Qt[g][q, cs(n)], lambda q: St[g][q, :], CH).then_inc(to_dve, 1)
                        for g in range(2):
                            b = 2 + 3 * g
                            pe.wait_ge(dve_pe, 1).then_inc(dve_pe, -1)
                            both(lambda q: ps[q, b + 2, 0:CH], lambda q: kd[g][q, n, :], lambda q: vn[g][q, :], CH).then_inc(to_dve, 1)
                            both(lambda q: ps[q, b, 0:CH], lambda q: aq[g][q, n, :], lambda q: vn[g][q, :], CH).then_inc(to_dve, 1)
                    for g in range(2):
                        pe.wait_ge(dve_pe, 1).then_inc(dve_pe, -1)
                    for g in range(2):
                        pe.wait_ge(dve_pe, 1).then_inc(dve_pe, -1)
                        for n in range(NC):
                            last = both(lambda q: ps[q, 2 + 3 * g, cs(n)], lambda q: oo[g][q, n, :], lambda q: id64[q, :], CH)
                        last.then_inc(to_dve, 1)
                    for g in range(2):
                        pe.wait_ge(dve_pe, 1).then_inc(dve_pe, -1)
                with pe.Fori(0, KT):
                    for s in (0, 1, 0):
                        unit(s, h_hi, h_lo).then_inc(to_act, 1)
                    pe.wait_ge(split_full[1], 1).then_inc(split_full[1], -1)
                    pe.wait_ge(dve_pe, 1).then_inc(dve_pe, -1)
                    for br, (k0, k1) in enumerate(((0, 2), (2, 4), (4, 8))):
                        for k in range(k0, k1):
                            last = prod3(ps[:, 2 + br, :], w_hi[:, 1, k * P:(k + 1) * P], w_lo[:, 1, k * P:(k + 1) * P],
                                         B_hi[:, k, :], B_lo[:, k, :], k == k0, k == k1 - 1)
                    last.then_inc(to_dve, 1)
                pe.wait_ge(dve_pe, 1).then_inc(dve_pe, -1)
                with pe.Fori(0, KT // 2):
                    for s in range(2):
                        unit(s, M_hi, M_lo).then_inc(to_dve, 1)
                sumsq()
                pe.wait_ge(dve_pe, 1).then_inc(dve_pe, -1)
                sumsq(MEM)
                pe.wait_ge(dve_pe, 1).then_inc(dve_pe, -1)
                for u in range(4):
                    s = u % 2
                    pe.wait_ge(split_full[s], 1).then_inc(split_full[s], -1)
                    for t in range(2):
                        for k in range(2):
                            last = prod3(ps[:, 4 + t, :], N_hi[:, 2 * u + k, t * P:(t + 1) * P],
                                         N_lo[:, 2 * u + k, t * P:(t + 1) * P],
                                         w_hi[:, s, k * SEQ:(k + 1) * SEQ], w_lo[:, s, k * SEQ:(k + 1) * SEQ],
                                         u == 0 and k == 0, u == 3 and k == 1)
                    last.then_inc(to_act, 1)
                pe.wait_ge(act_pe, 1).then_inc(act_pe, -1)
                with pe.Fori(0, XH):
                    unit(0, h_hi, h_lo).then_inc(to_dve, 1)
                    unit(1, N_hi, N_lo, MEM).then_inc(to_dve, 1)
                    pe.wait_ge(dve_pe, 1).then_inc(dve_pe, -1)
                    for t in range(TT):
                        mm(ps[:, 3, 0:MEM], xq[:, t * P:(t + 1) * P], xk, start=True, stop=True).then_inc(to_dve, 1)
                        pe.wait_ge(dve_pe, 1).then_inc(dve_pe, -1)
                        for k in range(2):
                            last = nc.tensor.transpose(ps[:, 4, k * P:(k + 1) * P], xp[:, k * P:(k + 1) * P], ident)
                        last.then_inc(to_act, 1)
                        pe.wait_ge(act_pe, 1).then_inc(act_pe, -1)
                    for k in range(2):
                        last = mm(ps[:, 5, :], xvh[:, k, :], xpT[:, k, :], start=(k == 0), stop=(k == 1))
                    last.then_inc(to_dve, 1)
                    pe.wait_ge(dve_pe, 1).then_inc(dve_pe, -1)
                with pe.Fori(0, KT // 4):
                    for s in range(2):
                        pe.wait_ge(split_full[s], 1).then_inc(split_full[s], -1)
                        pe.wait_ge(acc_free[s], 1).then_inc(acc_free[s], -1)
                        for j in range(2):
                            for k in range(4):
                                c = (j * 4 + k) * P
                                last = prod3(ps[:, (s, 2 + s)[j], :], w_hi[:, s, c:c + P], w_lo[:, s, c:c + P],
                                             B_hi[:, k, :], B_lo[:, k, :], k == 0, k == 3)
                        last.then_inc(to_dve, 1)
                sumsq()
                pe.wait_ge(dve_pe, 1).then_inc(dve_pe, -1)
                for i in range(2 * TT):
                    t, b = i // 2, 2 + i % 2
                    if i >= 2:
                        pe.wait_ge(dve_pe, 1).then_inc(dve_pe, -1)
                    for a in range(4):
                        last = nc.tensor.transpose(ps[:, b, a * P:(a + 1) * P],
                                                   hF[:, (i % 2) * 4 + a, t * P:(t + 1) * P], ident)
                    last.then_inc(to_dve, 1)
                for t in range(TT):
                    for k in range(KT):
                        c = 2 * P + KT * 16 + k * NE
                        last = mm(ps[:, 4 + t, 0:NE], hF[:, k, t * P:(t + 1) * P], wsmall[:, c:c + NE],
                                  start=(k == 0), stop=(k == KT - 1))
                last.then_inc(to_dve, 1)
                for _ in range(3):
                    pe.wait_ge(dve_pe, 1).then_inc(dve_pe, -1)
                for t in range(TT):
                    for u in range(t + 1):
                        mm(ps[:, 4, t * NE:(t + 1) * NE], C[:, C_SU:C_SU + P] if u == t else C[:, C_ONE:C_ONE + P],
                           mask[:, u, :], start=(u == 0), stop=(u == t))
                for u in range(TT):
                    last = mm(ps[:, 4, TT * NE:(TT + 1) * NE], C[:, C_ONE:C_ONE + P], mask[:, u, :],
                              start=(u == 0), stop=(u == TT - 1))
                last.then_inc(to_dve, 1)
                pe.wait_ge(dve_pe, 1).then_inc(dve_pe, -1)
                n_jobs = pe.value_load(jobs[0:1, NQ + 1:NQ + 2], min_val=1, max_val=NQ)
                for s in range(2):
                    pe.wait_ge(split_full[s], 1).then_inc(split_full[s], -1)
                    pe.sem_inc(first_full[s], 1)
                    pe.sem_inc(split_full[s], 1)
                pe.wait_ge(dve_pe, 1).then_inc(dve_pe, -1)
                gather()
                pe.wait_ge(act_pe, 1).then_inc(act_pe, -1)
                pe.wait_ge(dve_pe, 1).then_inc(dve_pe, -1)
                slots()
                with pe.Fori(0, n_jobs):
                    with pe.Fori(0, FT):
                        narrow(0).then_inc(to_act, 1)
                        narrow(1).then_inc(to_dve, 1)
                    pe.wait_ge(dve_pe, 1).then_inc(dve_pe, -1)
                    gather()
                    pe.wait_ge(hidden_ready, 1).then_inc(hidden_ready, -1)
                    for f in range(FT):
                        s = f % 2
                        for half in range(2):
                            pe.wait_ge(split_full[s] if half else first_full[s], 1).then_inc(split_full[s] if half else first_full[s], -1)
                            for st in range(ST):
                                c = slice(half * HALF, (half + 1) * HALF)
                                last = prod3(ps[:, 2 + 2 * st + half, :], hh[:, f, st * P:(st + 1) * P],
                                             hh[:, f, CAP + st * P:CAP + (st + 1) * P], w_hi[:, s, c], w_lo[:, s, c],
                                             f == 0, f == FT - 1)
                                if f == FT - 1:
                                    last.then_inc(to_act, 1)
                            if f < FT - 1:
                                last.then_inc(split_free[s] if half else half_free[s], 1)
                    pe.wait_ge(first_full[1], 1).then_inc(first_full[1], -1)
                    pe.wait_ge(split_full[1], 1).then_inc(split_full[1], -1)
                    pe.sem_inc(half_free[1], 1)
                    pe.sem_inc(split_free[1], 1)
                    pe.wait_ge(acc_free[0], 1).then_inc(acc_free[0], -1)
                    pe.wait_ge(acc_free[1], 1).then_inc(acc_free[1], -1)
                    pe.wait_ge(act_pe, 1).then_inc(act_pe, -1)
                    pe.wait_ge(dve_pe, 1).then_inc(dve_pe, -1)
                    for f in range(KT):
                        if f % 4 == 0:
                            for st in range(ST):
                                pe.wait_ge(dve_pe, 1).then_inc(dve_pe, -1)
                        for part in (Y_lo, Y_hi):
                            for st in range(ST):
                                last = mm(ps[:, SB[f], :], part[:, st, f * P:(f + 1) * P], PT[:, st, :],
                                          start=(part is Y_lo and st == 0), stop=(part is Y_hi and st == ST - 1))
                        last.then_inc(to_dve, 1)
                    pe.wait_ge(dve_pe, 1).then_inc(dve_pe, -1)
                    slots()
                    pe.wait_ge(dve_pe, 1).then_inc(dve_pe, -1)
                for s in range(2):
                    pe.wait_ge(first_full[s], 1).then_inc(first_full[s], -1)
            sumsq()

        @block.scalar
        def _(act):
            def fn(out, in_, f, *posts, **kw):
                nc.scalar.activation(out, in_, f, **kw).then_inc(act_own, 1)
                act.wait_ge(act_own, 1).then_inc(act_own, -1)
                for p in posts:
                    act.sem_inc(p, 1)

            def rsqrt(out, in_, scale, *posts):
                fn(out, in_, ACT.Ln, scale=scale, bias=C[0:out.shape[0], C_EPS:C_EPS + 1])
                fn(out, out, ACT.Exp, *posts, scale=-0.5)

            def norm(src, n=SEQ):
                act.preload_act_table_set("natural_log_exp_and_others")
                for k in range(KT):
                    if k >= 2:
                        act.wait_ge(to_act, 1).then_inc(to_act, -1)
                    fn((tA, tE)[k % 2][:, 0:n], src[:, k, 0:n], ACT.Square, act_pe)
                for _ in range(2):
                    act.wait_ge(to_act, 1).then_inc(to_act, -1)
                rsqrt(rinv[:, 0:n], ps[:, 2, 0:n], 1.0 / D, act_dve)

            def high(s, n=UNIT):
                act.wait_ge(raw_full[s], 16).then_inc(raw_full[s], -16)
                act.wait_ge(raw_full2[s], 16).then_inc(raw_full2[s], -16)
                act.wait_ge(split_free[s], 1).then_inc(split_free[s], -1)
                nc.scalar.activation(w_hi[:, s, 0:n], raw[:, s, 0:n], ACT.Copy).then_inc(hi_full[s], 1)

            def high1(s):
                act.wait_ge(raw_full[s], 16).then_inc(raw_full[s], -16)
                act.wait_ge(half_free[s], 1).then_inc(half_free[s], -1)
                nc.scalar.activation(w_hi[:, s, 0:HALF], raw[:, s, 0:HALF], ACT.Copy).then_inc(high_full[s], 1)

            def high2(s):
                act.wait_ge(raw_full2[s], 16).then_inc(raw_full2[s], -16)
                act.wait_ge(split_free[s], 1).then_inc(split_free[s], -1)
                nc.scalar.activation(w_hi[:, s, HALF:UNIT], raw[:, s, HALF:UNIT], ACT.Copy).then_inc(high_full[s], 1)

            def gathered():
                for f in range(0, KT, 2):
                    act.wait_ge(to_act, 1).then_inc(to_act, -1)
                    fn(hg[:, f, :], ps[:, GB[f], :], ACT.Copy, act_pe)

            def slots():
                for st in range(ST):
                    act.wait_ge(to_act, 1).then_inc(to_act, -1)
                    fn(PT[:, st, :], ps[:, 6 + st, :], ACT.Copy, act_pe)

            for s in range(2):
                act.sem_inc(split_free[s], 1)
            act.wait_ge(load_cst, 16)
            for s in range(2):
                high(s)
            act.wait_ge(load_x, 16)
            for t in (ropeC, ropeS):
                act.wait_ge(dve_act, 1).then_inc(dve_act, -1)
                fn(t[:, :], t[:, :], ACT.Sin, act_dve)
            with act.Fori(0, DEPTH) as lay:
                act.wait_ge(dve_act, 1).then_inc(dve_act, -1)
                norm(X)
                for s in range(2):
                    high(s)
                for s in range(2):
                    act.wait_ge(to_act, 1).then_inc(to_act, -1)
                    act.sem_inc(split_free[s], 1)
                    if s == 1:
                        fn(Vt, ps[:, 2:6, 0:256], ACT.Copy, act_pe)
                    high(s)
                with act.Fori(0, MOBA_PAIRS):
                    for s in range(2):
                        high(s)
                    for h in range(2):
                        for t in range(TT):
                            nk = t + 1
                            act.wait_ge(dve_act, 1).then_inc(dve_act, -1)
                            fn(pr[:, 0:nk * P], sc[:, 0:nk * P], ACT.Exp, act_dve, bias=stat[:, 0:1], accum_out=stat[:, 1:2])
                            act.wait_ge(to_act, 1).then_inc(to_act, -1)
                            fn(pT[:, 0:nk, :].rearrange("p a b -> p (a b)"), ps[:, 4, 0:nk * P], ACT.Copy, act_pe)
                act.wait_ge(to_act, 1).then_inc(to_act, -1)
                fn(baT[0:16, :], ps[0:16, 2, :], ACT.Copy, act_pe)
                act.wait_ge(dve_act, 1).then_inc(dve_act, -1)
                fn(spl[:, 0], spl[:, 0], ACT.Exp)
                fn(spl[:, 0], spl[:, 0], ACT.Ln, bias=C[:, C_ONE:C_ONE + 1])
                fn(ealog, vecs[:, V_ALOG:V_ALOG + PAIRS], ACT.Exp)
                fn(spl[:, 1], ba[:, 0], ACT.Exp, act_dve, scale=-1.0)
                act.wait_ge(to_act, 1).then_inc(to_act, -1)
                fn(tok[:, 3, :], ps[:, 2, 0:32], ACT.Exp)
                fn(tok[:, 4, :], ps[:, 2, 64:96], ACT.Exp)
                fn(tok[:, 5, :], ps[:, 2, 128:160], ACT.Exp, act_pe, act_dve)
                with act.Fori(0, PAIRS // 2):
                    act.preload_act_table_set("natural_log_exp_and_others")
                    for g in range(2):
                        act.wait_ge(to_act, 1).then_inc(to_act, -1)
                        fn(flat(E1[g]), ps[:, 2 + 3 * g, :], ACT.Exp)
                        fn(flat(E2[g]), ps[:, 3 + 3 * g, :], ACT.Exp, act_dve)
                    act.preload_act_table(ACT.Silu)
                    for g in range(2):
                        for u in range(3):
                            high(u % 2)
                            act.wait_ge(dve_act, 1).then_inc(dve_act, -1)
                            y = (Qt[g], Kt[g], Vv[g])[u]
                            fn(y, (tB, tC, tD)[u][:, :], ACT.Silu, *((act_dve,) if g == 0 else ()), *((act_pe,) if u == 2 else ()))
                            if u < 2:
                                fn(sqs[g][u], y, ACT.Square, act_pe)
                        act.wait_ge(to_act, 1).then_inc(to_act, -1)
                        act.sem_inc(split_free[1], 1)
                        fn(zz[g], ps[:, 1, :], ACT.Silu, acc_free[1])
                        high(1)
                    act.preload_act_table_set("natural_log_exp_and_others")
                    for g in range(2):
                        for u in range(2):
                            act.wait_ge(to_act, 1).then_inc(to_act, -1)
                            rsqrt(sqs[g][u], ps[:, 2 + 3 * g + u, :], 1.0, act_dve)
                    for l in range(1, LEVELS):
                        for g in range(2):
                            act.wait_ge(to_act, 1).then_inc(to_act, -1)
                            fn(flat(P1[g]), ps[:, 2 + 3 * g, :], ACT.Copy, act_pe)
                    for g in range(2):
                        act.wait_ge(to_act, 1).then_inc(to_act, -1)
                        fn(flat(Uu[g]), ps[:, 2 + 3 * g, :], ACT.Copy)
                        fn(flat(wT[g]), ps[:, 3 + 3 * g, :], ACT.Copy, act_pe)
                    for g in range(2):
                        act.wait_ge(dve_act, 1).then_inc(dve_act, -1)
                        rsqrt(ost[g], ost[g], 1.0 / HD, act_dve)
                act.preload_act_table(ACT.Sigmoid)
                with act.Fori(0, KT):
                    act.wait_ge(dve_act, 1).then_inc(dve_act, -1)
                    for b, s in enumerate((0, 1, 0)):
                        act.wait_ge(to_act, 1).then_inc(to_act, -1)
                        act.sem_inc(split_free[s], 1)
                        fn(gts[b][:, :], ps[:, s, :], ACT.Sigmoid, acc_free[s], act_dve)
                        high(s)
                    high(1)
                with act.Fori(0, KT // 2):
                    for s in range(2):
                        high(s)
                act.wait_ge(dve_act, 1).then_inc(dve_act, -1)
                act.wait_ge(dve_act, 1).then_inc(dve_act, -1)
                act.dma_start(memx, mem_t).then_inc(load_mem, 16)
                norm(X)
                act.wait_ge(load_mem, 16).then_inc(load_mem, -16)
                norm(memx, MEM)
                for u in range(4):
                    act.wait_ge(to_act, 1).then_inc(to_act, -1)
                    act.sem_inc(split_free[u % 2], 1)
                    if u == 3:
                        fn(xv, ps[:, 4:6, :], ACT.Copy, act_pe)
                    high(u % 2)
                with act.Fori(0, XH):
                    for s in range(2):
                        high(s)
                    for t in range(TT):
                        act.wait_ge(dve_act, 1).then_inc(dve_act, -1)
                        fn(xp, ps[:, 3, 0:MEM], ACT.Exp, act_dve, bias=xst[:, 0:1], scale=float(P) ** -0.5,
                           accum_out=xst[:, 1:2])
                        act.wait_ge(to_act, 1).then_inc(to_act, -1)
                        fn(xpT[:, :, t * P:(t + 1) * P], ps[:, 4, 0:MEM].rearrange("p (a b) -> p a b", a=2), ACT.Copy, act_pe)
                with act.Fori(0, KT // 4):
                    for s in range(2):
                        high(s)
                act.wait_ge(dve_act, 1).then_inc(dve_act, -1)
                norm(X)
                act.wait_ge(dve_act, 1).then_inc(dve_act, -1)
                fn(m3, m3, ACT.Exp, act_dve)
                act.preload_act_table(ACT.Silu)
                act.wait_ge(dve_act, 1).then_inc(dve_act, -1)
                n_jobs = act.value_load(jobs[0:1, NQ + 1:NQ + 2], min_val=1, max_val=NQ)
                gathered()
                slots()
                with act.Fori(0, n_jobs):
                    with act.Fori(0, FT) as i:
                        high1(0)
                        act.wait_ge(to_act, 1).then_inc(to_act, -1)
                        act.sem_inc(split_free[0], 1)
                        fn(gu, ps[:, 0, 0:CAP], ACT.Silu, acc_free[0], act_dve)
                        high2(0)
                        high1(1)
                        high2(1)
                        act.wait_ge(dve_act, 1).then_inc(dve_act, -1)
                        fn(hh[:, bass.ds(i, 1), 0:CAP].rearrange("p a n -> p (a n)"), hid, ACT.Copy, act_pool)
                    gathered()
                    with act.Fori(0, FT // 2):
                        for s in range(2):
                            high1(s)
                            high2(s)
                    for half in range(2):
                        for st in range(ST):
                            act.wait_ge(to_act, 1).then_inc(to_act, -1)
                            if st == ST - 1:
                                act.sem_inc(split_free[0] if half else half_free[0], 1)
                            fn(Y_hi[:, st, half * SEQ:(half + 1) * SEQ], ps[:, 2 + 2 * st + half, :], ACT.Copy,
                               act_dve, scale=ws[:, st:st + 1])
                    for s in range(2):
                        high1(s)
                        high2(s)
                    slots()
            act.wait_ge(dve_act, 1).then_inc(dve_act, -1)
            norm(X)

        @block.vector
        def _(dve):
            V = nc.vector

            def v(ins, *posts):
                ins.then_inc(dve_own, 1)
                dve.wait_ge(dve_own, 1).then_inc(dve_own, -1)
                for p in posts:
                    dve.sem_inc(p, 1)

            def parts(src, hi, lo, *posts):
                v(V.tensor_copy(hi, src))
                v(V.tensor_tensor(lo, src, hi.bitcast(F32), ALU.subtract), *posts)

            def tile_of(t, i):
                return t[:, bass.ds(i, 1), :].rearrange("p a n -> p (a n)")

            def norm(src, g, hi, lo, n=SEQ):
                dve.wait_ge(act_dve, 1).then_inc(act_dve, -1)
                for k in range(KT):
                    tmp = (tB, tC)[k % 2][:, 0:n]
                    v(V.scalar_tensor_tensor(out=tmp, in0=src[:, k, 0:n], scalar=vecs[:, g + k:g + k + 1],
                                             in1=rinv[:, 0:n], op0=ALU.mult, op1=ALU.mult))
                    parts(tmp, hi[:, k, 0:n], lo[:, k, 0:n])
                dve.sem_inc(dve_pe, 1)

            def rows(col, w):
                return C[:, None, col:col + w].to_broadcast([P, NC, w])

            def chan(g, i):
                return tk[g][:, i, :, None].to_broadcast([P, NC, CH])

            def bank(b):
                return chunked(ps[:, b, :])

            dve.sem_inc(dve_sp, 1)
            dve.wait_ge(load_cst, 16)
            dve.wait_ge(load_pos, 16)
            v(V.tensor_copy(tB[:, :], tA[:, :].bitcast(I32)))
            v(V.tensor_scalar(tB[:, :], tB[:, :], C[:, C_FREQ:C_FREQ + 1], None, ALU.mult))
            v(V.tensor_scalar(tC[:, :], tB[:, :], float(1 / (2 * np.pi)), MAGIC, ALU.mult, ALU.add))
            v(V.tensor_scalar(tC[:, :], tC[:, :], MAGIC, None, ALU.subtract))
            c1 = 6.28125
            c2 = float(np.float32(np.round((2 * np.pi - c1) * 2 ** 22) / 2 ** 22))
            c3 = float(2 * np.pi - c1 - c2)
            for c in (c1, c2, c3):
                v(V.scalar_tensor_tensor(out=tB[:, :], in0=tC[:, :], scalar=-c, in1=tB[:, :], op0=ALU.mult, op1=ALU.add))
            v(V.tensor_scalar(tC[:, :], tB[:, :], float(np.pi / 2), None, ALU.add))
            v(V.tensor_scalar(tD[:, :], tC[:, :], float(np.pi), -2 * float(np.pi), ALU.is_gt, ALU.mult))
            v(V.tensor_tensor(tC[:, :], tC[:, :], tD[:, :], ALU.add))
            for t, src in ((ropeC, tC), (ropeS, tB)):
                v(V.tensor_scalar(t[:, :], src[:, :], 3.14159, -3.14159, ALU.min, ALU.max), dve_act)
            for _ in range(2):
                dve.wait_ge(act_dve, 1).then_inc(act_dve, -1)
            dve.sem_inc(dve_act, 1)
            with dve.Fori(0, DEPTH) as lay:
                dve.wait_ge(load_vec, 16).then_inc(load_vec, -16)
                norm(X, V_MIXG, h_hi, h_lo)
                for b in range(2):
                    v(V.memset(px[b][:, 0:16], 0.0))
                    v(V.memset(pw[b][:, 0:16], 0.0))
                    dve.wait_ge(to_dve, 1).then_inc(to_dve, -1)
                    dve.sem_inc(split_free[b], 1)
                    v(V.tensor_copy(px[b][:, 16:], ps[:, b, :]), acc_free[b])

                def shifted(o, i, sh, rows=slice(0, P)):
                    v(V.tensor_tensor(o[rows, :], i[rows, 16:], i[rows, 16 - sh:16 + SEQ - sh], ALU.add))
                lo_half, hi_half = slice(0, HD), slice(HD, P)
                for b, out in ((0, tB), (1, tC)):
                    shifted(pw[0][:, 16:], px[b], 1)
                    if b == 1:
                        shifted(pw[1][:, 16:], pw[0], 2)
                        shifted(pw[0][:, 16:], pw[1], 4)
                    v(V.tensor_copy(out[lo_half, :], pw[0][lo_half, 16:]))
                    shifted(out[:, :], pw[0], (2, 8)[b], hi_half)
                    v(V.tensor_tensor(out[:, :], out[:, :], C[:, C_CNT + b * SEQ:C_CNT + (b + 1) * SEQ], ALU.mult))
                    v(V.tensor_tensor(out[:, :], out[:, :], px[b][:, 16:], ALU.subtract), dve_pe)
                for b in range(2):
                    dve.wait_ge(to_dve, 1).then_inc(to_dve, -1)
                    v(V.tensor_scalar(tD[:, :], ps[:, 2 + b, :], vecs[:, V_POOLS + b:V_POOLS + b + 1], None, ALU.mult))
                    parts(tD[:, :], B_hi[:, b, :], B_lo[:, b, :])
                dve.sem_inc(dve_pe, 1)
                with dve.Fori(0, MOBA_PAIRS) as j:
                    for s in range(2):
                        dve.wait_ge(to_dve, 1).then_inc(to_dve, -1)
                        dve.sem_inc(split_free[s], 1)
                        v(V.tensor_copy((qT, kT)[s], ps[:, s, :]), acc_free[s], dve_pe)
                    for s in range(2):
                        dve.wait_ge(to_dve, 1).then_inc(to_dve, -1)
                        x = (qT, kT)[s]
                        v(V.tensor_tensor(tB[:, :], ps[:, 2 + s, :], ropeS[:, :], ALU.mult))
                        v(V.tensor_tensor(x, x, ropeC[:, :], ALU.mult))
                        v(V.tensor_tensor(x, x, tB[:, :], ALU.add))
                    v(V.tensor_copy(vh, Vt[:, :, bass.ds(j * P, P)]), dve_pe)
                    for h in range(2):
                        for t in range(TT):
                            n = (t + 1) * P
                            dve.wait_ge(to_dve, 1).then_inc(to_dve, -1)
                            v(V.scalar_tensor_tensor(out=sc[:, 0:n], in0=ps[:, 3, 0:n], scalar=float(HD) ** -0.5,
                                                     in1=C[:, C_CAUS + SEQ - n:C_CAUS + SEQ], op0=ALU.mult, op1=ALU.add))
                            v(V.tensor_reduce(stat[:, 0:1], sc[:, 0:n], AX.X, ALU.max, negate=True), dve_act)
                            dve.wait_ge(act_dve, 1).then_inc(act_dve, -1)
                            v(V.reciprocal(stat[:, 2:3], stat[:, 1:2]))
                            v(V.tensor_scalar(pr[:, 0:n], pr[:, 0:n], stat[:, 2:3], None, ALU.mult), dve_pe)
                    dve.wait_ge(to_dve, 1).then_inc(to_dve, -1)
                    parts(ps[:, 5, :], tile_of(B_hi, j + 2), tile_of(B_lo, j + 2), dve_pe)
                dve.wait_ge(to_dve, 1).then_inc(to_dve, -1)
                for h in range(2):
                    q = slice(h * CH, (h + 1) * CH)
                    v(V.tensor_copy(ba[q].rearrange("p a b c -> p (a b) c"),
                                    ps[q, 3, 0:NC * 16].rearrange("p (n m h) -> p h m n", n=NC, h=2)[:, h]))
                dtb = vecs[:, V_DTB:V_DTB + PAIRS, None].to_broadcast([P, PAIRS, NC])
                v(V.tensor_tensor(spl[:, 2], ba[:, 1], dtb, ALU.add))
                v(V.scalar_tensor_tensor(out=spl[:, 0], in0=spl[:, 2], scalar=-1.0, in1=spl[:, 2], op0=ALU.mult, op1=ALU.min), dve_act)
                dve.wait_ge(act_dve, 1).then_inc(act_dve, -1)
                v(V.scalar_tensor_tensor(out=spl[:, 2], in0=spl[:, 2], scalar=0.0, in1=spl[:, 0], op0=ALU.max, op1=ALU.add))
                tg = tok[:, 0].rearrange("p (a b) -> p a b", a=PAIRS)
                v(V.scalar_tensor_tensor(out=tg, in0=spl[:, 2], scalar=-1.0, in1=ealog[:, :, None].to_broadcast([P, PAIRS, NC]),
                                         op0=ALU.mult, op1=ALU.mult), dve_pe)
                v(V.tensor_scalar(spl[:, 1], spl[:, 1], 1.0, None, ALU.add))
                v(V.reciprocal(tok[:, 1].rearrange("p (a b) -> p a b", a=PAIRS), spl[:, 1]))
                dve.wait_ge(act_dve, 1).then_inc(act_dve, -1)
                v(V.tensor_tensor(tok[:, 2], tok[:, 1], tok[:, 3], ALU.mult))
                with dve.Fori(0, PAIRS // 2) as j:
                    for g in range(2):
                        v(V.tensor_copy(tk[g], tok[:, :, bass.ds((j * 2 + g) * NC, NC)]))
                        v(V.tensor_copy(cw[g], vecs[:, bass.ds((j * 2 + g) * 12 + V_CONV, 12)]))
                        v(V.memset(St[g], 0.0))
                        v(V.memset(cv[g][:, :, 0:4], 0.0))
                        v(V.tensor_tensor(E1[g], rows(C_V64, CH), chan(g, 0), ALU.mult))
                        v(V.tensor_tensor(E2[g], rows(C_U64, CH), chan(g, 0), ALU.mult), dve_pe)
                    for g in range(2):
                        dve.wait_ge(act_dve, 1).then_inc(act_dve, -1)
                        v(V.tensor_tensor(E1[g], E1[g], rows(C_LOW, CH), ALU.mult))
                        v(V.tensor_tensor(E1[g], E1[g], chan(g, 1), ALU.mult))
                        v(V.tensor_tensor(E2[g], E2[g], rows(C_UPI, CH), ALU.mult))
                    for g in range(2):
                        for u in range(3):
                            dve.wait_ge(to_dve, 1).then_inc(to_dve, -1)
                            dve.sem_inc(split_free[u % 2], 1)
                            v(V.tensor_copy(cv[g][:, u, 4:], ps[:, u % 2, :]), acc_free[u % 2])
                            if g == 1:
                                dve.wait_ge(act_dve, 1).then_inc(act_dve, -1)
                            y = (tB, tC, tD)[u][:, :]
                            v(V.tensor_scalar(y, cv[g][:, u, 1:1 + SEQ], cw[g][:, u * 4:u * 4 + 1], None, ALU.mult))
                            for tap in range(1, 4):
                                v(V.scalar_tensor_tensor(out=y, in0=cv[g][:, u, 1 + tap:1 + tap + SEQ],
                                                         scalar=cw[g][:, u * 4 + tap:u * 4 + tap + 1], in1=y,
                                                         op0=ALU.mult, op1=ALU.add), *((dve_act,) if tap == 3 else ()))
                    for g in range(2):
                        dve.wait_ge(to_dve, 1).then_inc(to_dve, -1)
                        v(V.tensor_tensor(vb[g], bank(g), chan(g, 1), ALU.mult), acc_free[g])
                    for g in range(2):
                        dve.wait_ge(act_dve, 1).then_inc(act_dve, -1)
                        v(V.scalar_tensor_tensor(out=Qt[g], in0=Qt[g], scalar=float(HD) ** -0.5, in1=sqs[g][0],
                                                 op0=ALU.mult, op1=ALU.mult))
                        dve.wait_ge(act_dve, 1).then_inc(act_dve, -1)
                        v(V.tensor_tensor(Kt[g], Kt[g], sqs[g][1], ALU.mult), dve_pe)
                    for g in range(2):
                        b = 2 + 3 * g
                        dve.wait_ge(to_dve, 1).then_inc(to_dve, -1)
                        v(V.tensor_tensor(A_[g], bank(b), E1[g], ALU.mult), dve_pe)
                        v(V.tensor_tensor(aq[g], bank(b + 1), E2[g], ALU.mult))
                        v(V.tensor_tensor(kd[g], bank(b + 2), chan(g, 4), ALU.mult))
                        v(V.tensor_tensor(kg[g], bank(b + 2), chan(g, 2), ALU.mult))

                    for g in range(2):
                        dve.wait_ge(to_dve, 1).then_inc(to_dve, -1)
                        v(V.tensor_copy(AT[g], bank(2 + 3 * g)))
                        v(V.tensor_tensor(XX[g], A_[g], rows(C_LV1, CH), ALU.mult))
                        v(V.tensor_tensor(XX[g], rows(C_ID64, CH), XX[g], ALU.subtract))
                        v(V.tensor_tensor(XT[g], AT[g], rows(C_LVT, CH), ALU.mult))
                        v(V.tensor_tensor(XT[g], rows(C_ID64, CH), XT[g], ALU.subtract))
                        v(V.tensor_tensor(MT[g], AT[g], rows(C_LVT + CH, CH), ALU.mult), dve_pe)
                    for l in range(1, LEVELS):
                        for g in range(2):
                            if l < LEVELS - 1:
                                dve.wait_ge(to_dve, 1).then_inc(to_dve, -1)
                                v(V.tensor_tensor(XX[g], XX[g], bank(3 + 3 * g), ALU.subtract))
                                v(V.tensor_tensor(MT[g], AT[g], rows(C_LVT + (l + 1) * CH, CH), ALU.mult))
                            dve.wait_ge(to_dve, 1).then_inc(to_dve, -1)
                            v(V.tensor_tensor(XT[g], XT[g], bank(4 + 3 * g), ALU.subtract), dve_pe)
                    for n in range(NC):
                        for g in range(2):
                            dve.wait_ge(to_dve, 1).then_inc(to_dve, -1)
                            v(V.tensor_tensor(vn[g], Uu[g][:, n, :], ps[:, 2 + 3 * g, 0:CH], ALU.subtract), dve_pe)
                            dve.wait_ge(to_dve, 1).then_inc(to_dve, -1)
                            v(V.tensor_scalar(oo[g][:, n, :], ps[:, 3 + 3 * g, 0:CH], tk[g][:, 3, n:n + 1], None, ALU.mult))
                        for g in range(2):
                            dve.wait_ge(to_dve, 1).then_inc(to_dve, -1)
                            v(V.scalar_tensor_tensor(out=St[g], in0=St[g], scalar=tk[g][:, 5, n:n + 1],
                                                     in1=ps[:, 4 + 3 * g, 0:CH], op0=ALU.mult, op1=ALU.add))
                            dve.wait_ge(to_dve, 1).then_inc(to_dve, -1)
                            v(V.tensor_tensor(oo[g][:, n, :], oo[g][:, n, :], ps[:, 2 + 3 * g, 0:CH], ALU.add), dve_pe)
                    for g in range(2):
                        v(V.tensor_tensor(sq1[g], oo[g], oo[g], ALU.mult))
                        v(V.tensor_reduce(ost[g], sq1[g], AX.X, ALU.add), dve_act)
                    for g in range(2):
                        dve.wait_ge(act_dve, 1).then_inc(act_dve, -1)
                        v(V.tensor_tensor(oo[g], oo[g], ost[g][:, :, None].to_broadcast([P, NC, CH]), ALU.mult), dve_pe)
                    for g in range(2):
                        dve.wait_ge(to_dve, 1).then_inc(to_dve, -1)
                        v(V.scalar_tensor_tensor(out=tB[:, :], in0=ps[:, 2 + 3 * g, :], scalar=vecs[:, V_DNG:V_DNG + 1], in1=zz[g],
                                                 op0=ALU.mult, op1=ALU.mult))
                        parts(tB[:, :], tile_of(B_hi, j * 2 + g + 4), tile_of(B_lo, j * 2 + g + 4), dve_pe)
                dve.sem_inc(dve_pe, 1)
                dve.sem_inc(dve_act, 1)
                with dve.Fori(0, KT) as n:
                    dve.wait_ge(to_dve, 1).then_inc(to_dve, -1)
                    dve.sem_inc(split_free[1], 1)
                    for b in range(3):
                        dve.wait_ge(act_dve, 1).then_inc(act_dve, -1)
                        v(V.tensor_tensor(gts[b][:, :], gts[b][:, :], ps[:, 2 + b, :], ALU.mult))
                    for b in (1, 2):
                        v(V.tensor_tensor(tB[:, :], tB[:, :], gts[b][:, :], ALU.add))
                    parts(tB[:, :], tile_of(M_hi, n), tile_of(M_lo, n), dve_pe, dve_act)
                with dve.Fori(0, KT // 2) as i:
                    for s in range(2):
                        dve.wait_ge(to_dve, 1).then_inc(to_dve, -1)
                        dve.sem_inc(split_free[s], 1)
                        x = tile_of(X, i * 2 + s)
                        v(V.tensor_tensor(x, x, ps[:, s, :], ALU.add), acc_free[s])
                dve.sem_inc(dve_act, 1)
                norm(X, V_XAG, h_hi, h_lo)
                norm(memx, V_MEMG, N_hi, N_lo, MEM)
                with dve.Fori(0, XH) as h:
                    dve.wait_ge(to_dve, 1).then_inc(to_dve, -1)
                    dve.sem_inc(split_free[0], 1)
                    v(V.tensor_copy(xq, ps[:, 0, :]), acc_free[0])
                    dve.wait_ge(to_dve, 1).then_inc(to_dve, -1)
                    dve.sem_inc(split_free[1], 1)
                    v(V.tensor_copy(xk, ps[:, 1, 0:MEM]), acc_free[1])
                    v(V.tensor_copy(xvh, xv[:, :, bass.ds(h * P, P)]), dve_pe)
                    for t in range(TT):
                        dve.wait_ge(to_dve, 1).then_inc(to_dve, -1)
                        v(V.tensor_reduce(xst[:, 0:1], ps[:, 3, 0:MEM], AX.X, ALU.max))
                        v(V.tensor_scalar(xst[:, 0:1], xst[:, 0:1], -float(P) ** -0.5, None, ALU.mult), dve_act)
                        dve.wait_ge(act_dve, 1).then_inc(act_dve, -1)
                        v(V.reciprocal(xst[:, 2:3], xst[:, 1:2]))
                        v(V.tensor_scalar(xp, xp, xst[:, 2:3], None, ALU.mult), dve_pe)
                    dve.wait_ge(to_dve, 1).then_inc(to_dve, -1)
                    parts(ps[:, 5, :], tile_of(B_hi, h), tile_of(B_lo, h), dve_pe)
                with dve.Fori(0, KT // 4) as i:
                    for s in range(2):
                        dve.wait_ge(to_dve, 1).then_inc(to_dve, -1)
                        dve.sem_inc(split_free[s], 1)
                        for jj in range(2):
                            x = tile_of(X, i * 4 + 2 * s + jj)
                            v(V.tensor_tensor(x, x, ps[:, (s, 2 + s)[jj], :], ALU.add), *((acc_free[s],) if jj else ()))
                dve.sem_inc(dve_act, 1)
                dve.wait_ge(act_dve, 1).then_inc(act_dve, -1)
                for k in range(KT):
                    v(V.scalar_tensor_tensor(out=hF[:, k, :], in0=X[:, k, :], scalar=vecs[:, V_FFNG + k:V_FFNG + k + 1],
                                             in1=rinv[:, :], op0=ALU.mult, op1=ALU.mult))
                dve.sem_inc(dve_pe, 1)
                for i in range(2 * TT):
                    dve.wait_ge(to_dve, 1).then_inc(to_dve, -1)
                    c = slice((i % 2) * SEQ, (i % 2 + 1) * SEQ)
                    parts(ps[:, 2 + i % 2, :], H_hi[:, i // 2, c], H_lo[:, i // 2, c], dve_pe)
                dve.wait_ge(to_dve, 1).then_inc(to_dve, -1)
                v(V.tensor_copy(lg, ps[:, 4:8, 0:NE]))
                rank = C[:, None, C_RANK:C_RANK + NE].to_broadcast([P, TT, NE])

                def spread(m):
                    return m[:, :, None].to_broadcast([P, TT, NE])

                def best(m, oh):
                    v(V.tensor_reduce(m, lg, AX.X, ALU.max))
                    v(V.tensor_tensor(tt1, lg, spread(m), ALU.is_ge))
                    v(V.tensor_tensor(tt1, tt1, rank, ALU.mult))
                    v(V.tensor_reduce(m3, tt1, AX.X, ALU.max))
                    v(V.tensor_tensor(oh, tt1, spread(m3), ALU.is_ge))
                best(m1, oh1)
                v(V.scalar_tensor_tensor(out=lg, in0=oh1, scalar=NEG, in1=lg, op0=ALU.mult, op1=ALU.add))
                best(m2, oh2)
                v(V.tensor_tensor(m3, m2, m1, ALU.subtract), dve_act)
                dve.wait_ge(act_dve, 1).then_inc(act_dve, -1)
                v(V.tensor_scalar(m1, m3, 1.0, None, ALU.add))
                v(V.reciprocal(m1, m1))
                v(V.tensor_tensor(m2, m3, m1, ALU.mult))
                v(V.tensor_tensor(mask, oh1, oh2, ALU.add))
                v(V.tensor_tensor(oh1, oh1, spread(m1), ALU.mult))
                v(V.tensor_tensor(oh2, oh2, spread(m2), ALU.mult))
                v(V.tensor_tensor(comb[:, :, 0:NE], oh1, oh2, ALU.add))
                every = vecs[:, None, V_PART:V_PART + NE].to_broadcast([P, TT, NE])
                for m in (comb[:, :, 0:NE], mask):
                    v(V.scalar_tensor_tensor(out=m, in0=m, scalar=vecs[:, V_ROUTED:V_ROUTED + 1], in1=every,
                                             op0=ALU.mult, op1=ALU.add), *((dve_pe,) if m is mask else ()))
                dve.wait_ge(to_dve, 1).then_inc(to_dve, -1)
                v(V.scalar_tensor_tensor(out=rk[:, :, 0:NE], in0=ps[:, 4, 0:TT * NE].rearrange("p (a b) -> p a b", a=TT), scalar=1.0,
                                         in1=mask, op0=ALU.add, op1=ALU.mult))
                v(V.tensor_scalar(rk[:, :, 0:NE], rk[:, :, 0:NE], 1.0, None, ALU.subtract))
                v(V.memset(rk[:, :, NE:NE + 1], -1.0))
                v(V.memset(comb[:, :, NE:NE + 1], 0.0))
                v(V.tensor_copy(cnt, ps[:, 4, TT * NE:(TT + 1) * NE]))
                v(V.tensor_tensor(flag.rearrange("p (a b) -> p a b", a=NE), cnt[:, :, None].to_broadcast([P, NE, PASSES]),
                                  C[:, C_JPASS:C_JPASS + NQ].rearrange("p (a b) -> p a b", a=NE), ALU.is_gt))
                v(V.memset(flag[:, 0:1], 1.0))
                v(V.tensor_tensor(jw, C[:, C_JLT:C_JLT + NQ * NQ].rearrange("p (a b) -> p a b", a=NQ),
                                  flag[:, None, :].to_broadcast([P, NQ, NQ]), ALU.mult))
                v(V.tensor_reduce(jpos, jw, AX.X, ALU.add))
                v(V.tensor_reduce(jn, flag, AX.X, ALU.add))
                for table, col in ((jpart, C_JPART), (jbase, C_JPASS)):
                    v(V.tensor_tensor(jw2, jpos[:, None, :].to_broadcast([P, NQ + 1, NQ]),
                                      C[:, C_JNUM:C_JNUM + NQ + 1, None].to_broadcast([P, NQ + 1, NQ]), ALU.is_equal))
                    for w in (flag, C[:, col:col + NQ]):
                        v(V.tensor_tensor(jw2, jw2, w[:, None, :].to_broadcast([P, NQ + 1, NQ]), ALU.mult))
                    v(V.tensor_reduce(table, jw2, AX.X, ALU.add))
                v(V.tensor_scalar(jw2[:, :, 0], C[:, C_JNUM:C_JNUM + NQ + 1], jn[:, 0:1], vecs[:, V_NPART:V_NPART + 1],
                                  ALU.is_equal, ALU.mult))
                v(V.tensor_tensor(jobs[:, 0:NQ + 1], jpart, jw2[:, :, 0], ALU.add))
                v(V.tensor_copy(jobs[:, NQ + 1:NQ + 2], jn), dve_sp, dve_pe, dve_act, dve_pool)
                def halves(half):
                    return slice(half * HALF, (half + 1) * HALF)

                def rest(s, half):
                    c = halves(half)
                    dve.wait_ge(high_full[s], 1).then_inc(high_full[s], -1)
                    v(V.tensor_tensor(w_lo[:, s, c], raw[:, s, c], w_hi[:, s, c].bitcast(F32), ALU.subtract),
                      *((raw_free2[s], split_full[s]) if half else (raw_free[s], first_full[s])))

                def place(e, j):
                    v(V.tensor_scalar(rj, rk[:, :, bass.ds(e, 1)].rearrange("p a b -> p (a b)"), jbase[:, bass.ds(j, 1)],
                                      None, ALU.subtract))
                    v(V.tensor_copy(cj, comb[:, :, bass.ds(e, 1)].rearrange("p a b -> p (a b)")))
                    for t in range(TT):
                        v(V.tensor_scalar(Pm[:, t, :], C[:, C_SLOT:C_SLOT + CAP], rj[:, t:t + 1], None, ALU.is_equal))
                    dve.sem_inc(dve_pe, 1)

                def gathered():
                    for f in range(1, KT, 2):
                        dve.wait_ge(to_dve, 1).then_inc(to_dve, -1)
                        v(V.tensor_copy(hg[:, f, :], ps[:, GB[f], :]), dve_pe)

                def weights():
                    dve.wait_ge(to_dve, 1).then_inc(to_dve, -1)
                    v(V.tensor_copy(ws, ps[:, 6, 0:ST]))

                n_jobs = dve.value_load(jobs[0:1, NQ + 1:NQ + 2], min_val=1, max_val=NQ)
                place(0, 0)
                gathered()
                weights()
                with dve.Fori(0, n_jobs) as j:
                    e1 = dve.value_load(jobs[0:1, bass.ds(j + 1, 1)], min_val=0, max_val=NE)
                    place(e1, j + 1)
                    with dve.Fori(0, FT):
                        rest(0, 0)
                        rest(0, 1)
                        rest(1, 0)
                        dve.wait_ge(to_dve, 1).then_inc(to_dve, -1)
                        dve.sem_inc(split_free[1], 1)
                        dve.wait_ge(act_dve, 1).then_inc(act_dve, -1)
                        dve.wait_ge(pool_dve, 1).then_inc(pool_dve, -1)
                        v(V.tensor_tensor(hid, gu, ps[:, 1, 0:CAP], ALU.mult), acc_free[1], dve_act)
                        rest(1, 1)
                    dve.wait_ge(pool_dve, 1).then_inc(pool_dve, -1)
                    dve.sem_inc(hidden_ready, 1)
                    gathered()
                    with dve.Fori(0, FT // 2):
                        for s in range(2):
                            for half in range(2):
                                rest(s, half)
                    for half in range(2):
                        for st in range(ST):
                            c = slice(half * SEQ, (half + 1) * SEQ)
                            dve.wait_ge(act_dve, 1).then_inc(act_dve, -1)
                            v(V.scalar_tensor_tensor(out=Y_lo[:, st, c], in0=ps[:, 2 + 2 * st + half, :],
                                                     scalar=ws[:, st:st + 1], in1=Y_hi[:, st, c].bitcast(F32),
                                                     op0=ALU.mult, op1=ALU.subtract), dve_pe)
                    for half in range(2):
                        rest(0, half)
                    for f in range(KT):
                        dve.wait_ge(to_dve, 1).then_inc(to_dve, -1)
                        v(V.tensor_tensor(X[:, f, :], X[:, f, :], ps[:, SB[f], :], ALU.add),
                          *((acc_free[SB[f]],) if SB[f] < 2 else (dve_pe,) if f in (1, KT - 1) else ()))
                    for half in range(2):
                        rest(1, half)
                    weights()
                dve.sem_inc(dve_act, 1)
                dve.sem_inc(dve_sp, 1)
            dve.wait_ge(act_dve, 1).then_inc(act_dve, -1)
            for k in range(KT):
                v(V.scalar_tensor_tensor(out=final[:, k, :], in0=X[:, k, :],
                                         scalar=vecs[:, V_FING + k:V_FING + k + 1],
                                         in1=rinv[:, :], op0=ALU.mult, op1=ALU.mult))
            dve.sem_inc(dve_sp, 1)



def by_partition(w):
    return w.reshape(w.shape[0] // P, P, w.shape[1]).transpose(1, 0, 2)


def tiles(w, n_out):
    a = by_partition(w)
    k, n = a.shape[1], w.shape[1]
    a = a.reshape(P, k, n // (P * n_out), n_out, P).transpose(2, 0, 3, 1, 4)
    return a.reshape(n // (P * n_out), P, n_out * k * P)


def rows_first(w, k):
    a = by_partition(w)
    n = w.shape[1]
    return a.reshape(P, a.shape[1] // k, k, n).transpose(1, 0, 2, 3).reshape(-1, P, k * n)


def mix_stream(w_in, w_up, w_out, wq, wkv, wo):
    o_moba, o_dn = 256, 256 + 768
    o_ba = o_dn + 1536
    o_z = o_ba + 16
    o_gate = o_z + 512
    t = tiles(w_in[:, 0:256], 1)
    out = [t, rows_first(w_in[:, o_moba + 512:o_moba + 768], 4)]
    q, k = tiles(w_in[:, o_moba:o_moba + 256], 1), tiles(w_in[:, o_moba + 256:o_moba + 512], 1)
    out += [x[j:j + 1] for j in range(MOBA_PAIRS) for x in (q, k)]
    qkvz = [tiles(w_in[:, o:o + 512], 1) for o in (o_dn, o_dn + 512, o_dn + 1024, o_z)]
    out += [x[j:j + 1] for j in range(PAIRS) for x in qkvz]
    gates = [tiles(w_in[:, o_gate + b * D:o_gate + (b + 1) * D], 1) for b in range(3)]
    up = tiles(w_up, 1)
    out += [x[j:j + 1] for j in range(KT) for x in (*gates, up)]
    out += [tiles(w_out, 1), rows_first(wkv[:, 512:1024], 2)]
    q, k = tiles(wq, 1), tiles(wkv[:, 0:512], 1)
    out += [x[j:j + 1] for j in range(XH) for x in (q, k)]
    out += [tiles(wo, 2)]
    return out


def ffn_stream(w_gate_up, w_down, e):
    ff = w_gate_up.shape[1] // 2
    c = slice(e * FF, (e + 1) * FF)
    gate, up = tiles(w_gate_up[:, 0:ff][:, c], 1), tiles(w_gate_up[:, ff:][:, c], 1)
    return [x[j:j + 1] for j in range(FT) for x in (gate, up)] + [rows_first(w_down[c], 1), gate[0:1]]


def kernel(**inputs):
    import concourse.bacc as bacc
    from concourse.bass_utils import run_bass_kernel_spmd

    a = {k: np.asarray(v) for k, v in inputs.items()}
    stream = []
    vec = np.zeros((DEPTH, P, NV), np.float32)
    small = np.zeros((DEPTH, P, 2 * P + KT * 16 + KT * NE), np.float32)
    for l in range(DEPTH):
        w_up = np.concatenate([a["w_up_pool"][l], a["w_up_moba"][l], a["w_up_dn"][l]], axis=0)
        stream += mix_stream(a["w_in"][l], w_up, a["w_out"][l], a["xa_wq"][l], a["xa_wkv"][l], a["xa_wo"][l])
        for e in range(NE if l % 2 else DENSE_PARTS):
            stream += (ffn_stream(a["moe_w_gate_up"][l // 2, e], a["moe_w_down"][l // 2, e], 0) if l % 2
                       else ffn_stream(a["dense_w_gate_up"][l // 2], a["dense_w_down"][l // 2], e))
        for c, name in ((V_MIXG, "mix_norm_g"), (V_XAG, "xa_norm_g"), (V_MEMG, "mem_norm_g"), (V_FFNG, "ffn_norm_g")):
            vec[l, :, c:c + KT] = a[name][l].reshape(KT, P).T
        vec[l, :, V_FING:V_FING + KT] = a["final_norm_g"].reshape(KT, P).T
        vec[l, :, V_CONV:V_CONV + 48] = a["dn_conv_w"][l].reshape(4, 3, PAIRS, P).transpose(3, 2, 1, 0).reshape(P, 48)
        vec[l, :, V_POOLS:V_POOLS + 2] = a["pool_scale"][l].reshape(2, P).T
        vec[l, :, V_DNG] = np.concatenate([a["dn_norm_g"][l]] * 2)
        for c, name in ((V_ALOG, "dn_a_log"), (V_DTB, "dn_dt_bias")):
            vec[l, :, c:c + PAIRS] = np.repeat(a[name][l].reshape(PAIRS, 2).T, HD, axis=0)
        vec[l, :, V_ROUTED] = l % 2
        vec[l, :, V_PART:V_PART + DENSE_PARTS] = 1 - l % 2
        vec[l, :, V_NPART] = NE if l % 2 else DENSE_PARTS
        for b in range(4):
            r = slice((b % 2) * HD, (b % 2 + 1) * HD)
            c = (b // 2) * P + (b % 2) * HD
            small[l, r, c:c + HD] = a["pool_w"][l, b]
        small[l, :, 2 * P:2 * P + KT * 16] = by_partition(a["w_in"][l][:, 2560:2576]).reshape(P, KT * 16)
        small[l, :, 2 * P + KT * 16:] = by_partition(a["moe_router"][0]).reshape(P, KT * NE)

    nc = bacc.Bacc("TRN2", target_bir_lowering=False, num_devices=1)
    arrays = {
        "x_t": by_partition(a["x"][0].T),
        "mem_t": by_partition(a["mem"][0].T),
        "pos": a["positions"].astype(np.int32),
        "cst": constants(),
        "vec": vec,
        "wsm": small,
        "wst": np.concatenate(stream + [stream[0][0:1]] * 2, axis=0),
    }
    arrays = {k: np.ascontiguousarray(v) for k, v in arrays.items()}
    args = [nc.dram_tensor(k, v.shape, mybir.dt.from_np(v.dtype), kind="ExternalInput").ap() for k, v in arrays.items()]
    out = nc.dram_tensor("out_t", (P, KT, SEQ), F32, kind="ExternalOutput").ap()
    program(nc, *args, out)
    r = run_bass_kernel_spmd(nc, [arrays], core_ids=[0])
    got = np.asarray(r.results[0]["out_t"])
    return np.ascontiguousarray(got.transpose(1, 0, 2).reshape(D, SEQ).T).reshape(1, SEQ, D)
```

```python
from contextlib import ExitStack

import numpy as np

import concourse.bass as bass
from concourse import mybir

F32 = mybir.dt.float32
F32R = mybir.dt.float32r
I32 = mybir.dt.int32
ALU = mybir.AluOpType
ACT = mybir.ActivationFunctionType
AX = mybir.AxisListType

P = 128
SEQ = 512
D = 1024
DEPTH = 2
MEM = 256
KT = D // P
TT = SEQ // P
RMS_EPS = 1e-6
POOL_WINDOWS = (2, 4, 8, 16)
HD = 64
PAIRS = 4
CH = 64
NC = SEQ // CH
MOBA_PAIRS = 2
XH = 4
FF = 1408
FT = FF // P
NE = 8
DENSE_PARTS = 2
CAP = 256
PASSES = SEQ // CAP
NQ = NE * PASSES
ST = CAP // P
UNIT = KT * P
PART_UNITS = 3 * FT + 1
HALF = UNIT // 2
MIX_UNITS = 2 + 2 + MOBA_PAIRS * 2 + PAIRS * 4 + KT * 4 + KT + 4 + XH * 2 + KT // 2
LEVELS = 6
ROPE_HALF = 8
ROPE_THETA = 500000.0
NEG = -1e30
MAGIC = 12582912.0

V_MIXG, V_XAG, V_MEMG, V_FFNG, V_FING = 0, 8, 16, 24, 32
V_CONV = 40
V_POOLS = 88
V_DNG = 90
V_ALOG = 91
V_DTB = 95
V_ROUTED = 99
V_PART = 100
V_NPART = V_PART + NE
NV = V_NPART + 1

C_ID, C_ONE, C_BONE, C_ROT, C_UB, C_VB = 0, 128, 256, 384, 512, 640
C_V64, C_U64, C_LOW, C_UPI, C_ID64, C_LV1 = 768, 832, 896, 960, 1024, 1088
C_LVT = 1152
C_CAUS = C_LVT + LEVELS * 64
C_CNT = C_CAUS + SEQ
C_FREQ = C_CNT + 2 * SEQ
C_RANK = C_FREQ + 1
C_EPS = C_RANK + NE
C_SU = C_EPS + 1
C_SLOT = C_SU + P
C_JPASS = C_SLOT + CAP
C_JPART = C_JPASS + NQ
C_JNUM = C_JPART + NQ
C_JLT = C_JNUM + NQ + 1
NCST = C_JLT + NQ * NQ


def constants():
    c = np.zeros((P, NCST), np.float32)
    p = np.arange(P)[:, None]
    j = np.arange(P)[None, :]
    same = (p // HD) == (j // HD)
    c[:, C_ID:C_ID + P] = p == j
    c[:, C_ONE:C_ONE + P] = 1
    c[:, C_BONE:C_BONE + P] = same
    jd = j % HD
    c[:, C_ROT:C_ROT + P] = (1.0 * ((p == j - ROPE_HALF) & (jd >= ROPE_HALF) & (jd < 2 * ROPE_HALF))
                             - 1.0 * ((p == j + ROPE_HALF) & (jd < ROPE_HALF)))
    c[:, C_UB:C_UB + P] = same & (p <= j)
    c[:, C_VB:C_VB + P] = same & (p > j)
    r = p % CH
    k = np.arange(CH)[None, :]
    c[:, C_V64:C_V64 + CH] = r > k
    c[:, C_U64:C_U64 + CH] = r <= k
    c[:, C_LOW:C_LOW + CH] = r > k
    c[:, C_UPI:C_UPI + CH] = k >= r
    c[:, C_ID64:C_ID64 + CH] = r == k
    for l in range(LEVELS):
        s = 1 << l
        low = (r // (2 * s) == k // (2 * s)) & (r % (2 * s) >= s) & (k % (2 * s) < s)
        up = (r // (2 * s) == k // (2 * s)) & (k % (2 * s) >= s) & (r % (2 * s) < s)
        if l == 0:
            c[:, C_LV1:C_LV1 + CH] = low
        c[:, C_LVT + l * CH:C_LVT + (l + 1) * CH] = up
    t = np.arange(SEQ)[None, :]
    c[:, C_CAUS:C_CAUS + SEQ] = np.where(t - (SEQ - P) <= p, 0.0, NEG)
    for b in range(2):
        w = np.where(p < HD, POOL_WINDOWS[2 * b], POOL_WINDOWS[2 * b + 1])
        c[:, C_CNT + b * SEQ:C_CNT + (b + 1) * SEQ] = 1.0 / np.minimum(t + 1, w)
    freq = np.power(np.float32(ROPE_THETA), -np.arange(ROPE_HALF, dtype=np.float32) * np.float32(2.0) / np.float32(16))
    d = np.arange(P) % HD
    c[:, C_FREQ] = np.where(d < 2 * ROPE_HALF, freq[d % ROPE_HALF], 0.0)
    c[:, C_RANK:C_RANK + NE] = NE - np.arange(NE)[None, :]
    c[:, C_EPS] = RMS_EPS
    c[:, C_SU:C_SU + P] = p < j
    c[:, C_SLOT:C_SLOT + CAP] = np.arange(CAP)
    q = np.arange(NQ)
    c[:, C_JPASS:C_JPASS + NQ] = (q % PASSES) * CAP
    c[:, C_JPART:C_JPART + NQ] = q // PASSES
    c[:, C_JNUM:C_JNUM + NQ + 1] = np.arange(NQ + 1)
    c[:, C_JLT:C_JLT + NQ * NQ] = (q[None, :] < q[:, None]).reshape(-1)
    return c


def program(nc, x_t, mem_t, pos, cst, vec, wsm, wst, out_t):
    ctx = ExitStack()
    with ctx:
        def sb(name, shape, dt=F32):
            return ctx.enter_context(nc.sbuf_tensor(name, shape, dt))

        def sem(name):
            return ctx.enter_context(nc.semaphore(name))

        X = sb("X", [P, KT, SEQ])
        h_hi = sb("h_hi", [P, KT, SEQ], F32R)
        h_lo = sb("h_lo", [P, KT, SEQ], F32R)
        C = sb("C", [P, NCST])
        vecs = sb("vecs", [P, NV])
        NSM = 2 * P + KT * 16 + KT * NE
        wsmall = sb("wsmall", [P, NSM])
        raw = sb("raw", [P, 4, UNIT])
        w_hi = sb("w_hi", [P, 2, UNIT], F32R)
        w_lo = sb("w_lo", [P, 2, UNIT], F32R)
        ropeC = sb("ropeC", [P, SEQ])
        ropeS = sb("ropeS", [P, SEQ])
        rinv = sb("rinv", [P, SEQ])
        jobs = sb("jobs", [P, NQ + 2], I32)
        tA = sb("tA", [P, SEQ])
        tB = sb("tB", [P, SEQ])
        tC = sb("tC", [P, SEQ])
        tD = sb("tD", [P, SEQ])
        tE = sb("tE", [P, SEQ])
        B_hi = sb("B_hi", [P, FT, SEQ], F32R)
        B_lo = sb("B_lo", [P, KT, SEQ], F32R)
        AR_COLS = 12900
        with ExitStack() as same:
            def first(name, shape, dt):
                return same.enter_context(nc.sbuf_tensor(name, shape, dt))
            M_hi = first("M_hi", [P, KT, SEQ], F32R)
            M_lo = first("M_lo", [P, KT, SEQ], F32R)
            N_hi = first("N_hi", [P, KT, MEM], F32R)
            N_lo = first("N_lo", [P, KT, MEM], F32R)
        with ExitStack() as same:
            Y_hi = first("Y_hi", [P, ST, D], F32R)
            Y_lo = first("Y_lo", [P, ST, D], F32R)
            Pm = first("Pm", [P, TT, CAP], F32R)
            PT = first("PT", [P, ST, SEQ], F32R)
        AR = sb("AR", [P, AR_COLS])
        at = [0]

        def arena(*shape):
            n = int(np.prod(shape))
            a = AR[:, at[0]:at[0] + n]
            at[0] += n
            assert at[0] <= AR_COLS, at[0]
            if len(shape) == 2:
                return a.rearrange("p (a b) -> p a b", a=shape[0])
            if len(shape) == 3:
                return a.rearrange("p (a b c) -> p a b c", a=shape[0], b=shape[1])
            return a

        ps = ctx.enter_context(nc.psum_tensor("ps", [P, 8, SEQ], F32))

        ident = C[:, C_ID:C_ID + P]
        id64 = C[:, C_ID64:C_ID64 + CH]

        at[0] = 0
        Vt = arena(TT, 256)
        vh = arena(TT, P)
        qT = arena(SEQ)
        kT = arena(SEQ)
        sc = arena(2, SEQ)
        pr = arena(2, SEQ)
        pT = arena(2, TT, P)
        stat = arena(2, 4)
        STEPS = [(h, t) for h in range(2) for t in range(TT)]
        at[0] = 0
        px = [arena(16 + SEQ) for _ in range(2)]
        pw = [arena(16 + SEQ) for _ in range(2)]
        at[0] = 0
        ba = arena(2, PAIRS, NC)
        spl = arena(3, PAIRS, NC)
        ealog = arena(PAIRS)
        tok = arena(6, PAIRS * NC)
        tk = [arena(6, NC) for _ in range(2)]
        cw = [arena(12) for _ in range(2)]
        St = [arena(CH) for _ in range(2)]
        vn = [arena(CH) for _ in range(2)]
        ost = [arena(NC) for _ in range(2)]
        baT = AR[:, at[0]:at[0] + SEQ]
        AT, MT, XX, XT, P1, EE, cv, sq1 = [], [], [], [], [], [], [], []
        for g in range(2):
            cv.append(AR[:, at[0]:at[0] + 3 * (4 + SEQ)].rearrange("p (a b) -> p a b", a=3))
            sq1.append(AR[:, at[0] + SEQ:at[0] + 2 * SEQ].rearrange("p (a b) -> p a b", a=NC))
            AT.append(arena(NC, CH))
            MT.append(arena(NC, CH))
            arena(CH)
            XX.append(arena(NC, CH))
            XT.append(arena(NC, CH))
            P1.append(arena(NC, CH))
            EE.append(arena(2, SEQ))

        def flat(t):
            return t.rearrange("p a b -> p (a b)")

        def chunked(t):
            return t.rearrange("p (a b) -> p a b", a=NC)

        E1 = [chunked(t[:, 0, :]) for t in EE]
        E2 = [chunked(t[:, 1, :]) for t in EE]
        A_, Uu, wT, oo = XX, AT, XX, P1
        Kt, Vv = [flat(t) for t in XT], [flat(t) for t in P1]
        Qt = [arena(SEQ) for _ in range(2)]
        aq = [arena(NC, CH) for _ in range(2)]
        kd = [arena(NC, CH), chunked(tE[:, :])]
        zz = [rinv[:, :], arena(SEQ)]
        vb = [chunked(tB[:, :]), chunked(tD[:, :])]
        kg = [chunked(tC[:, :]), chunked(tA[:, :])]
        sqs = [(tA[:, :], tE[:, :]), (flat(aq[0]), flat(kd[0]))]
        at[0] = 2 * ST * D + TT * CAP + ST * SEQ
        hF = arena(KT, SEQ)
        lg, oh1, oh2, tt1, mask = (arena(TT, NE) for _ in range(5))
        comb, rk = (arena(TT, NE + 1) for _ in range(2))
        m1, m2, m3 = (arena(TT) for _ in range(3))
        cnt = arena(NE)
        flag = arena(NQ)
        jpos = arena(NQ)
        jw = arena(NQ, NQ)
        jw2 = arena(NQ + 1, NQ)
        jw3 = arena(NQ + 1, NQ)
        jpart = arena(NQ + 1)
        jbase = arena(NQ + 1)
        jn = arena(1)
        rj = arena(TT)
        cj = arena(TT)
        ws = arena(ST)
        gu, hid = tB[:, 0:CAP], tC[:, 0:CAP]
        at[0] = 0
        xv = arena(2, XH * P)
        xvh = arena(2, P)
        xq = arena(SEQ)
        xk = arena(MEM)
        xp = arena(2, MEM)
        xpT = arena(2, SEQ)
        xst = arena(2, 4)
        gmem = tE[:, 0:KT]
        at[0] = 2 * KT * SEQ
        memx = arena(KT, MEM)
        at[0] = 0
        final = arena(KT, SEQ)
        gts = [tB, tC, tD]

        load_x = sem("load_x")
        load_mem = sem("load_mem")
        load_pos = sem("load_pos")
        load_cst = sem("load_cst")
        load_vec = sem("load_vec")
        load_sm = sem("load_sm")
        landed = [sem(f"landed{s}") for s in range(2)]
        raw_full = [sem(f"raw_full{s}") for s in range(2)]
        raw_free = [sem(f"raw_free{s}") for s in range(2)]
        hi_full = [sem(f"hi_full{s}") for s in range(2)]
        split_full = [sem(f"split_full{s}") for s in range(2)]
        split_free = [sem(f"split_free{s}") for s in range(2)]
        first_full = [sem(f"first_full{s}") for s in range(2)]
        half_free = [sem(f"half_free{s}") for s in range(2)]
        high_full = [sem(f"high_full{s}") for s in range(2)]
        pool_own = sem("pool_own")
        act_own = sem("act_own")
        dve_own = sem("dve_own")
        acc_free = [sem(f"acc_free{s}") for s in range(2)]
        to_act = sem("to_act")
        to_dve = sem("to_dve")
        act_pe = sem("act_pe")
        dve_pe = sem("dve_pe")
        act_dve = sem("act_dve")
        dve_act = sem("dve_act")
        rope_ready = sem("rope_ready")
        conv_read = sem("conv_read")
        dve_sp = sem("dve_sp")
        store_out = sem("store_out")
        dve_pool = sem("dve_pool")
        pool_dve = sem("pool_dve")
        act_pool = sem("act_pool")
        hidden_ready = sem("hidden_ready")

        H_hi = h_hi[:, :, :].rearrange("p (t a) s -> p t (a s)", a=2)
        H_lo = h_lo[:, :, :].rearrange("p (t a) s -> p t (a s)", a=2)
        hg, hh = B_lo, B_hi

        def raw_of(s, turn, c=slice(0, UNIT)):
            return raw[:, bass.ds(turn * 2 + s, 1), c].rearrange("p a n -> p (a n)")

        GB = (6, 7, 2, 3, 4, 5, 6, 7)
        SB = (6, 7, 0, 1, 2, 3, 4, 5)

        block = ctx.enter_context(nc.Block())

        @block.sync
        def _(sp):
            sp.dma_start(C[:, :], cst).then_inc(load_cst, 16)
            sp.dma_start(tD[:, :].bitcast(I32), pos.to_broadcast([P, SEQ])).then_inc(load_pos, 16)
            sp.dma_start(X[:, :, :], x_t).then_inc(load_x, 16)
            for s in range(2):
                sp.dma_start(raw[:, s, :], wst[s:s + 1].rearrange("a p n -> (a p) n")).then_inc(landed[s], 16)
            for s in range(2):
                sp.wait_ge(landed[s], 16).then_inc(landed[s], -16)
                sp.sem_inc(raw_full[s], 1)
                sp.sem_inc(raw_free[s], 1)
            with sp.Fori(0, DEPTH) as lay:
                sp.wait_ge(dve_sp, 1).then_inc(dve_sp, -1)
                sp.dma_start(vecs[:, :], vec[bass.ds(lay, 1)].rearrange("a p n -> (a p) n")).then_inc(load_vec, 16)
                sp.dma_start(wsmall[:, :], wsm[bass.ds(lay, 1)].rearrange("a p n -> (a p) n")).then_inc(load_sm, 16)
                wbase = lay * (MIX_UNITS + DENSE_PARTS * PART_UNITS)

                def land(s):
                    sp.wait_ge(landed[s], 16).then_inc(landed[s], -16)
                    sp.sem_inc(raw_full[s], 1)

                def load(s, at, turn):
                    sp.wait_ge(raw_free[s], 1).then_inc(raw_free[s], -1)
                    sp.dma_start(raw_of(s, turn), wst[bass.ds(at + s, 1)].rearrange("a p n -> (a p) n")) \
                        .then_inc(landed[s], 16)

                def load_pair(at, turn):
                    for s in range(2):
                        land(s)
                        load(s, at, turn)

                for s in range(2):
                    load(s, wbase + 2, 1)
                with sp.Fori(0, MIX_UNITS // 2 - 2) as i:
                    load_pair(wbase + 4 + i * 2, i % 2)
                load_pair(wbase + MIX_UNITS, 0)
                for s in range(2):
                    land(s)
                sp.wait_ge(dve_sp, 1).then_inc(dve_sp, -1)
                n_jobs = sp.value_load(jobs[0:1, NQ + 1:NQ + 2], min_val=1, max_val=NQ)
                with sp.Fori(0, n_jobs) as j:
                    e = sp.value_load(jobs[0:1, bass.ds(j, 1)], min_val=0, max_val=NE - 1)
                    e1 = sp.value_load(jobs[0:1, bass.ds(j + 1, 1)], min_val=0, max_val=NE)
                    pbase = wbase + MIX_UNITS + e * PART_UNITS
                    for s in range(2):
                        load(s, pbase + 2, (j + 1) % 2)
                    with sp.Fori(0, PART_UNITS // 2 - 2) as i:
                        load_pair(pbase + 4 + i * 2, (j + i) % 2)
                    load_pair(wbase + MIX_UNITS + e1 * PART_UNITS, (j + 1) % 2)
                    for s in range(2):
                        land(s)
            sp.wait_ge(dve_sp, 1).then_inc(dve_sp, -1)
            sp.wait_ge(dve_sp, 1).then_inc(dve_sp, -1)
            sp.dma_start(out_t, final).then_inc(store_out, 16)
            sp.wait_ge(store_out, 16)

        @block.gpsimd
        def _(pool):
            def rest(s, turn):
                pool.wait_ge(hi_full[s], 1).then_inc(hi_full[s], -1)
                nc.gpsimd.tensor_tensor(w_lo[:, s, :], raw_of(s, turn), w_hi[:, s, :].bitcast(F32),
                                        ALU.subtract).then_inc(pool_own, 1)
                pool.wait_ge(pool_own, 1).then_inc(pool_own, -1)
                pool.sem_inc(raw_free[s], 1)
                pool.sem_inc(split_full[s], 1)

            for s in range(2):
                rest(s, 0)
            with pool.Fori(0, DEPTH):
                with pool.Fori(0, MIX_UNITS // 4):
                    for turn in (1, 0):
                        for s in range(2):
                            rest(s, turn)
                pool.wait_ge(dve_pool, 1).then_inc(dve_pool, -1)
                n_jobs = pool.value_load(jobs[0:1, NQ + 1:NQ + 2], min_val=1, max_val=NQ)
                with pool.Fori(0, n_jobs) as j:
                    pool.wait_ge(dve_pool, 1).then_inc(dve_pool, -1)
                    pool.sem_inc(pool_dve, 1)
                    with pool.Fori(0, FT) as i:
                        turn = pool.snap((j + i + 1) % 2, min_val=0, max_val=1)
                        for half in range(2):
                            pool.wait_ge(high_full[1], 1).then_inc(high_full[1], -1)
                            c = slice(half * HALF, (half + 1) * HALF)
                            nc.gpsimd.tensor_tensor(w_lo[:, 1, c], raw_of(1, turn, c), w_hi[:, 1, c].bitcast(F32),
                                                    ALU.subtract).then_inc(pool_own, 1)
                            pool.wait_ge(pool_own, 1).then_inc(pool_own, -1)
                            pool.sem_inc(split_full[1] if half else first_full[1], 1)
                        pool.sem_inc(raw_free[1], 1)
                        pool.wait_ge(act_pool, 1).then_inc(act_pool, -1)
                        t = hh[:, bass.ds(i, 1), :].rearrange("p a n -> p (a n)")
                        nc.gpsimd.tensor_tensor(t[:, CAP:2 * CAP], hid, t[:, 0:CAP].bitcast(F32),
                                                ALU.subtract).then_inc(pool_own, 1)
                        pool.wait_ge(pool_own, 1).then_inc(pool_own, -1)
                        pool.sem_inc(pool_dve, 1)

        @block.tensor
        def _(pe):
            mm = nc.tensor.matmul

            def prod3(acc, whi, wlo, xhi, xlo, start, stop):
                mm(acc, wlo, xhi, start=start, stop=False)
                mm(acc, whi, xlo, start=False, stop=False)
                return mm(acc, whi, xhi, start=False, stop=stop)

            def unit(s, hi, lo, n=SEQ, nk=KT, fresh=False):
                pe.wait_ge(split_full[s], 1).then_inc(split_full[s], -1)
                pe.wait_ge(acc_free[s], 1).then_inc(acc_free[s], -1)
                for k in range(nk):
                    if fresh:
                        pe.wait_ge(dve_pe, 1).then_inc(dve_pe, -1)
                    last = prod3(ps[:, s, 0:n], w_hi[:, s, k * P:(k + 1) * P], w_lo[:, s, k * P:(k + 1) * P],
                                 hi[:, k, 0:n], lo[:, k, 0:n], k == 0, k == nk - 1)
                return last

            def narrow(s):
                pe.wait_ge(first_full[s], 1).then_inc(first_full[s], -1)
                pe.wait_ge(acc_free[s], 1).then_inc(acc_free[s], -1)
                for k in range(KT):
                    if k == KT // 2:
                        pe.wait_ge(split_full[s], 1).then_inc(split_full[s], -1)
                    last = prod3(ps[:, s, 0:CAP], w_hi[:, s, k * P:(k + 1) * P], w_lo[:, s, k * P:(k + 1) * P],
                                 hg[:, k, 0:CAP], hg[:, k, CAP:2 * CAP], k == 0, k == KT - 1)
                    if k == KT // 2 - 1:
                        last.then_inc(half_free[s], 1)
                return last

            def gather(alone=False):
                for f in range(KT):
                    if f == 6 or alone and f == 7:
                        pe.wait_ge(act_pe, 1).then_inc(act_pe, -1)
                    elif f == 7:
                        pe.wait_ge(dve_pe, 1).then_inc(dve_pe, -1)
                    for h, part in enumerate((H_hi, H_lo)):
                        for t in range(TT):
                            last = mm(ps[:, GB[f], h * CAP:(h + 1) * CAP], part[:, t, f * P:(f + 1) * P], Pm[:, t, :],
                                      start=(t == 0), stop=(t == TT - 1))
                    last.then_inc(to_act if alone or f % 2 == 0 else to_dve, 1)
                for _ in range(2):
                    pe.wait_ge(act_pe, 1).then_inc(act_pe, -1)
                    if alone:
                        pe.wait_ge(act_pe, 1).then_inc(act_pe, -1)
                    else:
                        pe.wait_ge(dve_pe, 1).then_inc(dve_pe, -1)

            def slots():
                for st in range(ST):
                    for t in range(TT):
                        last = nc.tensor.transpose(ps[:, 6 + st, t * P:(t + 1) * P],
                                                   Pm[:, t, st * P:(st + 1) * P].bitcast(F32), ident)
                    last.then_inc(to_act, 1)
                for st in range(ST):
                    pe.wait_ge(act_pe, 1).then_inc(act_pe, -1)
                for st in range(ST):
                    for t in range(TT):
                        last = mm(ps[:, 6, st:st + 1], Pm[:, t, st * P:(st + 1) * P].bitcast(F32), cj[:, t:t + 1],
                                  start=(t == 0), stop=(t == TT - 1))
                last.then_inc(to_dve, 1)

            def sumsq(n=SEQ, b=2):
                for k in range(KT):
                    pe.wait_ge(act_pe, 1).then_inc(act_pe, -1)
                    mm(ps[:, b, 0:n], C[:, C_ONE:C_ONE + P], (tA, tE)[k % 2][:, 0:n],
                       start=(k == 0), stop=(k == KT - 1)).then_inc(to_act, 1)

            def both(o, a, b, n):
                for h in range(2):
                    q = slice(h * HD, (h + 1) * HD)
                    last = mm(o(q), a(q), b(q), start=True, stop=True)
                return last

            def cs(n):
                return slice(n * CH, (n + 1) * CH)

            pe.wait_ge(load_cst, 16)
            for s in range(2):
                pe.sem_inc(acc_free[s], 1)
            sumsq()
            with pe.Fori(0, DEPTH) as lay:
                pe.wait_ge(load_sm, 16).then_inc(load_sm, -16)
                for s in range(2):
                    unit(s, h_hi, h_lo, fresh=(s == 0)).then_inc(to_dve, 1)
                for b in range(2):
                    pe.wait_ge(dve_pe, 1).then_inc(dve_pe, -1)
                    mm(ps[:, 2 + b, :], wsmall[:, b * P:(b + 1) * P], (tB, tC)[b][:, :],
                       start=True, stop=True).then_inc(to_dve, 1)
                for s in range(2):
                    pe.wait_ge(split_full[s], 1).then_inc(split_full[s], -1)
                    if s == 0:
                        pe.wait_ge(dve_pe, 1).then_inc(dve_pe, -1)
                    for t in range(TT):
                        for k in range(4):
                            last = prod3(ps[:, 2 + t, 0:256], h_hi[:, 4 * s + k, t * P:(t + 1) * P],
                                         h_lo[:, 4 * s + k, t * P:(t + 1) * P],
                                         w_hi[:, s, k * 256:(k + 1) * 256], w_lo[:, s, k * 256:(k + 1) * 256],
                                         s == 0 and k == 0, s == 1 and k == 3)
                    last.then_inc(to_act, 1)
                pe.wait_ge(act_pe, 1).then_inc(act_pe, -1)
                for s in range(2):
                    unit(s, h_hi, h_lo).then_inc(to_dve, 1)

                def beta_alpha(i):
                    k, part = i // 2, (h_lo, h_hi)[i % 2]
                    return mm(ps[0:16, 2, :], wsmall[:, 2 * P + k * 16:2 * P + (k + 1) * 16], part[:, k, :].bitcast(F32),
                              start=(i == 0), stop=(i == 2 * KT - 1))

                for pair in range(MOBA_PAIRS):
                    for s in range(2):
                        pe.wait_ge(dve_pe, 1).then_inc(dve_pe, -1)
                        mm(ps[:, 2 + s, :], C[:, C_ROT:C_ROT + P], (qT, kT)[s], start=True, stop=True).then_inc(to_dve, 1)
                    pe.wait_ge(dve_pe, 1).then_inc(dve_pe, -1)
                    for i in range(-1, len(STEPS) + 1):
                        if i + 1 < len(STEPS):
                            h, t = STEPS[i + 1]
                            q = slice(h * HD, (h + 1) * HD)
                            mm(ps[:, 3 + 3 * ((i + 1) % 2), 0:(t + 1) * P], qT[q, t * P:(t + 1) * P], kT[q, 0:(t + 1) * P],
                               start=True, stop=True).then_inc(to_dve, 1)
                        if pair < MOBA_PAIRS - 1 and i in (1, 3):
                            unit(i // 2, h_hi, h_lo).then_inc(split_free[i // 2], 1)
                        if pair == MOBA_PAIRS - 1 and 0 <= i < len(STEPS):
                            beta_alpha(2 * i)
                            if i < len(STEPS) - 1:
                                beta_alpha(2 * i + 1)
                        if 0 <= i < len(STEPS):
                            h, t = STEPS[i]
                            pe.wait_ge(dve_pe, 1).then_inc(dve_pe, -1)
                            for k in range(t + 1):
                                last = nc.tensor.transpose(ps[:, 4 + 3 * (i % 2), k * P:(k + 1) * P],
                                                           pr[:, i % 2, k * P:(k + 1) * P], ident)
                            last.then_inc(to_act, 1)
                        if i >= 1:
                            h, t = STEPS[i - 1]
                            q = slice(h * HD, (h + 1) * HD)
                            pe.wait_ge(act_pe, 1).then_inc(act_pe, -1)
                            for k in range(t + 1):
                                last = mm(ps[q, 5, t * P:(t + 1) * P], vh[:, k, q], pT[:, (i - 1) % 2, k, :],
                                          start=(k == 0), stop=(k == t))
                    last.then_inc(to_dve, 1)
                    pe.wait_ge(dve_pe, 1).then_inc(dve_pe, -1)
                beta_alpha(2 * KT - 1).then_inc(to_act, 1)
                pe.wait_ge(act_pe, 1).then_inc(act_pe, -1)
                for n in range(NC):
                    for h in range(2):
                        last = mm(ps[h * CH:(h + 1) * CH, 3, n * 16:(n + 1) * 16], baT[0:16, cs(n)], ident[0:16, 0:16],
                                  start=True, stop=True)
                last.then_inc(to_dve, 1)
                pe.wait_ge(dve_pe, 1).then_inc(dve_pe, -1)
                mm(ps[:, 2, 0:32], C[:, C_UB:C_UB + P], tok[:, 0, :], start=True, stop=True)
                mm(ps[:, 2, 64:96], C[:, C_VB:C_VB + P], tok[:, 0, :], start=True, stop=True)
                mm(ps[:, 2, 128:160], C[:, C_BONE:C_BONE + P], tok[:, 0, :], start=True, stop=True).then_inc(to_act, 1)
                pe.wait_ge(act_pe, 1).then_inc(act_pe, -1)
                with pe.Fori(0, PAIRS // 2):
                    for u in range(2):
                        unit(u, h_hi, h_lo).then_inc(split_free[u], 1)
                    for g in range(2):
                        b = 2 + 3 * g
                        pe.wait_ge(dve_pe, 1).then_inc(dve_pe, -1)
                        mm(ps[:, b, :], C[:, C_UB:C_UB + P], flat(E1[g]), start=True, stop=True)
                        mm(ps[:, b + 1, :], C[:, C_VB:C_VB + P], flat(E2[g]), start=True, stop=True).then_inc(to_act, 1)
                    for g in range(2):
                        for u in range(2 if g == 0 else 0, 4):
                            unit(u % 2, h_hi, h_lo).then_inc(to_dve if u < 3 else to_act, 1)
                    for g in range(2):
                        for u in range(2):
                            pe.wait_ge(act_pe, 1).then_inc(act_pe, -1)
                            mm(ps[:, 2 + 3 * g + u, :], C[:, C_BONE:C_BONE + P], sqs[g][u], start=True, stop=True).then_inc(to_act, 1)
                        pe.wait_ge(act_pe, 1).then_inc(act_pe, -1)
                    for g in range(2):
                        pe.wait_ge(acc_free[g], 1).then_inc(acc_free[g], -1)
                        for n in range(NC):
                            last = both(lambda q: ps[q, g, cs(n)], lambda q: Vv[g][q, cs(n)], lambda q: id64[q, :], CH)
                        last.then_inc(to_dve, 1)
                    for g in range(2):
                        b = 2 + 3 * g
                        pe.wait_ge(dve_pe, 1).then_inc(dve_pe, -1)
                        for n in range(NC):
                            both(lambda q: ps[q, b, cs(n)], lambda q: Kt[g][q, cs(n)], lambda q: Kt[g][q, cs(n)], CH)
                            both(lambda q: ps[q, b + 1, cs(n)], lambda q: Kt[g][q, cs(n)], lambda q: Qt[g][q, cs(n)], CH)
                            last = both(lambda q: ps[q, b + 2, cs(n)], lambda q: Kt[g][q, cs(n)], lambda q: id64[q, :], CH)
                        last.then_inc(to_dve, 1)
                    for g in range(2):
                        pe.wait_ge(dve_pe, 1).then_inc(dve_pe, -1)
                        for n in range(NC):
                            last = both(lambda q: ps[q, 2 + 3 * g, cs(n)], lambda q: A_[g][q, n, :], lambda q: id64[q, :], CH)
                        last.then_inc(to_dve, 1)
                    for l in range(1, LEVELS):
                        for g in range(2):
                            pe.wait_ge(dve_pe, 1).then_inc(dve_pe, -1)
                            for n in range(NC):
                                last = both(lambda q: ps[q, 2 + 3 * g, cs(n)], lambda q: MT[g][q, n, :],
                                            lambda q: XX[g][q, n, :], CH)
                            last.then_inc(to_act, 1)
                        for g in range(2):
                            if l == 1:
                                pe.wait_ge(dve_pe, 1).then_inc(dve_pe, -1)
                            pe.wait_ge(act_pe, 1).then_inc(act_pe, -1)
                            if l < LEVELS - 1:
                                for n in range(NC):
                                    last = both(lambda q: ps[q, 3 + 3 * g, cs(n)], lambda q: XT[g][q, n, :],
                                                lambda q: P1[g][q, n, :], CH)
                                last.then_inc(to_dve, 1)
                            for n in range(NC):
                                last = both(lambda q: ps[q, 4 + 3 * g, cs(n)], lambda q: P1[g][q, n, :],
                                            lambda q: XT[g][q, n, :], CH)
                            last.then_inc(to_dve, 1)
                    for g in range(2):
                        pe.wait_ge(dve_pe, 1).then_inc(dve_pe, -1)
                        for n in range(NC):
                            both(lambda q: ps[q, 2 + 3 * g, cs(n)], lambda q: XT[g][q, n, :], lambda q: vb[g][q, n, :], CH)
                            last = both(lambda q: ps[q, 3 + 3 * g, cs(n)], lambda q: kg[g][q, n, :], lambda q: XT[g][q, n, :], CH)
                        last.then_inc(to_act, 1)
                    for n in range(NC):
                        for g in range(2):
                            b = 2 + 3 * g
                            if n == 0:
                                pe.wait_ge(act_pe, 1).then_inc(act_pe, -1)
                            else:
                                pe.wait_ge(dve_pe, 1).then_inc(dve_pe, -1)
                            both(lambda q: ps[q, b, 0:CH], lambda q: wT[g][q, n, :], lambda q: St[g][q, :], CH).then_inc(to_dve, 1)
                            both(lambda q: ps[q, b + 1, 0:CH], lambda q: Qt[g][q, cs(n)], lambda q: St[g][q, :], CH).then_inc(to_dve, 1)
                        for g in range(2):
                            b = 2 + 3 * g
                            pe.wait_ge(dve_pe, 1).then_inc(dve_pe, -1)
                            both(lambda q: ps[q, b + 2, 0:CH], lambda q: kd[g][q, n, :], lambda q: vn[g][q, :], CH).then_inc(to_dve, 1)
                            both(lambda q: ps[q, b, 0:CH], lambda q: aq[g][q, n, :], lambda q: vn[g][q, :], CH).then_inc(to_dve, 1)
                    for g in range(2):
                        pe.wait_ge(dve_pe, 1).then_inc(dve_pe, -1)
                    for g in range(2):
                        pe.wait_ge(dve_pe, 1).then_inc(dve_pe, -1)
                        for n in range(NC):
                            last = both(lambda q: ps[q, 2 + 3 * g, cs(n)], lambda q: oo[g][q, n, :], lambda q: id64[q, :], CH)
                        last.then_inc(to_dve, 1)
                    for g in range(2):
                        pe.wait_ge(dve_pe, 1).then_inc(dve_pe, -1)
                with pe.Fori(0, KT):
                    for s in (0, 1, 0):
                        unit(s, h_hi, h_lo).then_inc(to_act, 1)
                    pe.wait_ge(split_full[1], 1).then_inc(split_full[1], -1)
                    pe.wait_ge(dve_pe, 1).then_inc(dve_pe, -1)
                    for br, (k0, k1) in enumerate(((0, 2), (2, 4), (4, 8))):
                        for k in range(k0, k1):
                            last = prod3(ps[:, 2 + br, :], w_hi[:, 1, k * P:(k + 1) * P], w_lo[:, 1, k * P:(k + 1) * P],
                                         B_hi[:, k, :], B_lo[:, k, :], k == k0, k == k1 - 1)
                    last.then_inc(to_dve, 1)
                sumsq(MEM, 3)
                pe.wait_ge(dve_pe, 1).then_inc(dve_pe, -1)
                with pe.Fori(0, KT // 2):
                    for s in range(2):
                        unit(s, M_hi, M_lo).then_inc(to_dve, 1)
                sumsq()
                for u in range(4):
                    s = u % 2
                    pe.wait_ge(split_full[s], 1).then_inc(split_full[s], -1)
                    for t in range(2):
                        for k in range(2):
                            last = prod3(ps[:, 4 + t, :], N_hi[:, 2 * u + k, t * P:(t + 1) * P],
                                         N_lo[:, 2 * u + k, t * P:(t + 1) * P],
                                         w_hi[:, s, k * SEQ:(k + 1) * SEQ], w_lo[:, s, k * SEQ:(k + 1) * SEQ],
                                         u == 0 and k == 0, u == 3 and k == 1)
                    last.then_inc(to_act, 1)
                pe.wait_ge(act_pe, 1).then_inc(act_pe, -1)
                unit(0, h_hi, h_lo, fresh=True).then_inc(to_dve, 1)
                unit(1, N_hi, N_lo, MEM).then_inc(to_dve, 1)

                def head(more):
                    pe.wait_ge(dve_pe, 1).then_inc(dve_pe, -1)
                    for t in range(-1, TT):
                        if t + 1 < TT:
                            mm(ps[:, 3 + 3 * ((t + 1) % 2), 0:MEM], xq[:, (t + 1) * P:(t + 2) * P], xk,
                               start=True, stop=True).then_inc(to_dve, 1)
                        if more and t == 0:
                            unit(0, h_hi, h_lo).then_inc(split_free[0], 1)
                        if more and t == 1:
                            unit(1, N_hi, N_lo, MEM).then_inc(split_free[1], 1)
                        if t >= 0:
                            if t >= 2:
                                pe.wait_ge(act_pe, 1).then_inc(act_pe, -1)
                            pe.wait_ge(dve_pe, 1).then_inc(dve_pe, -1)
                            for k in range(2):
                                last = nc.tensor.transpose(ps[:, 4 + 3 * (t % 2), k * P:(k + 1) * P],
                                                           xp[:, t % 2, k * P:(k + 1) * P], ident)
                            last.then_inc(to_act, 1)
                    for _ in range(2):
                        pe.wait_ge(act_pe, 1).then_inc(act_pe, -1)
                    for k in range(2):
                        last = mm(ps[:, 5, :], xvh[:, k, :], xpT[:, k, :], start=(k == 0), stop=(k == 1))
                    last.then_inc(to_dve, 1)
                    pe.wait_ge(dve_pe, 1).then_inc(dve_pe, -1)

                with pe.Fori(0, XH - 1):
                    head(True)
                head(False)
                with pe.Fori(0, KT // 4):
                    for s in range(2):
                        pe.wait_ge(split_full[s], 1).then_inc(split_full[s], -1)
                        pe.wait_ge(acc_free[s], 1).then_inc(acc_free[s], -1)
                        for j in range(2):
                            for k in range(4):
                                c = (j * 4 + k) * P
                                last = prod3(ps[:, (s, 2 + s)[j], :], w_hi[:, s, c:c + P], w_lo[:, s, c:c + P],
                                             B_hi[:, k, :], B_lo[:, k, :], k == 0, k == 3)
                        last.then_inc(to_dve, 1)
                sumsq()
                pe.wait_ge(dve_pe, 1).then_inc(dve_pe, -1)
                for i in range(2 * TT):
                    t, b = i // 2, 2 + i % 2
                    if i >= 2:
                        pe.wait_ge(dve_pe, 1).then_inc(dve_pe, -1)
                    for a in range(4):
                        last = nc.tensor.transpose(ps[:, b, a * P:(a + 1) * P],
                                                   hF[:, (i % 2) * 4 + a, t * P:(t + 1) * P], ident)
                    last.then_inc(to_act, 1)
                for t in range(TT):
                    for k in range(KT):
                        c = 2 * P + KT * 16 + k * NE
                        last = mm(ps[:, 4 + t, 0:NE], hF[:, k, t * P:(t + 1) * P], wsmall[:, c:c + NE],
                                  start=(k == 0), stop=(k == KT - 1))
                last.then_inc(to_dve, 1)
                for _ in range(3):
                    pe.wait_ge(dve_pe, 1).then_inc(dve_pe, -1)
                for t in range(TT):
                    for u in range(t + 1):
                        mm(ps[:, 4, t * NE:(t + 1) * NE], C[:, C_SU:C_SU + P] if u == t else C[:, C_ONE:C_ONE + P],
                           mask[:, u, :], start=(u == 0), stop=(u == t))
                for u in range(TT):
                    last = mm(ps[:, 4, TT * NE:(TT + 1) * NE], C[:, C_ONE:C_ONE + P], mask[:, u, :],
                              start=(u == 0), stop=(u == TT - 1))
                last.then_inc(to_dve, 1)
                for s in range(2):
                    pe.wait_ge(split_full[s], 1).then_inc(split_full[s], -1)
                    pe.sem_inc(first_full[s], 1)
                    pe.sem_inc(split_full[s], 1)
                pe.wait_ge(dve_pe, 1).then_inc(dve_pe, -1)
                gather(alone=True)
                for _ in range(2):
                    pe.wait_ge(act_pe, 1).then_inc(act_pe, -1)
                slots()
                pe.wait_ge(dve_pe, 1).then_inc(dve_pe, -1)
                n_jobs = pe.value_load(jobs[0:1, NQ + 1:NQ + 2], min_val=1, max_val=NQ)
                with pe.Fori(0, n_jobs):
                    with pe.Fori(0, FT):
                        narrow(0).then_inc(to_act, 1)
                        narrow(1).then_inc(to_dve, 1)
                    pe.wait_ge(dve_pe, 1).then_inc(dve_pe, -1)
                    gather()
                    pe.wait_ge(hidden_ready, 1).then_inc(hidden_ready, -1)
                    for f in range(FT):
                        s = f % 2
                        for half in range(2):
                            pe.wait_ge(split_full[s] if half else first_full[s], 1).then_inc(split_full[s] if half else first_full[s], -1)
                            for st in range(ST):
                                c = slice(half * HALF, (half + 1) * HALF)
                                last = prod3(ps[:, 2 + 2 * st + half, :], hh[:, f, st * P:(st + 1) * P],
                                             hh[:, f, CAP + st * P:CAP + (st + 1) * P], w_hi[:, s, c], w_lo[:, s, c],
                                             f == 0, f == FT - 1)
                                if f == FT - 1:
                                    last.then_inc(to_act, 1)
                            if f < FT - 1:
                                last.then_inc(split_free[s] if half else half_free[s], 1)
                    pe.wait_ge(first_full[1], 1).then_inc(first_full[1], -1)
                    pe.wait_ge(split_full[1], 1).then_inc(split_full[1], -1)
                    pe.sem_inc(half_free[1], 1)
                    pe.sem_inc(split_free[1], 1)
                    pe.wait_ge(acc_free[0], 1).then_inc(acc_free[0], -1)
                    pe.wait_ge(acc_free[1], 1).then_inc(acc_free[1], -1)
                    pe.wait_ge(act_pe, 1).then_inc(act_pe, -1)
                    pe.wait_ge(dve_pe, 1).then_inc(dve_pe, -1)
                    for f in range(KT):
                        if f % 4 == 0:
                            for st in range(ST):
                                pe.wait_ge(dve_pe, 1).then_inc(dve_pe, -1)
                        for part in (Y_lo, Y_hi):
                            for st in range(ST):
                                last = mm(ps[:, SB[f], :], part[:, st, f * P:(f + 1) * P], PT[:, st, :],
                                          start=(part is Y_lo and st == 0), stop=(part is Y_hi and st == ST - 1))
                        last.then_inc(to_dve, 1)
                    pe.wait_ge(dve_pe, 1).then_inc(dve_pe, -1)
                    slots()
                    pe.wait_ge(dve_pe, 1).then_inc(dve_pe, -1)
                for s in range(2):
                    pe.wait_ge(first_full[s], 1).then_inc(first_full[s], -1)
                sumsq()

        @block.scalar
        def _(act):
            def fn(out, in_, f, *posts, **kw):
                nc.scalar.activation(out, in_, f, **kw).then_inc(act_own, 1)
                act.wait_ge(act_own, 1).then_inc(act_own, -1)
                for p in posts:
                    act.sem_inc(p, 1)

            def rsqrt(out, in_, scale, *posts):
                fn(out, in_, ACT.Ln, scale=scale, bias=C[0:out.shape[0], C_EPS:C_EPS + 1])
                fn(out, out, ACT.Exp, *posts, scale=-0.5)

            def norm_high(k):
                act.wait_ge(dve_act, 1).then_inc(dve_act, -1)
                fn(h_hi[:, k, :], (tB, tC)[k % 2][:, :], ACT.Copy, act_dve)

            def norm(src, n=SEQ, b=2):
                act.preload_act_table_set("natural_log_exp_and_others")
                for k in range(KT):
                    if k >= 2:
                        act.wait_ge(to_act, 1).then_inc(to_act, -1)
                    fn((tA, tE)[k % 2][:, 0:n], src[:, k, 0:n], ACT.Square, act_pe)
                for _ in range(2):
                    act.wait_ge(to_act, 1).then_inc(to_act, -1)
                rsqrt(rinv[:, 0:n], ps[:, b, 0:n], 1.0 / D, act_dve)

            def high(s, turn):
                act.wait_ge(raw_full[s], 1).then_inc(raw_full[s], -1)
                act.wait_ge(split_free[s], 1).then_inc(split_free[s], -1)
                nc.scalar.activation(w_hi[:, s, :], raw_of(s, turn), ACT.Copy).then_inc(hi_full[s], 1)

            def high1(s, turn):
                act.wait_ge(raw_full[s], 1).then_inc(raw_full[s], -1)
                act.wait_ge(half_free[s], 1).then_inc(half_free[s], -1)
                nc.scalar.activation(w_hi[:, s, 0:HALF], raw_of(s, turn, slice(0, HALF)), ACT.Copy).then_inc(high_full[s], 1)

            def high2(s, turn):
                act.wait_ge(split_free[s], 1).then_inc(split_free[s], -1)
                nc.scalar.activation(w_hi[:, s, HALF:UNIT], raw_of(s, turn, slice(HALF, UNIT)), ACT.Copy) \
                    .then_inc(high_full[s], 1)

            def gathered(step):
                for f in range(0, KT, step):
                    act.wait_ge(to_act, 1).then_inc(to_act, -1)
                    fn(hg[:, f, :], ps[:, GB[f], :], ACT.Copy, act_pe)

            def slots():
                for st in range(ST):
                    act.wait_ge(to_act, 1).then_inc(to_act, -1)
                    fn(PT[:, st, :], ps[:, 6 + st, :], ACT.Copy, act_pe)

            for s in range(2):
                act.sem_inc(split_free[s], 1)
            act.wait_ge(load_cst, 16)
            for s in range(2):
                high(s, 0)
            act.wait_ge(load_x, 16)
            norm(X)
            for t in (ropeC, ropeS):
                act.wait_ge(dve_act, 1).then_inc(dve_act, -1)
                fn(t[:, :], t[:, :], ACT.Sin, rope_ready)
            with act.Fori(0, DEPTH) as lay:
                for k in range(KT):
                    norm_high(k)
                for s in range(2):
                    high(s, 1)
                for s in range(2):
                    act.wait_ge(to_act, 1).then_inc(to_act, -1)
                    act.sem_inc(split_free[s], 1)
                    if s == 1:
                        fn(Vt, ps[:, 2:6, 0:256], ACT.Copy, act_pe)
                    high(s, 0)
                for s in range(2):
                    high(s, 1)
                for pair in range(MOBA_PAIRS):
                    for i in range(len(STEPS) + 1):
                        if i < len(STEPS):
                            b, n = i % 2, (STEPS[i][1] + 1) * P
                            act.wait_ge(dve_act, 1).then_inc(dve_act, -1)
                            fn(pr[:, b, 0:n], sc[:, b, 0:n], ACT.Exp, act_dve, bias=stat[:, b, 0:1],
                               accum_out=stat[:, b, 1:2])
                        if pair < MOBA_PAIRS - 1 and i in (2, 4):
                            high(i // 2 - 1, 0)
                        if i > 0:
                            b, nk = (i - 1) % 2, STEPS[i - 1][1] + 1
                            act.wait_ge(to_act, 1).then_inc(to_act, -1)
                            fn(pT[:, b, 0:nk, :].rearrange("p a b -> p (a b)"), ps[:, 4 + 3 * b, 0:nk * P], ACT.Copy, act_pe)
                act.wait_ge(to_act, 1).then_inc(to_act, -1)
                fn(baT[0:16, :], ps[0:16, 2, :], ACT.Copy, act_pe)
                act.wait_ge(dve_act, 1).then_inc(dve_act, -1)
                fn(spl[:, 0], spl[:, 0], ACT.Exp)
                fn(spl[:, 0], spl[:, 0], ACT.Ln, bias=C[:, C_ONE:C_ONE + 1])
                fn(ealog, vecs[:, V_ALOG:V_ALOG + PAIRS], ACT.Exp)
                fn(spl[:, 1], ba[:, 0], ACT.Exp, act_dve, scale=-1.0)
                act.wait_ge(to_act, 1).then_inc(to_act, -1)
                fn(tok[:, 3, :], ps[:, 2, 0:32], ACT.Exp)
                fn(tok[:, 4, :], ps[:, 2, 64:96], ACT.Exp)
                fn(tok[:, 5, :], ps[:, 2, 128:160], ACT.Exp, act_pe, act_dve)
                with act.Fori(0, PAIRS // 2):
                    act.preload_act_table_set("natural_log_exp_and_others")
                    for s in range(2):
                        high(s, 1)
                    for g in range(2):
                        act.wait_ge(to_act, 1).then_inc(to_act, -1)
                        fn(flat(E1[g]), ps[:, 2 + 3 * g, :], ACT.Exp)
                        fn(flat(E2[g]), ps[:, 3 + 3 * g, :], ACT.Exp, act_dve)
                    act.preload_act_table(ACT.Silu)
                    for g in range(2):
                        for u in range(3):
                            if g == 1 or u == 2:
                                high(u % 2, (1, 1, 0)[u])
                            act.wait_ge(dve_act, 1).then_inc(dve_act, -1)
                            y = (Qt[g], Kt[g], Vv[g])[u]
                            fn(y, (tB, tC, tD)[u][:, :], ACT.Silu, *((conv_read,) if g == 0 else ()), *((act_pe,) if u == 2 else ()))
                            if u < 2:
                                fn(sqs[g][u], y, ACT.Square, act_pe)
                        act.wait_ge(to_act, 1).then_inc(to_act, -1)
                        act.sem_inc(split_free[1], 1)
                        fn(zz[g], ps[:, 1, :], ACT.Silu, acc_free[1])
                        high(1, 0)
                    act.preload_act_table_set("natural_log_exp_and_others")
                    for g in range(2):
                        for u in range(2):
                            act.wait_ge(to_act, 1).then_inc(to_act, -1)
                            rsqrt(sqs[g][u], ps[:, 2 + 3 * g + u, :], 1.0, act_dve)
                    for l in range(1, LEVELS):
                        for g in range(2):
                            act.wait_ge(to_act, 1).then_inc(to_act, -1)
                            fn(flat(P1[g]), ps[:, 2 + 3 * g, :], ACT.Copy, act_pe)
                    for g in range(2):
                        act.wait_ge(to_act, 1).then_inc(to_act, -1)
                        fn(flat(Uu[g]), ps[:, 2 + 3 * g, :], ACT.Copy)
                        fn(flat(wT[g]), ps[:, 3 + 3 * g, :], ACT.Copy, act_pe)
                    for g in range(2):
                        act.wait_ge(dve_act, 1).then_inc(dve_act, -1)
                        rsqrt(ost[g], ost[g], 1.0 / HD, act_dve)
                act.wait_ge(dve_act, 1).then_inc(dve_act, -1)
                act.dma_start(memx, mem_t).then_inc(load_mem, 16)
                act.preload_act_table(ACT.Sigmoid)
                with act.Fori(0, KT):
                    act.wait_ge(dve_act, 1).then_inc(dve_act, -1)
                    for b, s in enumerate((0, 1, 0)):
                        act.wait_ge(to_act, 1).then_inc(to_act, -1)
                        act.sem_inc(split_free[s], 1)
                        fn(gts[b][:, :], ps[:, s, :], ACT.Sigmoid, acc_free[s], act_dve)
                        high(s, (1, 1, 0)[b])
                    high(1, 0)
                act.wait_ge(dve_act, 1).then_inc(dve_act, -1)
                act.wait_ge(load_mem, 16).then_inc(load_mem, -16)
                norm(memx, MEM, 3)
                with act.Fori(0, KT // 2) as i:
                    for s in range(2):
                        high(s, (i + 1) % 2)
                act.wait_ge(dve_act, 1).then_inc(dve_act, -1)
                norm(X)
                for u in range(4):
                    norm_high(2 * u)
                    act.wait_ge(to_act, 1).then_inc(to_act, -1)
                    act.sem_inc(split_free[u % 2], 1)
                    norm_high(2 * u + 1)
                    if u == 3:
                        fn(xv, ps[:, 4:6, :], ACT.Copy, act_pe)
                    high(u % 2, 1 - u // 2)
                for s in range(2):
                    high(s, 1)

                def head(turn):
                    for t in range(TT + 1):
                        if t < TT:
                            b = t % 2
                            act.wait_ge(dve_act, 1).then_inc(dve_act, -1)
                            fn(xp[:, b], ps[:, 3 + 3 * b, 0:MEM], ACT.Exp, act_dve, bias=xst[:, b, 0:1],
                               scale=float(P) ** -0.5, accum_out=xst[:, b, 1:2])
                        if turn is not None and t in (1, 2):
                            high(t - 1, turn)
                        if t > 0:
                            b = (t - 1) % 2
                            act.wait_ge(to_act, 1).then_inc(to_act, -1)
                            fn(xpT[:, :, (t - 1) * P:t * P], ps[:, 4 + 3 * b, 0:MEM].rearrange("p (a b) -> p a b", a=2),
                               ACT.Copy, act_pe)

                with act.Fori(0, XH - 1) as h:
                    head(h % 2)
                head(None)
                with act.Fori(0, KT // 4) as i:
                    for s in range(2):
                        high(s, (i + 1) % 2)
                act.wait_ge(dve_act, 1).then_inc(dve_act, -1)
                norm(X)
                for i in range(2 * TT):
                    act.wait_ge(to_act, 1).then_inc(to_act, -1)
                    fn(H_hi[:, i // 2, (i % 2) * SEQ:(i % 2 + 1) * SEQ], ps[:, 2 + i % 2, :], ACT.Copy, act_dve)
                act.wait_ge(dve_act, 1).then_inc(dve_act, -1)
                fn(m3, m3, ACT.Exp, act_dve)
                act.preload_act_table(ACT.Silu)
                gathered(1)
                slots()
                act.wait_ge(dve_act, 1).then_inc(dve_act, -1)
                n_jobs = act.value_load(jobs[0:1, NQ + 1:NQ + 2], min_val=1, max_val=NQ)
                with act.Fori(0, n_jobs) as j:
                    with act.Fori(0, FT) as i:
                        turn = act.snap((j + i + 1) % 2, min_val=0, max_val=1)
                        high1(0, turn)
                        act.wait_ge(to_act, 1).then_inc(to_act, -1)
                        act.sem_inc(split_free[0], 1)
                        fn(gu, ps[:, 0, 0:CAP], ACT.Silu, acc_free[0], act_dve)
                        high2(0, turn)
                        high1(1, turn)
                        high2(1, turn)
                        act.wait_ge(dve_act, 1).then_inc(dve_act, -1)
                        fn(hh[:, bass.ds(i, 1), 0:CAP].rearrange("p a n -> p (a n)"), hid, ACT.Copy, act_pool)
                    gathered(2)
                    with act.Fori(0, FT // 2) as i:
                        turn = act.snap((j + i) % 2, min_val=0, max_val=1)
                        for s in range(2):
                            high1(s, turn)
                            high2(s, turn)
                    for half in range(2):
                        for st in range(ST):
                            act.wait_ge(to_act, 1).then_inc(to_act, -1)
                            if st == ST - 1:
                                act.sem_inc(split_free[0] if half else half_free[0], 1)
                            fn(Y_hi[:, st, half * SEQ:(half + 1) * SEQ], ps[:, 2 + 2 * st + half, :], ACT.Copy,
                               act_dve, scale=ws[:, st:st + 1])
                    for s in range(2):
                        high1(s, (j + 1) % 2)
                        high2(s, (j + 1) % 2)
                    slots()
                act.wait_ge(dve_act, 1).then_inc(dve_act, -1)
                norm(X)

        @block.vector
        def _(dve):
            V = nc.vector

            def v(ins, *posts):
                ins.then_inc(dve_own, 1)
                dve.wait_ge(dve_own, 1).then_inc(dve_own, -1)
                for p in posts:
                    dve.sem_inc(p, 1)

            def parts(src, hi, lo, *posts):
                v(V.tensor_copy(hi, src))
                v(V.tensor_tensor(lo, src, hi.bitcast(F32), ALU.subtract), *posts)

            def tile_of(t, i):
                return t[:, bass.ds(i, 1), :].rearrange("p a n -> p (a n)")

            def norm(g):
                dve.wait_ge(act_dve, 1).then_inc(act_dve, -1)

                def scaled(k):
                    V.scalar_tensor_tensor(out=(tB, tC)[k % 2][:, :], in0=X[:, k, :], scalar=vecs[:, g + k:g + k + 1],
                                           in1=rinv[:, :], op0=ALU.mult, op1=ALU.mult).then_inc(dve_act, 1)
                scaled(0)
                scaled(1)
                for k in range(KT):
                    dve.wait_ge(act_dve, 1).then_inc(act_dve, -1)
                    v(V.tensor_tensor(h_lo[:, k, :], (tB, tC)[k % 2][:, :], h_hi[:, k, :].bitcast(F32), ALU.subtract), dve_pe)
                    if k + 2 < KT:
                        scaled(k + 2)

            def rows(col, w):
                return C[:, None, col:col + w].to_broadcast([P, NC, w])

            def chan(g, i):
                return tk[g][:, i, :, None].to_broadcast([P, NC, CH])

            def bank(b):
                return chunked(ps[:, b, :])

            dve.sem_inc(dve_sp, 1)
            dve.wait_ge(load_cst, 16)
            dve.wait_ge(load_pos, 16)
            v(V.tensor_copy(tB[:, :], tD[:, :].bitcast(I32)))
            v(V.tensor_scalar(tB[:, :], tB[:, :], C[:, C_FREQ:C_FREQ + 1], None, ALU.mult))
            v(V.tensor_scalar(tC[:, :], tB[:, :], float(1 / (2 * np.pi)), MAGIC, ALU.mult, ALU.add))
            v(V.tensor_scalar(tC[:, :], tC[:, :], MAGIC, None, ALU.subtract))
            c1 = 6.28125
            c2 = float(np.float32(np.round((2 * np.pi - c1) * 2 ** 22) / 2 ** 22))
            c3 = float(2 * np.pi - c1 - c2)
            for c in (c1, c2, c3):
                v(V.scalar_tensor_tensor(out=tB[:, :], in0=tC[:, :], scalar=-c, in1=tB[:, :], op0=ALU.mult, op1=ALU.add))
            v(V.tensor_scalar(tC[:, :], tB[:, :], float(np.pi / 2), None, ALU.add))
            v(V.tensor_scalar(tD[:, :], tC[:, :], float(np.pi), -2 * float(np.pi), ALU.is_gt, ALU.mult))
            v(V.tensor_tensor(tC[:, :], tC[:, :], tD[:, :], ALU.add))
            for t, src in ((ropeC, tC), (ropeS, tB)):
                v(V.tensor_scalar(t[:, :], src[:, :], 3.14159, -3.14159, ALU.min, ALU.max), dve_act)
            with dve.Fori(0, DEPTH) as lay:
                dve.wait_ge(load_vec, 16).then_inc(load_vec, -16)
                norm(V_MIXG)
                for b in range(2):
                    v(V.memset(px[b][:, 0:16], 0.0))
                    v(V.memset(pw[b][:, 0:16], 0.0))
                    dve.wait_ge(to_dve, 1).then_inc(to_dve, -1)
                    dve.sem_inc(split_free[b], 1)
                    v(V.tensor_copy(px[b][:, 16:], ps[:, b, :]), acc_free[b])

                def shifted(o, i, sh, rows=slice(0, P)):
                    v(V.tensor_tensor(o[rows, :], i[rows, 16:], i[rows, 16 - sh:16 + SEQ - sh], ALU.add))
                lo_half, hi_half = slice(0, HD), slice(HD, P)
                for b, out in ((0, tB), (1, tC)):
                    shifted(pw[0][:, 16:], px[b], 1)
                    if b == 1:
                        shifted(pw[1][:, 16:], pw[0], 2)
                        shifted(pw[0][:, 16:], pw[1], 4)
                    v(V.tensor_copy(out[lo_half, :], pw[0][lo_half, 16:]))
                    shifted(out[:, :], pw[0], (2, 8)[b], hi_half)
                    v(V.tensor_tensor(out[:, :], out[:, :], C[:, C_CNT + b * SEQ:C_CNT + (b + 1) * SEQ], ALU.mult))
                    v(V.tensor_tensor(out[:, :], out[:, :], px[b][:, 16:], ALU.subtract), dve_pe)
                for b in range(2):
                    dve.wait_ge(to_dve, 1).then_inc(to_dve, -1)
                    v(V.tensor_scalar(tD[:, :], ps[:, 2 + b, :], vecs[:, V_POOLS + b:V_POOLS + b + 1], None, ALU.mult))
                    parts(tD[:, :], B_hi[:, b, :], B_lo[:, b, :])
                dve.sem_inc(dve_pe, 1)
                dve.wait_ge(rope_ready, 2)
                for s in range(2):
                    dve.wait_ge(to_dve, 1).then_inc(to_dve, -1)
                    dve.sem_inc(split_free[s], 1)
                with dve.Fori(0, MOBA_PAIRS) as j:
                    for s in range(2):
                        v(V.tensor_copy((qT, kT)[s], ps[:, s, :]), acc_free[s], dve_pe)
                    for s in range(2):
                        dve.wait_ge(to_dve, 1).then_inc(to_dve, -1)
                        x = (qT, kT)[s]
                        v(V.tensor_tensor(tB[:, :], ps[:, 2 + s, :], ropeS[:, :], ALU.mult))
                        v(V.tensor_tensor(x, x, ropeC[:, :], ALU.mult))
                        v(V.tensor_tensor(x, x, tB[:, :], ALU.add))
                    v(V.tensor_copy(vh, Vt[:, :, bass.ds(j * P, P)]), dve_pe)
                    for i in range(len(STEPS) + 1):
                        if i < len(STEPS):
                            b, n = i % 2, (STEPS[i][1] + 1) * P
                            dve.wait_ge(to_dve, 1).then_inc(to_dve, -1)
                            v(V.scalar_tensor_tensor(out=sc[:, b, 0:n], in0=ps[:, 3 + 3 * b, 0:n], scalar=float(HD) ** -0.5,
                                                     in1=C[:, C_CAUS + SEQ - n:C_CAUS + SEQ], op0=ALU.mult, op1=ALU.add))
                            v(V.tensor_reduce(stat[:, b, 0:1], sc[:, b, 0:n], AX.X, ALU.max, negate=True), dve_act)
                        if i > 0:
                            b, n = (i - 1) % 2, (STEPS[i - 1][1] + 1) * P
                            dve.wait_ge(act_dve, 1).then_inc(act_dve, -1)
                            v(V.reciprocal(stat[:, b, 2:3], stat[:, b, 1:2]))
                            v(V.tensor_scalar(pr[:, b, 0:n], pr[:, b, 0:n], stat[:, b, 2:3], None, ALU.mult), dve_pe)
                    dve.wait_ge(to_dve, 1).then_inc(to_dve, -1)
                    parts(ps[:, 5, :], tile_of(B_hi, j + 2), tile_of(B_lo, j + 2), dve_pe)
                dve.wait_ge(to_dve, 1).then_inc(to_dve, -1)
                for h in range(2):
                    q = slice(h * CH, (h + 1) * CH)
                    v(V.tensor_copy(ba[q].rearrange("p a b c -> p (a b) c"),
                                    ps[q, 3, 0:NC * 16].rearrange("p (n m h) -> p h m n", n=NC, h=2)[:, h]))
                dtb = vecs[:, V_DTB:V_DTB + PAIRS, None].to_broadcast([P, PAIRS, NC])
                v(V.tensor_tensor(spl[:, 2], ba[:, 1], dtb, ALU.add))
                v(V.scalar_tensor_tensor(out=spl[:, 0], in0=spl[:, 2], scalar=-1.0, in1=spl[:, 2], op0=ALU.mult, op1=ALU.min), dve_act)
                dve.wait_ge(act_dve, 1).then_inc(act_dve, -1)
                v(V.scalar_tensor_tensor(out=spl[:, 2], in0=spl[:, 2], scalar=0.0, in1=spl[:, 0], op0=ALU.max, op1=ALU.add))
                tg = tok[:, 0].rearrange("p (a b) -> p a b", a=PAIRS)
                v(V.scalar_tensor_tensor(out=tg, in0=spl[:, 2], scalar=-1.0, in1=ealog[:, :, None].to_broadcast([P, PAIRS, NC]),
                                         op0=ALU.mult, op1=ALU.mult), dve_pe)
                v(V.tensor_scalar(spl[:, 1], spl[:, 1], 1.0, None, ALU.add))
                v(V.reciprocal(tok[:, 1].rearrange("p (a b) -> p a b", a=PAIRS), spl[:, 1]))
                dve.wait_ge(act_dve, 1).then_inc(act_dve, -1)
                v(V.tensor_tensor(tok[:, 2], tok[:, 1], tok[:, 3], ALU.mult))
                with dve.Fori(0, PAIRS // 2) as j:
                    for g in range(2):
                        v(V.tensor_copy(tk[g], tok[:, :, bass.ds((j * 2 + g) * NC, NC)]))
                        v(V.tensor_copy(cw[g], vecs[:, bass.ds((j * 2 + g) * 12 + V_CONV, 12)]))
                        v(V.memset(St[g], 0.0))
                        v(V.memset(cv[g][:, :, 0:4], 0.0))
                        v(V.tensor_tensor(E1[g], rows(C_V64, CH), chan(g, 0), ALU.mult))
                        v(V.tensor_tensor(E2[g], rows(C_U64, CH), chan(g, 0), ALU.mult), dve_pe)
                    for g in range(2):
                        for u in range(3):
                            if g == 0 and u < 2:
                                dve.wait_ge(act_dve, 1).then_inc(act_dve, -1)
                            else:
                                dve.wait_ge(to_dve, 1).then_inc(to_dve, -1)
                                dve.sem_inc(split_free[u % 2], 1)
                            v(V.tensor_copy(cv[g][:, u, 4:], ps[:, u % 2, :]), acc_free[u % 2])
                            if g == 1:
                                dve.wait_ge(conv_read, 1).then_inc(conv_read, -1)
                            y = (tB, tC, tD)[u][:, :]
                            v(V.tensor_scalar(y, cv[g][:, u, 1:1 + SEQ], cw[g][:, u * 4:u * 4 + 1], None, ALU.mult))
                            for tap in range(1, 4):
                                v(V.scalar_tensor_tensor(out=y, in0=cv[g][:, u, 1 + tap:1 + tap + SEQ],
                                                         scalar=cw[g][:, u * 4 + tap:u * 4 + tap + 1], in1=y,
                                                         op0=ALU.mult, op1=ALU.add), *((dve_act,) if tap == 3 else ()))
                    for g in range(2):
                        v(V.tensor_tensor(E1[g], E1[g], rows(C_LOW, CH), ALU.mult))
                        v(V.tensor_tensor(E1[g], E1[g], chan(g, 1), ALU.mult))
                        v(V.tensor_tensor(E2[g], E2[g], rows(C_UPI, CH), ALU.mult))
                    for g in range(2):
                        dve.wait_ge(to_dve, 1).then_inc(to_dve, -1)
                        v(V.tensor_tensor(vb[g], bank(g), chan(g, 1), ALU.mult), acc_free[g])
                    for g in range(2):
                        dve.wait_ge(act_dve, 1).then_inc(act_dve, -1)
                        v(V.scalar_tensor_tensor(out=Qt[g], in0=Qt[g], scalar=float(HD) ** -0.5, in1=sqs[g][0],
                                                 op0=ALU.mult, op1=ALU.mult))
                        dve.wait_ge(act_dve, 1).then_inc(act_dve, -1)
                        v(V.tensor_tensor(Kt[g], Kt[g], sqs[g][1], ALU.mult), dve_pe)
                    for g in range(2):
                        b = 2 + 3 * g
                        dve.wait_ge(to_dve, 1).then_inc(to_dve, -1)
                        v(V.tensor_tensor(A_[g], bank(b), E1[g], ALU.mult), dve_pe)
                        v(V.tensor_tensor(aq[g], bank(b + 1), E2[g], ALU.mult))
                        v(V.tensor_tensor(kd[g], bank(b + 2), chan(g, 4), ALU.mult))
                        v(V.tensor_tensor(kg[g], bank(b + 2), chan(g, 2), ALU.mult))

                    for g in range(2):
                        dve.wait_ge(to_dve, 1).then_inc(to_dve, -1)
                        v(V.tensor_copy(AT[g], bank(2 + 3 * g)))
                        v(V.tensor_tensor(XX[g], A_[g], rows(C_LV1, CH), ALU.mult))
                        v(V.tensor_tensor(XX[g], rows(C_ID64, CH), XX[g], ALU.subtract))
                        v(V.tensor_tensor(MT[g], AT[g], rows(C_LVT + CH, CH), ALU.mult), dve_pe)
                    for g in range(2):
                        v(V.tensor_tensor(XT[g], AT[g], rows(C_LVT, CH), ALU.mult))
                        v(V.tensor_tensor(XT[g], rows(C_ID64, CH), XT[g], ALU.subtract), dve_pe)
                    for l in range(1, LEVELS):
                        for g in range(2):
                            if l < LEVELS - 1:
                                dve.wait_ge(to_dve, 1).then_inc(to_dve, -1)
                                v(V.tensor_tensor(XX[g], XX[g], bank(3 + 3 * g), ALU.subtract))
                                v(V.tensor_tensor(MT[g], AT[g], rows(C_LVT + (l + 1) * CH, CH), ALU.mult))
                            dve.wait_ge(to_dve, 1).then_inc(to_dve, -1)
                            v(V.tensor_tensor(XT[g], XT[g], bank(4 + 3 * g), ALU.subtract), dve_pe)
                    for n in range(NC):
                        for g in range(2):
                            dve.wait_ge(to_dve, 1).then_inc(to_dve, -1)
                            v(V.tensor_tensor(vn[g], Uu[g][:, n, :], ps[:, 2 + 3 * g, 0:CH], ALU.subtract), dve_pe)
                            dve.wait_ge(to_dve, 1).then_inc(to_dve, -1)
                            v(V.tensor_scalar(oo[g][:, n, :], ps[:, 3 + 3 * g, 0:CH], tk[g][:, 3, n:n + 1], None, ALU.mult))
                        for g in range(2):
                            dve.wait_ge(to_dve, 1).then_inc(to_dve, -1)
                            v(V.scalar_tensor_tensor(out=St[g], in0=St[g], scalar=tk[g][:, 5, n:n + 1],
                                                     in1=ps[:, 4 + 3 * g, 0:CH], op0=ALU.mult, op1=ALU.add))
                            dve.wait_ge(to_dve, 1).then_inc(to_dve, -1)
                            v(V.tensor_tensor(oo[g][:, n, :], oo[g][:, n, :], ps[:, 2 + 3 * g, 0:CH], ALU.add), dve_pe)
                    for g in range(2):
                        v(V.tensor_tensor(sq1[g], oo[g], oo[g], ALU.mult))
                        v(V.tensor_reduce(ost[g], sq1[g], AX.X, ALU.add), dve_act)
                    for g in range(2):
                        dve.wait_ge(act_dve, 1).then_inc(act_dve, -1)
                        v(V.tensor_tensor(oo[g], oo[g], ost[g][:, :, None].to_broadcast([P, NC, CH]), ALU.mult), dve_pe)
                    for g in range(2):
                        dve.wait_ge(to_dve, 1).then_inc(to_dve, -1)
                        v(V.scalar_tensor_tensor(out=tB[:, :], in0=ps[:, 2 + 3 * g, :], scalar=vecs[:, V_DNG:V_DNG + 1], in1=zz[g],
                                                 op0=ALU.mult, op1=ALU.mult))
                        parts(tB[:, :], tile_of(B_hi, j * 2 + g + 4), tile_of(B_lo, j * 2 + g + 4), dve_pe)
                dve.sem_inc(dve_pe, 1)
                dve.sem_inc(dve_act, 1)
                dve.sem_inc(dve_act, 1)
                with dve.Fori(0, KT) as n:
                    dve.wait_ge(to_dve, 1).then_inc(to_dve, -1)
                    dve.sem_inc(split_free[1], 1)
                    for b in range(3):
                        dve.wait_ge(act_dve, 1).then_inc(act_dve, -1)
                        v(V.tensor_tensor(gts[b][:, :], gts[b][:, :], ps[:, 2 + b, :], ALU.mult))
                    for b in (1, 2):
                        v(V.tensor_tensor(tB[:, :], tB[:, :], gts[b][:, :], ALU.add))
                    parts(tB[:, :], tile_of(M_hi, n), tile_of(M_lo, n), dve_pe, dve_act)
                dve.wait_ge(act_dve, 1).then_inc(act_dve, -1)
                v(V.tensor_copy(gmem, vecs[:, V_MEMG:V_MEMG + KT]))
                with dve.Fori(0, KT // 2) as i:
                    for s in range(2):
                        dve.wait_ge(to_dve, 1).then_inc(to_dve, -1)
                        dve.sem_inc(split_free[s], 1)
                        x = tile_of(X, i * 2 + s)
                        v(V.tensor_tensor(x, x, ps[:, s, :], ALU.add), acc_free[s])
                        v(V.scalar_tensor_tensor(out=tD[:, 0:MEM], in0=tile_of(memx, i * 2 + s), scalar=gmem[:, bass.ds(i * 2 + s, 1)],
                                                 in1=rinv[:, 0:MEM], op0=ALU.mult, op1=ALU.mult))
                        parts(tD[:, 0:MEM], tile_of(N_hi, i * 2 + s), tile_of(N_lo, i * 2 + s))
                dve.sem_inc(dve_act, 1)
                norm(V_XAG)
                for s in range(2):
                    dve.wait_ge(to_dve, 1).then_inc(to_dve, -1)
                    dve.sem_inc(split_free[s], 1)
                with dve.Fori(0, XH) as h:
                    v(V.tensor_copy(xq, ps[:, 0, :]), acc_free[0])
                    v(V.tensor_copy(xk, ps[:, 1, 0:MEM]), acc_free[1])
                    v(V.tensor_copy(xvh, xv[:, :, bass.ds(h * P, P)]), dve_pe)
                    for t in range(TT + 1):
                        if t < TT:
                            b = t % 2
                            dve.wait_ge(to_dve, 1).then_inc(to_dve, -1)
                            v(V.tensor_reduce(xst[:, b, 0:1], ps[:, 3 + 3 * b, 0:MEM], AX.X, ALU.max))
                            v(V.tensor_scalar(xst[:, b, 0:1], xst[:, b, 0:1], -float(P) ** -0.5, None, ALU.mult), dve_act)
                        if t > 0:
                            b = (t - 1) % 2
                            dve.wait_ge(act_dve, 1).then_inc(act_dve, -1)
                            v(V.reciprocal(xst[:, b, 2:3], xst[:, b, 1:2]))
                            v(V.tensor_scalar(xp[:, b], xp[:, b], xst[:, b, 2:3], None, ALU.mult), dve_pe)
                    dve.wait_ge(to_dve, 1).then_inc(to_dve, -1)
                    parts(ps[:, 5, :], tile_of(B_hi, h), tile_of(B_lo, h), dve_pe)
                with dve.Fori(0, KT // 4) as i:
                    for s in range(2):
                        dve.wait_ge(to_dve, 1).then_inc(to_dve, -1)
                        dve.sem_inc(split_free[s], 1)
                        for jj in range(2):
                            x = tile_of(X, i * 4 + 2 * s + jj)
                            v(V.tensor_tensor(x, x, ps[:, (s, 2 + s)[jj], :], ALU.add), *((acc_free[s],) if jj else ()))
                dve.sem_inc(dve_act, 1)
                dve.wait_ge(act_dve, 1).then_inc(act_dve, -1)
                for k in range(KT):
                    v(V.scalar_tensor_tensor(out=hF[:, k, :], in0=X[:, k, :], scalar=vecs[:, V_FFNG + k:V_FFNG + k + 1],
                                             in1=rinv[:, :], op0=ALU.mult, op1=ALU.mult))
                dve.sem_inc(dve_pe, 1)
                for i in range(2 * TT):
                    dve.wait_ge(act_dve, 1).then_inc(act_dve, -1)
                    c = slice((i % 2) * SEQ, (i % 2 + 1) * SEQ)
                    v(V.tensor_tensor(H_lo[:, i // 2, c], ps[:, 2 + i % 2, :], H_hi[:, i // 2, c].bitcast(F32), ALU.subtract),
                      dve_pe)
                dve.wait_ge(to_dve, 1).then_inc(to_dve, -1)
                v(V.tensor_copy(lg, ps[:, 4:8, 0:NE]))
                rank = C[:, None, C_RANK:C_RANK + NE].to_broadcast([P, TT, NE])

                def spread(m):
                    return m[:, :, None].to_broadcast([P, TT, NE])

                def best(m, oh):
                    v(V.tensor_reduce(m, lg, AX.X, ALU.max))
                    v(V.tensor_tensor(tt1, lg, spread(m), ALU.is_ge))
                    v(V.tensor_tensor(tt1, tt1, rank, ALU.mult))
                    v(V.tensor_reduce(m3, tt1, AX.X, ALU.max))
                    v(V.tensor_tensor(oh, tt1, spread(m3), ALU.is_ge))
                best(m1, oh1)
                v(V.scalar_tensor_tensor(out=lg, in0=oh1, scalar=NEG, in1=lg, op0=ALU.mult, op1=ALU.add))
                best(m2, oh2)
                v(V.tensor_tensor(m3, m2, m1, ALU.subtract), dve_act)
                dve.wait_ge(act_dve, 1).then_inc(act_dve, -1)
                v(V.tensor_scalar(m1, m3, 1.0, None, ALU.add))
                v(V.reciprocal(m1, m1))
                v(V.tensor_tensor(m2, m3, m1, ALU.mult))
                v(V.tensor_tensor(mask, oh1, oh2, ALU.add))
                v(V.tensor_tensor(oh1, oh1, spread(m1), ALU.mult))
                v(V.tensor_tensor(oh2, oh2, spread(m2), ALU.mult))
                v(V.tensor_tensor(comb[:, :, 0:NE], oh1, oh2, ALU.add))
                every = vecs[:, None, V_PART:V_PART + NE].to_broadcast([P, TT, NE])
                for m in (comb[:, :, 0:NE], mask):
                    v(V.scalar_tensor_tensor(out=m, in0=m, scalar=vecs[:, V_ROUTED:V_ROUTED + 1], in1=every,
                                             op0=ALU.mult, op1=ALU.add), *((dve_pe,) if m is mask else ()))
                dve.wait_ge(to_dve, 1).then_inc(to_dve, -1)
                v(V.scalar_tensor_tensor(out=rk[:, :, 0:NE], in0=ps[:, 4, 0:TT * NE].rearrange("p (a b) -> p a b", a=TT), scalar=1.0,
                                         in1=mask, op0=ALU.add, op1=ALU.mult))
                v(V.tensor_scalar(rk[:, :, 0:NE], rk[:, :, 0:NE], 1.0, None, ALU.subtract))
                v(V.memset(rk[:, :, NE:NE + 1], -1.0))
                v(V.memset(comb[:, :, NE:NE + 1], 0.0))
                v(V.tensor_copy(cnt, ps[:, 4, TT * NE:(TT + 1) * NE]))
                v(V.tensor_copy(rj, rk[:, :, 0]))
                v(V.tensor_copy(cj, comb[:, :, 0]))
                for t in range(TT):
                    v(V.tensor_scalar(Pm[:, t, :], C[:, C_SLOT:C_SLOT + CAP], rj[:, t:t + 1], None, ALU.is_equal))
                dve.sem_inc(dve_pe, 1)
                v(V.tensor_tensor(flag.rearrange("p (a b) -> p a b", a=NE), cnt[:, :, None].to_broadcast([P, NE, PASSES]),
                                  C[:, C_JPASS:C_JPASS + NQ].rearrange("p (a b) -> p a b", a=NE), ALU.is_gt))
                v(V.memset(flag[:, 0:1], 1.0))
                v(V.tensor_tensor(jw, C[:, C_JLT:C_JLT + NQ * NQ].rearrange("p (a b) -> p a b", a=NQ),
                                  flag[:, None, :].to_broadcast([P, NQ, NQ]), ALU.mult))
                v(V.tensor_reduce(jpos, jw, AX.X, ALU.add))
                v(V.tensor_reduce(jn, flag, AX.X, ALU.add))
                v(V.tensor_tensor(jw2, jpos[:, None, :].to_broadcast([P, NQ + 1, NQ]),
                                  C[:, C_JNUM:C_JNUM + NQ + 1, None].to_broadcast([P, NQ + 1, NQ]), ALU.is_equal))
                v(V.tensor_tensor(jw2, jw2, flag[:, None, :].to_broadcast([P, NQ + 1, NQ]), ALU.mult))
                for table, col in ((jpart, C_JPART), (jbase, C_JPASS)):
                    v(V.tensor_tensor(jw3, jw2, C[:, None, col:col + NQ].to_broadcast([P, NQ + 1, NQ]), ALU.mult))
                    v(V.tensor_reduce(table, jw3, AX.X, ALU.add))
                v(V.tensor_scalar(jw2[:, :, 0], C[:, C_JNUM:C_JNUM + NQ + 1], jn[:, 0:1], vecs[:, V_NPART:V_NPART + 1],
                                  ALU.is_equal, ALU.mult))
                v(V.tensor_tensor(jobs[:, 0:NQ + 1], jpart, jw2[:, :, 0], ALU.add))
                v(V.tensor_copy(jobs[:, NQ + 1:NQ + 2], jn), dve_sp, dve_pe, dve_act, dve_pool)
                def halves(half):
                    return slice(half * HALF, (half + 1) * HALF)

                def rest(s, half, turn):
                    c = halves(half)
                    dve.wait_ge(high_full[s], 1).then_inc(high_full[s], -1)
                    v(V.tensor_tensor(w_lo[:, s, c], raw_of(s, turn, c), w_hi[:, s, c].bitcast(F32), ALU.subtract),
                      *((split_full[s], raw_free[s]) if half else (first_full[s],)))

                def place(e, j):
                    v(V.tensor_scalar(rj, rk[:, :, bass.ds(e, 1)].rearrange("p a b -> p (a b)"), jbase[:, bass.ds(j, 1)],
                                      None, ALU.subtract))
                    v(V.tensor_copy(cj, comb[:, :, bass.ds(e, 1)].rearrange("p a b -> p (a b)")))
                    for t in range(TT):
                        v(V.tensor_scalar(Pm[:, t, :], C[:, C_SLOT:C_SLOT + CAP], rj[:, t:t + 1], None, ALU.is_equal))
                    dve.sem_inc(dve_pe, 1)

                def gathered():
                    for f in range(1, KT, 2):
                        dve.wait_ge(to_dve, 1).then_inc(to_dve, -1)
                        v(V.tensor_copy(hg[:, f, :], ps[:, GB[f], :]), dve_pe)

                def weights():
                    dve.wait_ge(to_dve, 1).then_inc(to_dve, -1)
                    v(V.tensor_copy(ws, ps[:, 6, 0:ST]))

                n_jobs = dve.value_load(jobs[0:1, NQ + 1:NQ + 2], min_val=1, max_val=NQ)
                weights()
                with dve.Fori(0, n_jobs) as j:
                    e1 = dve.value_load(jobs[0:1, bass.ds(j + 1, 1)], min_val=0, max_val=NE)
                    place(e1, j + 1)
                    dve.sem_inc(dve_pool, 1)
                    with dve.Fori(0, FT) as i:
                        turn = dve.snap((j + i + 1) % 2, min_val=0, max_val=1)
                        rest(0, 0, turn)
                        rest(0, 1, turn)
                        dve.wait_ge(to_dve, 1).then_inc(to_dve, -1)
                        dve.sem_inc(split_free[1], 1)
                        dve.wait_ge(act_dve, 1).then_inc(act_dve, -1)
                        dve.wait_ge(pool_dve, 1).then_inc(pool_dve, -1)
                        v(V.tensor_tensor(hid, gu, ps[:, 1, 0:CAP], ALU.mult), acc_free[1], dve_act)
                    dve.wait_ge(pool_dve, 1).then_inc(pool_dve, -1)
                    dve.sem_inc(hidden_ready, 1)
                    gathered()
                    with dve.Fori(0, FT // 2) as i:
                        turn = dve.snap((j + i) % 2, min_val=0, max_val=1)
                        for s in range(2):
                            for half in range(2):
                                rest(s, half, turn)
                    for half in range(2):
                        for st in range(ST):
                            c = slice(half * SEQ, (half + 1) * SEQ)
                            dve.wait_ge(act_dve, 1).then_inc(act_dve, -1)
                            v(V.scalar_tensor_tensor(out=Y_lo[:, st, c], in0=ps[:, 2 + 2 * st + half, :],
                                                     scalar=ws[:, st:st + 1], in1=Y_hi[:, st, c].bitcast(F32),
                                                     op0=ALU.mult, op1=ALU.subtract), dve_pe)
                    for half in range(2):
                        rest(0, half, (j + 1) % 2)
                    for f in range(KT):
                        dve.wait_ge(to_dve, 1).then_inc(to_dve, -1)
                        v(V.tensor_tensor(X[:, f, :], X[:, f, :], ps[:, SB[f], :], ALU.add),
                          *((acc_free[SB[f]],) if SB[f] < 2 else (dve_pe,) if f in (1, KT - 1) else ()))
                    for half in range(2):
                        rest(1, half, (j + 1) % 2)
                    weights()
                dve.sem_inc(dve_act, 1)
                dve.sem_inc(dve_sp, 1)
            dve.wait_ge(act_dve, 1).then_inc(act_dve, -1)
            for k in range(KT):
                v(V.scalar_tensor_tensor(out=final[:, k, :], in0=X[:, k, :],
                                         scalar=vecs[:, V_FING + k:V_FING + k + 1],
                                         in1=rinv[:, :], op0=ALU.mult, op1=ALU.mult))
            dve.sem_inc(dve_sp, 1)



def by_partition(w):
    return w.reshape(w.shape[0] // P, P, w.shape[1]).transpose(1, 0, 2)


def tiles(w, n_out):
    a = by_partition(w)
    k, n = a.shape[1], w.shape[1]
    a = a.reshape(P, k, n // (P * n_out), n_out, P).transpose(2, 0, 3, 1, 4)
    return a.reshape(n // (P * n_out), P, n_out * k * P)


def rows_first(w, k):
    a = by_partition(w)
    n = w.shape[1]
    return a.reshape(P, a.shape[1] // k, k, n).transpose(1, 0, 2, 3).reshape(-1, P, k * n)


def mix_stream(w_in, w_up, w_out, wq, wkv, wo):
    o_moba, o_dn = 256, 256 + 768
    o_ba = o_dn + 1536
    o_z = o_ba + 16
    o_gate = o_z + 512
    t = tiles(w_in[:, 0:256], 1)
    out = [t, rows_first(w_in[:, o_moba + 512:o_moba + 768], 4)]
    q, k = tiles(w_in[:, o_moba:o_moba + 256], 1), tiles(w_in[:, o_moba + 256:o_moba + 512], 1)
    out += [x[j:j + 1] for j in range(MOBA_PAIRS) for x in (q, k)]
    qkvz = [tiles(w_in[:, o:o + 512], 1) for o in (o_dn, o_dn + 512, o_dn + 1024, o_z)]
    out += [x[j:j + 1] for j in range(PAIRS) for x in qkvz]
    gates = [tiles(w_in[:, o_gate + b * D:o_gate + (b + 1) * D], 1) for b in range(3)]
    up = tiles(w_up, 1)
    out += [x[j:j + 1] for j in range(KT) for x in (*gates, up)]
    out += [tiles(w_out, 1), rows_first(wkv[:, 512:1024], 2)]
    q, k = tiles(wq, 1), tiles(wkv[:, 0:512], 1)
    out += [x[j:j + 1] for j in range(XH) for x in (q, k)]
    out += [tiles(wo, 2)]
    return out


def ffn_stream(w_gate_up, w_down, e):
    ff = w_gate_up.shape[1] // 2
    c = slice(e * FF, (e + 1) * FF)
    gate, up = tiles(w_gate_up[:, 0:ff][:, c], 1), tiles(w_gate_up[:, ff:][:, c], 1)
    return [x[j:j + 1] for j in range(FT) for x in (gate, up)] + [rows_first(w_down[c], 1), gate[0:1]]


def kernel(**inputs):
    import concourse.bacc as bacc
    from concourse.bass_utils import run_bass_kernel_spmd

    a = {k: np.asarray(v) for k, v in inputs.items()}
    stream = []
    vec = np.zeros((DEPTH, P, NV), np.float32)
    small = np.zeros((DEPTH, P, 2 * P + KT * 16 + KT * NE), np.float32)
    for l in range(DEPTH):
        w_up = np.concatenate([a["w_up_pool"][l], a["w_up_moba"][l], a["w_up_dn"][l]], axis=0)
        stream += mix_stream(a["w_in"][l], w_up, a["w_out"][l], a["xa_wq"][l], a["xa_wkv"][l], a["xa_wo"][l])
        for e in range(NE if l % 2 else DENSE_PARTS):
            stream += (ffn_stream(a["moe_w_gate_up"][l // 2, e], a["moe_w_down"][l // 2, e], 0) if l % 2
                       else ffn_stream(a["dense_w_gate_up"][l // 2], a["dense_w_down"][l // 2], e))
        for c, name in ((V_MIXG, "mix_norm_g"), (V_XAG, "xa_norm_g"), (V_MEMG, "mem_norm_g"), (V_FFNG, "ffn_norm_g")):
            vec[l, :, c:c + KT] = a[name][l].reshape(KT, P).T
        vec[l, :, V_FING:V_FING + KT] = a["final_norm_g"].reshape(KT, P).T
        vec[l, :, V_CONV:V_CONV + 48] = a["dn_conv_w"][l].reshape(4, 3, PAIRS, P).transpose(3, 2, 1, 0).reshape(P, 48)
        vec[l, :, V_POOLS:V_POOLS + 2] = a["pool_scale"][l].reshape(2, P).T
        vec[l, :, V_DNG] = np.concatenate([a["dn_norm_g"][l]] * 2)
        for c, name in ((V_ALOG, "dn_a_log"), (V_DTB, "dn_dt_bias")):
            vec[l, :, c:c + PAIRS] = np.repeat(a[name][l].reshape(PAIRS, 2).T, HD, axis=0)
        vec[l, :, V_ROUTED] = l % 2
        vec[l, :, V_PART:V_PART + DENSE_PARTS] = 1 - l % 2
        vec[l, :, V_NPART] = NE if l % 2 else DENSE_PARTS
        for b in range(4):
            r = slice((b % 2) * HD, (b % 2 + 1) * HD)
            c = (b // 2) * P + (b % 2) * HD
            small[l, r, c:c + HD] = a["pool_w"][l, b]
        small[l, :, 2 * P:2 * P + KT * 16] = by_partition(a["w_in"][l][:, 2560:2576]).reshape(P, KT * 16)
        small[l, :, 2 * P + KT * 16:] = by_partition(a["moe_router"][0]).reshape(P, KT * NE)

    nc = bacc.Bacc("TRN2", target_bir_lowering=False, num_devices=1)
    arrays = {
        "x_t": by_partition(a["x"][0].T),
        "mem_t": by_partition(a["mem"][0].T),
        "pos": a["positions"].astype(np.int32),
        "cst": constants(),
        "vec": vec,
        "wsm": small,
        "wst": np.concatenate(stream + [stream[0][0:1]] * 2, axis=0),
    }
    arrays = {k: np.ascontiguousarray(v) for k, v in arrays.items()}
    args = [nc.dram_tensor(k, v.shape, mybir.dt.from_np(v.dtype), kind="ExternalInput").ap() for k, v in arrays.items()]
    out = nc.dram_tensor("out_t", (P, KT, SEQ), F32, kind="ExternalOutput").ap()
    program(nc, *args, out)
    r = run_bass_kernel_spmd(nc, [arrays], core_ids=[0])
    got = np.asarray(r.results[0]["out_t"])
    return np.ascontiguousarray(got.transpose(1, 0, 2).reshape(D, SEQ).T).reshape(1, SEQ, D)
```
